# Optimizing a Trainium2 kernel written in Bass

```python
import jax, jax.numpy as jnp
from jax import lax
import numpy as np

D_MODEL = 1024
BATCH = 1
SEQ = 512
DEPTH = 1

N_META = 16
N_HEADS = 8
N_KV_HEADS = 2
HEAD_DIM = 128
Q_PER_KV = N_HEADS // N_KV_HEADS
ATTN_WIDTH = N_HEADS * HEAD_DIM
KV_WIDTH = N_KV_HEADS * HEAD_DIM
WINDOW = 128
BLOCK = 128
LRU_WIDTH = D_MODEL
LRU_BLOCKS = 8
LRU_BLOCK_DIM = LRU_WIDTH // LRU_BLOCKS
CONV_WIDTH = 4
LRU_C = 8.0
N_GROUPS = 4
EXPERTS_PER_GROUP = 4
N_EXPERTS = N_GROUPS * EXPERTS_PER_GROUP
TOP_K = 2
EXPERT_FF = 512
N_BRANCHES = 2
IN_WIDTH = ATTN_WIDTH + 2 * KV_WIDTH + 2 * LRU_WIDTH + N_BRANCHES * D_MODEL
IN_SPLITS = (ATTN_WIDTH, ATTN_WIDTH + KV_WIDTH, ATTN_WIDTH + 2 * KV_WIDTH,
             ATTN_WIDTH + 2 * KV_WIDTH + LRU_WIDTH, ATTN_WIDTH + 2 * KV_WIDTH + 2 * LRU_WIDTH)
EPS = 1e-6
NEG_INF = -1e30

kernel_name = 'hybrid_rglru_swa_hmoe_encoder_block'

def rms_norm(x, g):
    xf = x.astype(jnp.float32)
    y = xf * lax.rsqrt(jnp.mean(xf * xf, axis=-1, keepdims=True) + EPS)
    return (y * g.astype(jnp.float32)).astype(x.dtype)

def alibi_slopes():
    return jnp.exp2(-8.0 * (jnp.arange(N_HEADS, dtype=jnp.float32) + 1.0) / N_HEADS)

def banded_window_attention(q, k, v, sink):
    batch, t_len = q.shape[0], q.shape[1]
    lead = BLOCK - N_META
    p_len = t_len + lead
    nb = p_len // BLOCK
    pad = ((0, 0), (lead, 0), (0, 0), (0, 0))
    qb = jnp.pad(q, pad).reshape(batch, nb, BLOCK, N_KV_HEADS, Q_PER_KV, HEAD_DIM)

    def band(z):
        zb = jnp.pad(z, pad).reshape(batch, nb, BLOCK, N_KV_HEADS, HEAD_DIM)
        zb = jnp.pad(zb, ((0, 0), (1, 1), (0, 0), (0, 0), (0, 0)))
        return jnp.concatenate([zb[:, :-2], zb[:, 1:-1], zb[:, 2:]], axis=2)

    kb, vb = band(k), band(v)
    blk = jnp.arange(nb)[:, None]
    q_pos = blk * BLOCK + jnp.arange(BLOCK)[None, :] - lead
    k_idx = (blk - 1) * BLOCK + jnp.arange(3 * BLOCK)[None, :]
    k_pos = k_idx - lead
    k_ok = (k_pos >= N_META) & (k_idx < p_len)
    dist = jnp.abs(q_pos[:, :, None] - k_pos[:, None, :])
    band_ok = (dist <= WINDOW) & k_ok[:, None, :]
    scale = HEAD_DIM ** -0.5
    slopes = alibi_slopes().reshape(N_KV_HEADS, Q_PER_KV)
    s_band = jnp.einsum('bnqkgd,bnskd->bnkgqs', qb, kb, preferred_element_type=jnp.float32) * scale
    s_band = s_band - slopes[None, None, :, :, None, None] * dist.astype(jnp.float32)[None, :, None, None]
    s_band = jnp.where(band_ok[None, :, None, None], s_band, NEG_INF)
    k_meta, v_meta = k[:, :N_META], v[:, :N_META]
    s_meta = jnp.einsum('bnqkgd,bmkd->bnkgqm', qb, k_meta, preferred_element_type=jnp.float32) * scale
    s_sink = jnp.broadcast_to(sink.astype(jnp.float32).reshape(1, 1, N_KV_HEADS, Q_PER_KV, 1, 1),
                              s_band.shape[:-1] + (1,))
    probs = jax.nn.softmax(jnp.concatenate([s_band, s_meta, s_sink], axis=-1), axis=-1).astype(v.dtype)
    out = (jnp.einsum('bnkgqs,bnskd->bnqkgd', probs[..., :3 * BLOCK], vb)
           + jnp.einsum('bnkgqm,bmkd->bnqkgd', probs[..., 3 * BLOCK:3 * BLOCK + N_META], v_meta))
    return out.reshape(batch, p_len, ATTN_WIDTH)[:, lead:]

def centred_depthwise_conv(x, w, b):
    y = lax.conv_general_dilated(x, w[:, None, :].astype(x.dtype), window_strides=(1,),
                                 padding=[(CONV_WIDTH // 2, CONV_WIDTH - 1 - CONV_WIDTH // 2)],
                                 dimension_numbers=('NWC', 'WIO', 'NWC'),
                                 feature_group_count=x.shape[-1])
    return y + b

def linear_combine(left, right):
    a1, b1 = left
    a2, b2 = right
    return a1 * a2, a2 * b1 + b2

def rg_lru(xc, w_a, b_a, w_x, b_x, lam, reverse):
    batch, t_len = xc.shape[0], xc.shape[1]
    xb = xc.reshape(batch, t_len, LRU_BLOCKS, LRU_BLOCK_DIM)
    r = jax.nn.sigmoid((jnp.einsum('btnd,nde->btne', xb, w_a).reshape(batch, t_len, LRU_WIDTH) + b_a).astype(jnp.float32))
    i = jax.nn.sigmoid((jnp.einsum('btnd,nde->btne', xb, w_x).reshape(batch, t_len, LRU_WIDTH) + b_x).astype(jnp.float32))
    log_a = -LRU_C * r * jax.nn.softplus(-lam.astype(jnp.float32))
    a = jnp.exp(log_a)
    u = jnp.sqrt(-jnp.expm1(2.0 * log_a)) * (i * xc.astype(jnp.float32))
    _, h = lax.associative_scan(linear_combine, (a, u), axis=1, reverse=reverse)
    return h

def hierarchical_moe(x2, w_group, b_group, w_router, b_router, w_gate, w_up, w_down):
    n = x2.shape[0]
    g_prob = jax.nn.softmax((x2 @ w_group + b_group).astype(jnp.float32), axis=-1)
    g_top_p, g_idx = lax.top_k(g_prob, 1)
    e_logits = (x2 @ w_router + b_router).astype(jnp.float32).reshape(n, N_GROUPS, EXPERTS_PER_GROUP)
    e_in_group = jnp.take_along_axis(e_logits, g_idx[:, :, None], axis=1)[:, 0]
    e_top, e_idx = lax.top_k(e_in_group, TOP_K)
    weights = jax.nn.softmax(e_top, axis=-1) * g_top_p
    expert_ids = g_idx * EXPERTS_PER_GROUP + e_idx
    gates = jnp.einsum('nk,nke->ne', weights,
                       jax.nn.one_hot(expert_ids, N_EXPERTS, dtype=jnp.float32)).astype(x2.dtype)
    out = jnp.zeros_like(x2)
    for e in range(N_EXPERTS):
        hdn = jax.nn.silu(x2 @ w_gate[e]) * (x2 @ w_up[e])
        out = out + gates[:, e:e + 1] * (hdn @ w_down[e])
    return out

def setup_inputs(seed: int = 0) -> dict:
    key = jax.random.key(seed)
    ks = jax.random.split(key, 24)
    f32 = jnp.float32

    def nrm(k, shape, scale):
        return jax.random.normal(k, shape, f32) * scale

    a0 = jax.random.uniform(ks[12], (DEPTH, 2, LRU_WIDTH), f32, 0.9, 0.999)
    return {
        'x': nrm(ks[0], (BATCH, SEQ, D_MODEL), 1.0),
        'meta_tokens': nrm(ks[1], (N_META, D_MODEL), 1.0),
        'norm_mix_g': 1.0 + nrm(ks[2], (DEPTH, D_MODEL), 0.02),
        'w_in': nrm(ks[3], (DEPTH, D_MODEL, IN_WIDTH), D_MODEL ** -0.5),
        'conv_w': nrm(ks[4], (DEPTH, CONV_WIDTH, LRU_WIDTH), CONV_WIDTH ** -0.5),
        'conv_b': nrm(ks[5], (DEPTH, LRU_WIDTH), 0.01),
        'lru_w_a': nrm(ks[6], (DEPTH, 2, LRU_BLOCKS, LRU_BLOCK_DIM, LRU_BLOCK_DIM), LRU_BLOCK_DIM ** -0.5),
        'lru_b_a': nrm(ks[7], (DEPTH, 2, LRU_WIDTH), 0.01),
        'lru_w_x': nrm(ks[8], (DEPTH, 2, LRU_BLOCKS, LRU_BLOCK_DIM, LRU_BLOCK_DIM), LRU_BLOCK_DIM ** -0.5),
        'lru_b_x': nrm(ks[9], (DEPTH, 2, LRU_WIDTH), 0.01),
        'lru_lambda': jnp.log(a0) - jnp.log1p(-a0),
        'attn_sink': nrm(ks[10], (DEPTH, N_HEADS), 0.5),
        'w_attn_branch': nrm(ks[11], (DEPTH, ATTN_WIDTH, D_MODEL), ATTN_WIDTH ** -0.5),
        'w_rec_branch': nrm(ks[13], (DEPTH, LRU_WIDTH, D_MODEL), LRU_WIDTH ** -0.5),
        'w_out': nrm(ks[14], (DEPTH, D_MODEL, D_MODEL), D_MODEL ** -0.5),
        'norm_ffn_g': 1.0 + nrm(ks[15], (DEPTH, D_MODEL), 0.02),
        'w_group': nrm(ks[16], (DEPTH, D_MODEL, N_GROUPS), D_MODEL ** -0.5),
        'b_group': nrm(ks[17], (DEPTH, N_GROUPS), 0.01),
        'w_router': nrm(ks[18], (DEPTH, D_MODEL, N_EXPERTS), D_MODEL ** -0.5),
        'b_router': nrm(ks[19], (DEPTH, N_EXPERTS), 0.01),
        'moe_w_gate': nrm(ks[20], (DEPTH, N_EXPERTS, D_MODEL, EXPERT_FF), D_MODEL ** -0.5),
        'moe_w_up': nrm(ks[21], (DEPTH, N_EXPERTS, D_MODEL, EXPERT_FF), D_MODEL ** -0.5),
        'moe_w_down': nrm(ks[22], (DEPTH, N_EXPERTS, EXPERT_FF, D_MODEL), EXPERT_FF ** -0.5),
        'final_norm_g': 1.0 + nrm(ks[23], (D_MODEL,), 0.02),
    }

def reference(x, meta_tokens, norm_mix_g, w_in, conv_w, conv_b, lru_w_a, lru_b_a, lru_w_x, lru_b_x,
              lru_lambda, attn_sink, w_attn_branch, w_rec_branch, w_out, norm_ffn_g, w_group, b_group,
              w_router, b_router, moe_w_gate, moe_w_up, moe_w_down, final_norm_g):
    batch = x.shape[0]
    meta = jnp.broadcast_to(meta_tokens[None].astype(x.dtype), (batch, N_META, D_MODEL))
    h = jnp.concatenate([meta, x], axis=1)
    t_len = h.shape[1]
    for l in range(DEPTH):
        n = rms_norm(h, norm_mix_g[l])
        z = n @ w_in[l]
        q, k, v, xr, yr, gate_logits = jnp.split(z, IN_SPLITS, axis=-1)
        q = q.reshape(batch, t_len, N_HEADS, HEAD_DIM)
        k = k.reshape(batch, t_len, N_KV_HEADS, HEAD_DIM)
        v = v.reshape(batch, t_len, N_KV_HEADS, HEAD_DIM)
        attn = banded_window_attention(q, k, v, attn_sink[l]) @ w_attn_branch[l]
        xc = centred_depthwise_conv(xr, conv_w[l], conv_b[l])
        rec = (rg_lru(xc, lru_w_a[l, 0], lru_b_a[l, 0], lru_w_x[l, 0], lru_b_x[l, 0], lru_lambda[l, 0], False)
               + rg_lru(xc, lru_w_a[l, 1], lru_b_a[l, 1], lru_w_x[l, 1], lru_b_x[l, 1], lru_lambda[l, 1], True))
        rec = (rec.astype(x.dtype) * jax.nn.gelu(yr)) @ w_rec_branch[l]
        g_attn, g_rec = jnp.split(jax.nn.sigmoid(gate_logits), N_BRANCHES, axis=-1)
        h = h + (g_attn * attn + g_rec * rec) @ w_out[l]
        n2 = rms_norm(h, norm_ffn_g[l]).reshape(-1, D_MODEL)
        h = h + hierarchical_moe(n2, w_group[l], b_group[l], w_router[l], b_router[l],
                                 moe_w_gate[l], moe_w_up[l], moe_w_down[l]).reshape(h.shape)
    return rms_norm(h, final_norm_g)[:, N_META:]


_drawn_inputs = setup_inputs


def setup_inputs(seed=0):
    import zlib

    import numpy as np

    out = dict(_drawn_inputs(seed))
    spreads = {}
    factors = {'norm_mix_g': 2.689,
     'lru_b_a': 30.168,
     'lru_b_x': 24.391,
     'attn_sink': 64.0,
     'b_group': 26.713,
     'b_router': 43.888,
     'final_norm_g': 8.468,
     'conv_b': 3.499,
     'norm_ffn_g': 5.876}
    for name, (base, spread) in spreads.items():
        noise = np.random.default_rng([zlib.crc32(name.encode()), seed]).standard_normal(out[name].shape)
        drawn = base * np.exp(spread * noise) if base else spread * noise
        out[name] = __import__('jax').numpy.asarray(drawn.astype(out[name].dtype))
    for name, factor in factors.items():
        out[name] = (out[name] * factor).astype(out[name].dtype)
    return out
```

```python
import concourse.bass as bass
from concourse import mybir
from contextlib import ExitStack

P = 128
D = 1024
KT = D // P
SEQ = 512
META = 16
T = META + SEQ
HALF = T // 2
TT = SEQ // P
HEADS = 8
KV = 2
HD = 128
N_E = 16
N_G = 4
E_G = N_E // N_G
FF = 512
FT = FF // P
CHUNK = 96
MAXC = N_E + (2 * SEQ) // CHUNK
NIDX = MAXC + 1
EPS = 1e-6
COL_Q, COL_K, COL_V, COL_X, COL_Y, COL_GA, COL_GR = 0, 1024, 1280, 1536, 2560, 3584, 4608

F32 = mybir.dt.float32
F32R = mybir.dt.float32r
I32 = mybir.dt.int32
ACT = mybir.ActivationFunctionType
ALU = mybir.AluOpType
AX = mybir.AxisListType

PHASES = ["kv", "mix", "branch", "out"]
UNIT_SLOTS = {"kv": [0, 1, 2, 1], "mix": [0, 1, 2, 0, 1, 2, 1], "branch": [0, 1, 2, 1], "out": [0, 1]}
RUNS = {"kv": 1, "mix": 4, "branch": 8, "out": 4}

def unit(phase, u, it=0):
    slots = UNIT_SLOTS[phase]
    if u >= len(slots):
        return unit(phase, u - len(slots), it + 1)
    s = slots[u]
    before = 0
    for q in PHASES[:PHASES.index(phase)]:
        before += RUNS[q] * UNIT_SLOTS[q].count(s)
    before += slots[:u].count(s)
    return s, it * slots.count(s) + before


def w_in_target(phase, u, it=0):
    s, n = unit(phase, u, it)
    lru_slot = UNIT_SLOTS["mix"][4]
    extra = 0
    if s == lru_slot:
        order = PHASES.index(phase) * 1
        if phase == "mix":
            run, at = it, u
            if u >= 7:
                run, at = it + 1, u - 7
            extra = run * 32 + (32 if at >= 4 else 0)
        elif order > PHASES.index("mix"):
            extra = RUNS["mix"] * 32
    return n * 32 + 32 + extra


def is_const(v):
    return isinstance(v, int)


class Chain:

    def __init__(self, eng, sem):
        self.eng, self.sem, self.base, self.it, self.per, self.n = eng, sem, 0, 0, 0, 0

    def body(self, it, per):
        self.it, self.per, self.n = it, per, 0

    def mark(self, ins):
        ins.then_inc(self.sem, 1)
        self.n += 1
        return self.n

    def need(self, n):
        self.eng.wait_ge(self.sem, self.it * self.per + (self.base + n))

    def link(self, ins):
        self.need(self.mark(ins))

    def close(self, runs=1):
        assert runs == 1 or self.n == self.per, (self.n, self.per)
        self.base += runs * self.n
        self.it, self.per, self.n = 0, 0, 0


def block_program(nc, x, meta_tokens, norm_mix_g, w_in, conv_w, conv_b, lru_w_a, lru_b_a, lru_w_x, lru_b_x,
                  lru_lambda, attn_sink, w_attn_branch, w_rec_branch, w_out, norm_ffn_g, w_group, b_group,
                  w_router, b_router, moe_w_gate, moe_w_up, moe_w_down, final_norm_g, out):
    ctx = ExitStack()
    KB = 1024
    X_AT = 16512
    CONST_AT = X_AT + 16 * KB
    R1 = CONST_AT + 7 * KB
    REST = R1 + 68 * KB
    TAIL = REST + 96 * KB
    END = nc.sbuf_usable_end
    assert X_AT >= nc.sbuf_base

    class Region:

        def __init__(self, at, end):
            self.at, self.end = at, end

        def put(self, name, shape, dt=F32):
            size = 4
            for n in shape[1:]:
                size *= n
            t = nc.alloc_sbuf_tensor_at(name, shape, dt, offset=self.at)
            self.at += (size + 31) // 32 * 32
            assert self.at <= self.end, (name, self.at - self.end)
            return t

    X = Region(X_AT, CONST_AT).put("resid", [P, TT, D])
    cr = Region(CONST_AT, R1)
    ident = cr.put("ident", [P, P])
    nd = cr.put("neg_dist", [P, 944])
    tri = cr.put("tri", [P, P])
    ones = cr.put("ones", [P, P])
    g12 = cr.put("g12", [P, 2, KT])
    stat = cr.put("norm_stat", [P, 3, TT + 1])
    stat2 = cr.put("norm_stat2", [P, 3, TT])
    stat3 = cr.put("norm_stat3", [P, 3, TT])
    thr = cr.put("chunk_thresholds", [P, 5])
    iota_e = cr.put("iota_e", [P, E_G])
    tok = cr.put("token_ids", [P, TT])
    bias_r = cr.put("router_bias", [P, N_G + N_E])
    wr = Region(R1, R1 + 36 * KB)
    w_raw = [wr.put(f"w_raw{s}", [P, KT, P]) for s in range(3)]
    w_hi = [wr.put(f"w_hi{s}", [P, KT, P], F32R) for s in range(3)]
    w_lo = [wr.put(f"w_lo{s}", [P, KT, P], F32R) for s in range(3)]
    mr = Region(R1 + 36 * KB, REST)
    kT_hi = mr.put("kT_hi", [P, KV, T], F32R)
    kT_lo = mr.put("kT_lo", [P, KV, T], F32R)
    V = mr.put("v_rows", [P, TT + 1, KV * HD])
    qT_hi = mr.put("qT_hi", [P, 2, SEQ], F32R)
    qT_lo = mr.put("qT_lo", [P, 2, SEQ], F32R)
    pt_sb = [mr.put(f"pt_sb{i}", [P, 4 * P]) for i in range(2)]
    o_sb = mr.put("o_sb", [P, TT, P])
    ndh = mr.put("neg_dist_h", [P, 944])
    rr = Region(REST, END)
    nT_hi = rr.put("nT_hi", [P, KT, T], F32R)
    nT_lo = rr.put("nT_lo", [P, KT, T], F32R)
    rec_at = rr.at
    rec = rr.put("rec", [P, KT, SEQ])
    attn = rr.put("attn", [P, KT, SEQ])
    PV = rr.put("par", [P, 15, 8])
    cur = rr.put("par_now", [P, 15, 2])
    nmax = rr.put("neg_max", [P, 2, TT])
    mx = rr.put("row_max", [P, 2, TT])
    rsum = rr.put("row_sum", [P, 2, TT])
    esink = rr.put("exp_sink", [P, TT])
    den = rr.put("denom", [P, TT])
    mix_at = rr.at
    ab = rr.put("lru_a", [P, 4, T])
    wb = rr.put("lru_w", [P, 4, T])
    vb = rr.put("lru_v", [P, 4, T])
    xr = rr.put("xr_pad", [P, 2, T + 4])
    xc = rr.put("xc", [P, 2, T])
    xc_hi = rr.put("xc_hi", [P, 2, T], F32R)
    xc_lo = rr.put("xc_lo", [P, 2, T], F32R)
    s_sb = [rr.put(f"s_sb{i}", [P, 400]) for i in range(2)]
    a2 = [rr.put(f"lru_a2_{i}", [P, T]) for i in range(2)]
    nr = Region(mix_at, END)
    xn = nr.put("xn_rows", [P, TT, D])
    msb = nr.put("meta_rows", [META, D])
    mn = nr.put("meta_n", [META, D])
    junk = nr.put("square_junk", [P, D])
    prm = nr.put("prm_rows", [104, P])
    spt = nr.put("softplus_tmp", [P, 8, 16])
    lo_r = Region(rec_at, mix_at)
    rec_lo = lo_r.put("rec_lo", [P, KT, SEQ], F32R)
    attn_lo = lo_r.put("attn_lo", [P, KT, SEQ], F32R)
    br = Region(mix_at, END)
    rec_hi = br.put("rec_hi", [P, KT, SEQ], F32R)
    attn_hi = br.put("attn_hi", [P, KT, SEQ], F32R)
    g_sb = br.put("gates", [P, 2, SEQ])
    m2 = br.put("gated", [P, 2, SEQ])
    ms = br.put("gated_sum", [P, SEQ])
    gr_ = Region(R1 + 36 * KB, REST)
    mg_hi = gr_.put("mergeT_hi", [P, KT, SEQ], F32R)
    mg_lo = gr_.put("mergeT_lo", [P, KT, SEQ], F32R)
    tr = Region(TAIL, END)
    xn2 = tr.put("xn2_rows", [P, TT, D])
    tail2 = tr.at
    oT_sb = [tr.put(f"oT_sb{i}", [P, SEQ]) for i in range(2)]
    rt = Region(tail2, END)
    lg = rt.put("logits", [P, TT, N_G + N_E])
    g1h = rt.put("group_onehot", [P, TT, N_G])
    gex = rt.put("group_exp", [P, TT, N_G])
    e_in = rt.put("e_in_group", [P, TT, E_G])
    e16 = rt.put("e_masked", [P, TT, N_G, E_G])
    o1h = [rt.put(f"expert_onehot{i}", [P, TT, E_G]) for i in range(2)]
    t4 = [rt.put(f"tmp4_{i}", [P, TT, E_G]) for i in range(2)]
    r1 = [rt.put(f"tmp1_{i}", [P, TT]) for i in range(8)]
    m16 = [rt.put(f"mask16_{i}", [P, TT, N_G, E_G]) for i in range(3)]
    slot_w = [rt.put(f"pair_weight{i}", [P, TT]) for i in range(2)]
    slot_i = [rt.put(f"pair_slot{i}", [P, TT], I32) for i in range(2)]
    idx = rt.put("chunk_rows", [CHUNK, NIDX], I32)
    idx_now = rt.put("chunk_rows_now", [CHUNK, 1], I32)
    ends = rt.put("chunk_ends", [P, N_E + 1], I32)
    endf = rt.put("chunk_endf", [P, N_E + 1])
    mz = Region(R1 + 48 * KB, REST)
    n2T = mz.put("n2T", [P, KT, SEQ])
    gfin = mz.put("final_gain", [P, D])
    mz2 = Region(R1 + 48 * KB, R1 + 64 * KB)
    rank = mz2.put("rank", [P, TT, N_E])
    cge = mz2.put("rank_over", [P, TT, N_E])
    fl = mz2.put("rank_chunk", [P, TT, N_E])
    nch = mz2.put("n_chunks", [P, N_E])
    ctmp = mz2.put("count_over", [P, N_E])
    pr = mz2.put("pair_tmp", [P, TT, N_E])
    prow = [mz2.put(f"pair_row{i}", [P, TT]) for i in range(2)]
    pch = [mz2.put(f"pair_chunk{i}", [P, TT]) for i in range(2)]
    roh = mz2.put("row_onehot", [P, 8, CHUNK])
    coh = mz2.put("chunk_onehot", [P, 8, NIDX])
    io_r = mz2.put("iota_rows", [P, CHUNK])
    io_c = mz2.put("iota_chunks", [P, NIDX])
    wgr = Region(TAIL, END)
    slots_at = [REST, REST + 48 * KB, R1]
    wg_sb, wu_sb, wd_sb = [], [], []
    for s, at in enumerate(slots_at):
        r = Region(at, at + 48 * KB)
        wg_sb.append(r.put(f"e_gate{s}", [P, KT, FF]))
        wu_sb.append(r.put(f"e_up{s}", [P, KT, FF]))
        wd_sb.append(r.put(f"e_down{s}", [P, FT, D]))
    er = Region(R1 + 56 * KB, R1 + 64 * KB)
    xT = er.put("chunk_xT", [P, KT, CHUNK])
    hT = er.put("chunk_hT", [P, FT, CHUNK])
    sg = er.put("chunk_silu", [P, FT, CHUNK])
    er2 = Region(TAIL, TAIL + 16 * KB)
    G = er2.put("chunk_rows_x", [CHUNK, D])
    y_sb = er2.put("chunk_y", [CHUNK, D])
    rw = Region(TAIL - 0, END)
    fr = Region(REST, REST + 48 * KB)
    F = [fr.put(f"pair_rows{i}", [P, TT, D]) for i in range(2)]
    fo = fr.put("final_rows", [P, 2, D])
    wrt = cr.put("router_w", [P, KT, N_G + N_E])

    n2_dram = nc.dram_tensor("n2_rows", [SEQ, D], F32, kind="Internal").ap()
    y_dram = nc.dram_tensor("y_rows", [MAXC * CHUNK, D], F32, kind="Internal").ap()

    pj = ctx.enter_context(nc.psum_tensor("pj", [P, 4, 512], F32))
    s_ps = ctx.enter_context(nc.psum_tensor("s_ps", [P, 2, 512], F32))
    pt_ps = ctx.enter_context(nc.psum_tensor("pt_ps", [P, 512], F32))
    o_ps = ctx.enter_context(nc.psum_tensor("o_ps", [P, 512], F32))

    def sem(name):
        return ctx.enter_context(nc.semaphore(name))

    def sems(name, n):
        return [sem(f"{name}{i}") for i in range(n)]

    x_in = sems("x_in", TT)
    meta_in = sem("meta_in")
    prm_in = sem("prm_in")
    wrt_in = sem("wrt_in")
    gfin_in = sem("gfin_in")
    act_chain, dve_chain, pool_chain = sem("act_chain"), sem("dve_chain"), sem("pool_chain")
    const_ok = sem("const_ok")
    ssq_ok, var_ok, std_ok, xn_ok = sem("ssq_ok"), sem("var_ok"), sem("std_ok"), sem("xn_ok")
    prmT_ok, lam_abs_ok, lam_exp_ok, par_ok = sem("prmT_ok"), sem("lam_abs_ok"), sem("lam_exp_ok"), sem("par_ok")
    nT_hi_ok = sem("nT_hi_ok")
    w_in_ok, w_hi_ok, w_lo_ok, w_used = sems("w_in_ok", 3), sems("w_hi_ok", 3), sems("w_lo_ok", 3), sems("w_used", 3)
    nt_full, nt_lo_ok = sem("nt_full"), sem("nt_lo_ok")
    k_hi_ok, k_lo_ok, v_rows_ok = sem("k_hi_ok"), sem("k_lo_ok"), sem("v_rows_ok")
    lru_full, tha_ok = sem("lru_full"), sem("tha_ok")
    cur_ok, xr_ok, xc_ok, xch_ok, xcl_ok = sem("cur_ok"), sem("xr_ok"), sem("xc_ok"), sem("xch_ok"), sem("xcl_ok")
    qh_ok, q_ok = sem("qh_ok"), sem("q_ok")
    s_full, tt_ok, neg_ok, p_ok = sem("s_full"), sem("tt_ok"), sem("neg_ok"), sem("p_ok")
    pt_full, pt_free, o_done, onorm_ok, es_ok, ndh_ok = (sem("pt_full"), sem("pt_free"), sem("o_done"),
                                                         sem("onorm_ok"), sem("es_ok"), sem("ndh_ok"))
    thi_ok, a_ok, a2_ok, w_ok, v_ok, sq_ok, u_ok, scan_ok, gelu_ok, rec_ok = (
        sem(n) for n in ("thi_ok", "a_ok", "a2_ok", "w_ok", "v_ok", "sq_ok", "u_ok", "scan_ok", "gelu_ok", "rec_ok"))
    hsum_ok = sem("hsum_ok")
    br_hi_ok, br_lo_ok = sem("br_hi_ok"), sem("br_lo_ok")
    gate_ok, m2_ok, ms_ok, mh_ok, ml_ok = (sem(n) for n in ("gate_ok", "m2_ok", "ms_ok", "mh_ok", "ml_ok"))
    oT_ok, oT_full, h_ok = sem("oT_ok"), sem("oT_full"), sem("h_ok")
    ssq2_ok, var2_ok, std2_ok, xn2_ok = sem("ssq2_ok"), sem("var2_ok"), sem("std2_ok"), sem("xn2_ok")
    n2_out, rt_full, rt_free, lg_ok = sem("n2_out"), sem("rt_full"), sem("rt_free"), sem("lg_ok")
    gd_ok, gexp_ok, ed_ok, eexp_ok, m_ok, rank_ok, oh_ok, idxp_ok, route_ok = (
        sem(n) for n in ("gd_ok", "gexp_ok", "ed_ok", "eexp_ok", "m_ok", "rank_ok", "oh_ok", "idxp_ok", "route_ok"))
    iota_ok, idx_ok = sem("iota_ok"), sem("idx_ok")
    e_gate_in, e_up_in, e_down_in = sems("e_gate_in", 3), sems("e_up_in", 3), sems("e_down_in", 3)
    g_in, xt_full, xt_ok, gate_done, silu_ok, up_done, hid_ok, y_full, y_evac_a, y_evac_d, y_out = (
        sem(n) for n in ("g_in", "xt_full", "xt_ok", "gate_done", "silu_ok", "up_done", "hid_ok", "y_full",
                         "y_evac_a", "y_evac_d", "y_out"))
    f_in = sems("f_in", 8)
    out_done = sems("out_done", 2)
    ssq3_ok, var3_ok, std3_ok, hf_ok, fo_ok = (
        sem(n) for n in ("ssq3_ok", "var3_ok", "std3_ok", "hf_ok", "fo_ok"))
    flush = sem("flush")
    pad_ok, zero_ok, y_zeroed = sem("pad_ok"), sem("zero_ok"), sem("y_zeroed")

    def made(eng, phase, u, it=0):
        s, n = unit(phase, u, it)
        eng.wait_ge(w_used[s], n + 1)

    block = ctx.enter_context(nc.Block())

    w_in_v = w_in[0].rearrange("(k p) c -> p k c", p=P)
    wa_v = w_attn_branch[0].rearrange("(k p) c -> p k c", p=P)
    wr_v = w_rec_branch[0].rearrange("(k p) c -> p k c", p=P)
    wo_v = w_out[0].rearrange("(k p) c -> p k c", p=P)
    lwa_v = lru_w_a[0].rearrange("r b d e -> d r b e")
    lwx_v = lru_w_x[0].rearrange("r b d e -> d r b e")

    PASSES = ((0, 0), (0, 1), (1, 0))
    NT = (nT_hi, nT_lo)
    S_W = {1: 272, 2: 400, 3: 400, 4: 272}
    S_ND = {1: 0, 2: 272, 3: 272, 4: 672}
    S_K = {1: 16, 2: 16, 3: 144, 4: 272}
    S_V = {1: (1, 2), 2: (1, 2, 3), 3: (2, 3, 4), 4: (3, 4)}
    PT_N = {a: (a + 1 if a <= 4 else a + 2) for a in range(8)}
    OT_N = {0: 6, 1: 10}

    @block.sync
    def _(sp):
        for i in range(TT):
            sp.dma_start(X[:, i, :], x[0, i * P:(i + 1) * P, :]).then_inc(x_in[i], 16)
            if i == 0:
                sp.dma_start(msb[:, :], meta_tokens[:, :]).then_inc(meta_in, 16)

        def load_unit(phase, u, it, src):
            s, n = unit(phase, u, it)
            if not (is_const(n) and n == 0):
                sp.wait_ge(w_lo_ok[s], n)
                sp.sem_inc(flush, 1)
            for h in range(2):
                sp.dma_start(w_raw[s][:, 4 * h:4 * h + 4, :], src(h)).then_inc(w_in_ok[s], 16)

        def cols(view, c):
            return lambda h: view[:, 4 * h:4 * h + 4, bass.ds(c, P)]

        for u, c in enumerate((COL_K, COL_K + P, COL_V, COL_V + P)):
            load_unit("kv", u, 0, cols(w_in_v, c))
        sp.wait_ge(zero_ok, 1)
        for c in range(N_E, MAXC):
            sp.dma_start(y_dram[c * CHUNK:(c + 1) * CHUNK, :].rearrange("p (a t) -> p a t", a=2),
                         rec[0:CHUNK, 0:2, :]).then_inc(y_zeroed, 16)
        with sp.Fori(0, 4) as it:
            c = sp.snap(it * 256)
            b = sp.snap(it * 2)
            load_unit("mix", 0, it, cols(w_in_v, c + COL_X))
            load_unit("mix", 1, it, cols(w_in_v, c + (COL_X + P)))
            load_unit("mix", 2, it, cols(w_in_v, c + COL_Q))
            load_unit("mix", 3, it, cols(w_in_v, c + (COL_Q + P)))
            s, n = unit("mix", 4, it)
            sp.wait_ge(w_lo_ok[s], n)
            sp.sem_inc(flush, 1)
            for h, view in enumerate((lwa_v, lwx_v)):
                for r in range(2):
                    sp.dma_start(w_raw[s][:, 4 * h + 2 * r:4 * h + 2 * r + 2, :],
                                 view[:, r, bass.ds(b, 2), :]).then_inc(w_in_ok[s], 16)
            load_unit("mix", 5, it, cols(w_in_v, c + COL_Y))
            load_unit("mix", 6, it, cols(w_in_v, c + (COL_Y + P)))
        with sp.Fori(0, 8) as m:
            c = sp.snap(m * 128)
            load_unit("branch", 0, m, cols(w_in_v, c + COL_GA))
            load_unit("branch", 1, m, cols(w_in_v, c + COL_GR))
            load_unit("branch", 2, m, cols(wa_v, c))
            load_unit("branch", 3, m, cols(wr_v, c))
        with sp.Fori(0, 4) as it:
            c = sp.snap(it * 256)
            load_unit("out", 0, it, cols(wo_v, c))
            load_unit("out", 1, it, cols(wo_v, c + P))

        def load_expert(s, e, more):
            sp.dma_start(wg_sb[s][:, :, :], moe_w_gate[0, bass.ds(e, 1)].rearrange("a (k p) f -> p (a k) f", p=P)
                         ).then_inc(e_gate_in[s], 16)
            sp.dma_start(wu_sb[s][:, :, :], moe_w_up[0, bass.ds(e, 1)].rearrange("a (k p) f -> p (a k) f", p=P)
                         ).then_inc(e_up_in[s], 16)
            sp.dma_start(wd_sb[s][:, :, :], moe_w_down[0, bass.ds(e, 1)].rearrange("a (k p) f -> p (a k) f", p=P)
                         ).then_inc(e_down_in[s], 16)

        made(sp, "branch", 3, KT - 1)
        sp.wait_ge(ml_ok, KT)
        load_expert(0, 0, False)
        load_expert(1, 1, False)
        sp.wait_ge(oT_full, KT)
        sp.dma_start(gfin[:, :], final_norm_g.partition_broadcast(P)).then_inc(gfin_in, 16)
        load_expert(2, 2, False)
        sp.wait_ge(xn2_ok, TT)
        for i in range(TT):
            sp.dma_start(n2_dram[i * P:(i + 1) * P, :], xn2[:, i, :]).then_inc(n2_out, 16)
        sp.wait_ge(route_ok, 1)

        def reload(s, e):
            end = sp.value_load(ends[0:1, bass.ds(e - 2, 1)], min_val=1, max_val=MAXC)
            sp.wait_ge(y_full, end)
            sp.sem_inc(flush, 1)
            load_expert(s, e, True)

        with sp.Fori(1, 5) as r:
            for s in range(3):
                reload(s, sp.snap(r * 3 + s))
        reload(0, 15)
        for i in range(TT):
            sp.wait_ge(fo_ok, i + 1)
            sp.dma_start(out[0, i * P:(i + 1) * P, :], fo[:, i % 2, :]).then_inc(out_done[i % 2], 16)
        sp.wait_ge(out_done[0], 16 * TT // 2)
        sp.wait_ge(out_done[1], 16 * TT // 2)

    @block.gpsimd
    def _(pool):
        ch = Chain(pool, pool_chain)
        nc.gpsimd.memset(rec[0:CHUNK, 0:2, :], 0.0).then_inc(zero_ok, 1)
        nc.gpsimd.memset(ones[:, :], 1.0)
        nc.gpsimd.memset(stat[:, :, :], 1.0)
        for h in range(HEADS):
            nc.gpsimd.memset(PV[:, 13, h:h + 1], 2.0 ** (-8.0 * (h + 1) / HEADS))
        for k in range(5):
            nc.gpsimd.memset(thr[:, k:k + 1], float(CHUNK * (k + 1)))
        nc.gpsimd.iota(iota_e[:, :], pattern=[[1, E_G]], base=0, channel_multiplier=0,
                       allow_small_or_imprecise_dtypes=True)
        nc.gpsimd.iota(tok[:, :], pattern=[[P, TT]], base=0, channel_multiplier=1,
                       allow_small_or_imprecise_dtypes=True)
        nc.gpsimd.memset(nd[:, 0:16], 0.0)
        nc.gpsimd.memset(nd[:, 272:288], 0.0)
        nc.gpsimd.memset(nd[:, 672:688], 0.0)
        ch.link(nc.gpsimd.iota(nd[:, 288:672], pattern=[[1, 384]], base=-P, channel_multiplier=-1,
                               allow_small_or_imprecise_dtypes=True))
        ch.link(nc.gpsimd.affine_select(out=ident[:, :], in_=ones[:, :], compare_op=ALU.is_equal, fill=0.0, base=0,
                                        pattern=[[-1, P]], channel_multiplier=1))
        nc.gpsimd.affine_select(out=tri[:, :], in_=ones[:, :], compare_op=ALU.is_gt, fill=0.0, base=0,
                                pattern=[[1, P]], channel_multiplier=-1).then_inc(const_ok, 1)
        ch.link(nc.gpsimd.tensor_scalar(ndh[:, 0:384], nd[:, 288:672], -1.0, None, ALU.mult))
        ch.link(nc.gpsimd.affine_select(out=nd[:, 288:672], in_=nd[:, 288:672], compare_op=ALU.is_gt, fill=0.0,
                                        base=P, pattern=[[-1, 384]], channel_multiplier=1))
        ch.link(nc.gpsimd.affine_select(out=ndh[:, 0:384], in_=ndh[:, 0:384], compare_op=ALU.is_ge, fill=0.0,
                                        base=-P, pattern=[[1, 384]], channel_multiplier=-1))
        ch.link(nc.gpsimd.tensor_tensor(nd[:, 288:672], nd[:, 288:672], ndh[:, 0:384], ALU.add))
        ch.link(nc.gpsimd.affine_select(out=nd[:, 288:672], in_=nd[:, 288:672], compare_op=ALU.is_ge, fill=-1e32,
                                        base=0, pattern=[[1, 384]], channel_multiplier=-1))
        ch.link(nc.gpsimd.affine_select(out=nd[:, 288:672], in_=nd[:, 288:672], compare_op=ALU.is_ge, fill=-1e32,
                                        base=256, pattern=[[-1, 384]], channel_multiplier=1))
        nc.gpsimd.tensor_copy(nd[:, 16:272], nd[:, 288 + 128:672])
        ch.link(nc.gpsimd.tensor_copy(nd[:, 688:944], nd[:, 288:288 + 256]))
        ch.close()
        pool.wait_ge(nt_lo_ok, KT)
        nc.gpsimd.memset(xr[:, :, 0:2], 0.0)
        nc.gpsimd.memset(xr[:, :, T + 2:T + 4], 0.0).then_inc(pad_ok, 1)

        with pool.Fori(0, 4) as it:
            ch.body(it, 2)

            def head_bias(hh):
                pool.wait_ge(cur_ok, it + 1)
                pool.wait_ge(tt_ok, it * 8 + 4 * hh)
                pool.sem_inc(flush, 1)
                nc.gpsimd.tensor_scalar(ndh[:, :], nd[:, :], cur[:, 13, hh:hh + 1], None, ALU.mult
                                        ).then_inc(ndh_ok, 1)

            def square_a(i, bd):
                o = 0 if bd < 2 else META
                pool.wait_ge(a_ok, it * 4 + (i + 1))
                if i >= 2:
                    pool.wait_ge(w_ok, it * 4 + (i - 1))
                nc.gpsimd.tensor_tensor(a2[i % 2][:, o:T], ab[:, bd, o:T], ab[:, bd, o:T], ALU.mult
                                        ).then_inc(a2_ok, 1)

            head_bias(0)
            square_a(0, 0)
            square_a(1, 2)
            head_bias(1)
            square_a(2, 1)
            square_a(3, 3)
            pool.wait_ge(v_ok, it * 4 + 4)
            for d in range(2):
                o = META * d
                pool.wait_ge(sq_ok, it * 2 + (d + 1))
                for bb in range(2):
                    bd = 2 * d + bb
                    nc.gpsimd.tensor_tensor(vb[:, bd, o:T], vb[:, bd, o:T], wb[:, bd, o:T], ALU.mult
                                            ).then_inc(u_ok, 1)
            r = pool.snap(it * 2)
            marks = []
            for bb in range(2):
                pool.wait_ge(scan_ok, it * 4 + (3 + bb))
                marks.append(ch.mark(nc.gpsimd.tensor_tensor(a2[bb][:, 0:SEQ], wb[:, bb, META:T],
                                                             wb[:, 2 + bb, META:T], ALU.add)))
            pool.wait_ge(gelu_ok, it + 1)
            for bb in range(2):
                ch.need(marks[bb])
                nc.gpsimd.sem_inc(flush, 1)
                dst = rec[:, bass.ds(r + bb, 1), :].rearrange("p a t -> p (a t)")
                nc.gpsimd.tensor_tensor(dst, dst, a2[bb][:, 0:SEQ], ALU.mult).then_inc(rec_ok, 1)
        ch.close(4)

        with pool.Fori(0, KT) as m:
            pool.wait_ge(ml_ok, m)
            pool.wait_ge(m2_ok, m + 1)
            nc.gpsimd.tensor_tensor(ms[:, :], m2[:, 0, :], m2[:, 1, :], ALU.add).then_inc(ms_ok, 1)

        pool.wait_ge(lg_ok, 1)
        nc.gpsimd.iota(io_r[:, :], pattern=[[1, CHUNK]], base=0, channel_multiplier=0,
                       allow_small_or_imprecise_dtypes=True)
        nc.gpsimd.iota(io_c[:, :], pattern=[[1, NIDX]], base=0, channel_multiplier=0,
                       allow_small_or_imprecise_dtypes=True).then_inc(iota_ok, 1)
        pool.wait_ge(n2_out, 16 * TT)
        pool.wait_ge(route_ok, 1)
        total = pool.value_load(ends[0:1, N_E:N_E + 1], min_val=N_E, max_val=MAXC)
        with pool.Fori(0, total + 1) as c:
            pool.wait_ge(g_in, c * 16)
            pool.sem_inc(flush, 1)
            nc.gpsimd.tensor_copy(idx_now[:, :], idx[:, bass.ds(c, 1)]).then_inc(idx_ok, 1)
            pool.wait_ge(idx_ok, c + 1)
            pool.wait_ge(xt_full, c)
            pool.sem_inc(flush, 1)
            pool.indirect_dma_start(G[:, :], None, n2_dram[:, :],
                                    bass.IndirectOffsetOnAxis(ap=idx_now[:, :], axis=0)).then_inc(g_in, 16)
        pool.wait_ge(y_out, total * 16)
        pool.sem_inc(flush, 1)
        for i in range(TT):
            for j in range(2):
                pool.indirect_dma_start(F[j][:, i, :], None, y_dram[:, :],
                                        bass.IndirectOffsetOnAxis(ap=slot_i[j][:, i:i + 1], axis=0)
                                        ).then_inc(f_in[2 * i + j], 16)

    @block.scalar
    def _(act):
        ch = Chain(act, act_chain)
        rows = lambda v: v.rearrange("(b c) -> b c", c=P)
        act.dma_start(prm[0:32, :], conv_w[0].rearrange("i (b c) -> (i b) c", c=P)).then_inc(prm_in, 16)
        act.dma_start(prm[32:40, :], rows(conv_b[0])).then_inc(prm_in, 16)
        act.dma_start(prm[40:56, :], lru_b_a[0].rearrange("r (b c) -> (r b) c", c=P)).then_inc(prm_in, 16)
        act.dma_start(prm[56:72, :], lru_b_x[0].rearrange("r (b c) -> (r b) c", c=P)).then_inc(prm_in, 16)
        act.dma_start(prm[72:88, :], lru_lambda[0].rearrange("r (b c) -> (r b) c", c=P)).then_inc(prm_in, 16)
        act.dma_start(prm[88:96, :], rows(norm_mix_g[0])).then_inc(prm_in, 16)
        act.dma_start(prm[96:104, :], rows(norm_ffn_g[0])).then_inc(prm_in, 16)
        act.dma_start(PV[:, 14, :], attn_sink[0].partition_broadcast(P)).then_inc(prm_in, 16)
        act.dma_start(wrt[:, :, 0:N_G], w_group[0].rearrange("(k p) g -> p k g", p=P)).then_inc(wrt_in, 16)
        act.dma_start(wrt[:, :, N_G:N_G + N_E], w_router[0].rearrange("(k p) g -> p k g", p=P)).then_inc(wrt_in, 16)
        act.dma_start(bias_r[:, 0:N_G], b_group[0].partition_broadcast(P)).then_inc(wrt_in, 16)
        act.dma_start(bias_r[:, N_G:N_G + N_E], b_router[0].partition_broadcast(P)).then_inc(wrt_in, 16)

        act.wait_ge(const_ok, 1)
        for i in range(TT):
            act.wait_ge(x_in[i], 16)
            ch.link(nc.scalar.activation(junk[:, :], X[:, i, :], ACT.Square, accum_out=stat[:, 0, i:i + 1]))
        act.wait_ge(meta_in, 16)
        nc.scalar.activation(junk[0:META, :], msb[:, :], ACT.Square,
                             accum_out=stat[0:META, 0, TT:TT + 1]).then_inc(ssq_ok, 1)
        act.wait_ge(var_ok, 1)
        nc.scalar.activation(stat[:, 2, :], stat[:, 1, :], ACT.Sqrt).then_inc(std_ok, 1)
        act.wait_ge(lam_abs_ok, 1)
        nc.scalar.activation(spt[:, 1, :], spt[:, 0, :], ACT.Exp, scale=-1.0).then_inc(lam_exp_ok, 1)

        def split_hi(phase, u, it=0):
            s, n = unit(phase, u, it)
            act.wait_ge(w_in_ok[s], w_in_target(phase, u, it))
            if not (is_const(n) and n == 0):
                act.wait_ge(w_used[s], n)
            nc.scalar.activation(w_hi[s][:, :, :], w_raw[s][:, :, :], ACT.Copy).then_inc(w_hi_ok[s], 1)

        split_hi("kv", 0)
        split_hi("kv", 1)
        for k in range(KT):
            p = k % 2
            act.wait_ge(nt_full, k + 1)
            if k == 0:
                act.wait_ge(par_ok, 1)
            nc.scalar.activation(nT_hi[:, k, 0:400], pj[:, 2 * p, 0:400], ACT.Copy, scale=g12[:, 0, k:k + 1])
            nc.scalar.activation(nT_hi[:, k, 400:T], pj[:, 2 * p + 1, 0:P], ACT.Copy, scale=g12[:, 0, k:k + 1]
                                 ).then_inc(nT_hi_ok, 1)

        for kv in range(KV):
            split_hi("kv", kv + 2) if kv == 0 else None
            p = kv
            made(act, "kv", kv)
            nc.scalar.activation(kT_hi[:, kv, :].rearrange("p (h c) -> p h c", h=2), pj[:, 2 * p:2 * p + 2, 0:HALF],
                                 ACT.Copy).then_inc(k_hi_ok, 1)
        split_hi("kv", 3)
        for c in range(2):
            split_hi("kv", 4 + c) if c == 0 else None
            p = c
            made(act, "kv", 2 + c)
            nc.scalar.activation(V[:, 1:TT + 1, c * P:(c + 1) * P],
                                 pj[:, 2 * p, :].rearrange("p (t c) -> p t c", c=P), ACT.Copy)
            nc.scalar.activation(V[:, 0, c * P:(c + 1) * P], pj[:, 2 * p + 1, 0:P], ACT.Copy
                                 ).then_inc(v_rows_ok, 1)
        split_hi("kv", 5)
        ch.close()

        act.wait_ge(y_zeroed, 16 * (MAXC - N_E))
        with act.Fori(0, 4) as it:
            ch.body(it, 6)
            r = act.snap(it * 2)
            act.wait_ge(tt_ok, it * 8)
            act.sem_inc(flush, 1)
            nc.scalar.activation(cur[:, :, :], PV[:, :, bass.ds(r, 2)], ACT.Copy).then_inc(cur_ok, 1)
            act.wait_ge(cur_ok, it + 1)
            split_hi("mix", 2, it)
            for bb in range(2):
                p = bb
                act.wait_ge(xc_ok, it * 2)
                made(act, "mix", bb, it)
                nc.scalar.activation(xr[:, bb, 2:T + 2].rearrange("p (h c) -> p h c", h=2),
                                     pj[:, 2 * p:2 * p + 2, 0:HALF], ACT.Copy).then_inc(xr_ok, 1)
                split_hi("mix", 3 + bb, it)
            s4, n4 = unit("mix", 4, it)
            for bb in range(2):
                act.wait_ge(xc_ok, it * 2 + (bb + 1))
                act.wait_ge(w_used[s4], n4)
                nc.scalar.activation(xc_hi[:, bb, :], xc[:, bb, :], ACT.Copy).then_inc(xch_ok, 1)
            split_hi("mix", 5, it)
            p = 0
            made(act, "mix", 3, it)
            act.wait_ge(s_full, it * 8)
            nc.scalar.activation(qT_hi[:, :, :], pj[:, 2 * p:2 * p + 2, :], ACT.Copy, scale=HD ** -0.5
                                 ).then_inc(qh_ok, 1)

            def lru_a(j, bd):
                d, bb = divmod(bd, 2)
                o = META * d
                act.wait_ge(scan_ok, it * 4)
                act.wait_ge(rec_ok, it * 2)
                p = j % 2
                if j == 8:
                    made(act, "mix", 4, it)
                else:
                    act.wait_ge(lru_full, it * 5 + (j - 2))
                if d == 0:
                    two = lambda t: t.rearrange("p (h c) -> p h c", h=2)
                    nc.scalar.activation(two(ab[:, bd, :]), pj[:, 2 * p:2 * p + 2, 0:HALF], ACT.Tanh,
                                         bias=cur[:, 5, bb:bb + 1], scale=0.5).then_inc(tha_ok, 1)
                    return None
                q = ch.mark(nc.scalar.activation(ab[:, bd, o:T], pj[:, 2 * p, :], ACT.Tanh,
                                                 bias=cur[:, 6, bb:bb + 1], scale=0.5))
                nc.scalar.activation(vb[:, bd, o:T], pj[:, 2 * p + 1, :], ACT.Tanh, bias=cur[:, 8, bb:bb + 1],
                                     scale=0.5).then_inc(thi_ok, 1)
                return q

            def lru_x(j, bb):
                p = j % 2
                act.wait_ge(lru_full, it * 5 + (j - 2))
                nc.scalar.activation(vb[:, bb, :].rearrange("p (h c) -> p h c", h=2), pj[:, 2 * p:2 * p + 2, 0:HALF],
                                     ACT.Tanh, bias=cur[:, 7, bb:bb + 1], scale=0.5).then_inc(thi_ok, 1)

            def lru_decay(q, bd):
                d, bb = divmod(bd, 2)
                o = META * d
                if q is None:
                    act.wait_ge(tha_ok, it * 2 + (bb + 1))
                else:
                    ch.need(q)
                q2 = ch.mark(nc.scalar.activation(wb[:, bd, o:T], ab[:, bd, o:T], ACT.Tanh,
                                                  bias=cur[:, 11 + d, bb:bb + 1], scale=cur[:, 11 + d, bb:bb + 1]))
                ch.need(q2)
                nc.scalar.activation(ab[:, bd, o:T], ab[:, bd, o:T], ACT.Exp,
                                     bias=cur[:, 9 + d, bb:bb + 1], scale=cur[:, 9 + d, bb:bb + 1]).then_inc(a_ok, 1)

            def exps(a):
                hh, j = divmod(a, 4)
                act.wait_ge(neg_ok, it * 8 + (a + 1))
                if a < 4:
                    act.wait_ge(onorm_ok, it * 2)
                w = S_W[j + 1]
                nc.scalar.activation(s_sb[a % 2][:, 0:w], s_sb[a % 2][:, 0:w], ACT.Exp, bias=nmax[:, hh, j:j + 1],
                                     accum_out=rsum[:, hh, j:j + 1]).then_inc(p_ok, 1)

            def exp_sink(hh):
                act.wait_ge(onorm_ok, it * 2 + hh)
                nc.scalar.activation(esink[:, :], nmax[:, hh, :], ACT.Exp, bias=cur[:, 14, hh:hh + 1]
                                     ).then_inc(es_ok, 1)

            def evac_o(hh):
                act.wait_ge(pt_full, it * 10 + OT_N[hh])
                act.sem_inc(flush, 1)
                nc.scalar.activation(attn[:, bass.ds(r + hh, 1), :].rearrange("p a t -> p (a t)"), pt_ps[:, :],
                                     ACT.Copy).then_inc(pt_free, 1)

            q0 = lru_a(3, 0)
            lru_x(4, 0)
            exps(0)
            q1 = lru_a(5, 2)
            lru_decay(q0, 0)
            exps(1)
            lru_decay(q1, 2)
            q2 = lru_a(6, 1)
            exps(2)
            lru_x(7, 1)
            exps(3)
            exp_sink(0)
            q3 = lru_a(8, 3)
            split_hi("mix", 6, it)
            exps(4)
            lru_decay(q2, 1)
            lru_decay(q3, 3)
            exps(5)
            split_hi("mix", 7, it)
            exps(6)
            evac_o(0)
            exps(7)
            exp_sink(1)
            act.wait_ge(w_ok, it * 4 + 4)
            for d in range(2):
                o = META * d
                nc.scalar.activation(wb[:, 2 * d:2 * d + 2, o:T], wb[:, 2 * d:2 * d + 2, o:T], ACT.Sqrt, scale=0.25
                                     ).then_inc(sq_ok, 1)
            p = 1
            made(act, "mix", 6, it)
            act.sem_inc(flush, 1)
            nc.scalar.activation(rec[:, bass.ds(r, 2), :], pj[:, 2 * p:2 * p + 2, :], ACT.Gelu_apprx_tanh
                                 ).then_inc(gelu_ok, 1)
            act.wait_ge(gelu_ok, it + 1)
            evac_o(1)
            split_hi("mix", 8, it)
        ch.close(4)

        act.wait_ge(o_done, 32)
        act.wait_ge(onorm_ok, 8)
        act.wait_ge(pt_free, 40)
        act.wait_ge(rec_ok, KT)
        nc.scalar.activation(attn_hi[:, :, :], attn[:, :, :], ACT.Copy).then_inc(br_hi_ok, 1)
        nc.scalar.activation(rec_hi[:, :, :], rec[:, :, :], ACT.Copy).then_inc(br_hi_ok, 1)
        with act.Fori(0, KT) as m:
            split_hi("branch", 2, m)
            p = 0
            act.wait_ge(m2_ok, m)
            made(act, "branch", 1, m)
            nc.scalar.activation(g_sb[:, :, :], pj[:, 2 * p:2 * p + 2, :], ACT.Tanh, scale=0.5
                                 ).then_inc(gate_ok, 1)
            split_hi("branch", 3, m)
            split_hi("branch", 4, m)
            act.wait_ge(ms_ok, m + 1)
            act.sem_inc(flush, 1)
            nc.scalar.activation(mg_hi[:, bass.ds(m, 1), :].rearrange("p a t -> p (a t)"), ms[:, :], ACT.Copy,
                                 scale=0.5).then_inc(mh_ok, 1)
            split_hi("branch", 5, m)

        def out_run(it, last):
            for j in range(2):
                p = j
                act.wait_ge(oT_full, it * 2 + j)
                made(act, "out", j, it)
                nc.scalar.activation(oT_sb[j][:, :], pj[:, 2 * p, :], ACT.Copy).then_inc(oT_ok, 1)
                if not last:
                    split_hi("out", 2 + j, it)

        with act.Fori(0, 3) as it:
            out_run(it, False)
        out_run(3, True)

        act.wait_ge(h_ok, KT)
        for i in range(TT):
            q = ch.mark(nc.scalar.activation(xn2[:, i, :], X[:, i, :], ACT.Square, accum_out=stat2[:, 0, i:i + 1]))
            ch.need(q)
        nc.scalar.activation(oT_sb[0][:, 0:1], oT_sb[0][:, 1:2], ACT.Copy).then_inc(ssq2_ok, 1)
        act.wait_ge(var2_ok, 1)
        nc.scalar.activation(stat2[:, 2, :], stat2[:, 1, :], ACT.Sqrt).then_inc(std2_ok, 1)
        for k in range(KT):
            act.wait_ge(rt_full, k + 1)
            nc.scalar.activation(n2T[:, k, :], pj[:, k % 4, :], ACT.Copy, scale=g12[:, 1, k:k + 1]
                                 ).then_inc(rt_free, 1)
        act.wait_ge(gd_ok, 1)
        nc.scalar.activation(gex[:, :, :], gex[:, :, :], ACT.Exp).then_inc(gexp_ok, 1)
        act.wait_ge(ed_ok, 1)
        nc.scalar.activation(r1[3][:, :], r1[3][:, :], ACT.Exp).then_inc(eexp_ok, 1)

        act.wait_ge(route_ok, 1)

        def chunk(c):
            act.wait_ge(gate_done, c + 1)
            act.wait_ge(hid_ok, c)
            nc.scalar.activation(sg[:, :, :].rearrange("p f c -> p (f c)"), pj[:, 0, 0:FT * CHUNK], ACT.Silu
                                 ).then_inc(silu_ok, 1)
            row = act.snap(c * CHUNK)
            act.wait_ge(y_out, c * 16)
            act.wait_ge(y_full, c + 1)
            nc.scalar.activation(y_sb[:, 0:512], s_ps[0:CHUNK, 0, :], ACT.Copy).then_inc(y_evac_a, 1)
            act.wait_ge(y_evac_a, c + 1)
            act.wait_ge(y_evac_d, c + 1)
            act.dma_start(y_dram[bass.ds(row, CHUNK), :], y_sb[:, :]).then_inc(y_out, 16)

        total = act.value_load(ends[0:1, N_E:N_E + 1], min_val=N_E, max_val=MAXC)
        with act.Fori(0, total) as c:
            chunk(c)

        for i in range(TT):
            act.wait_ge(hf_ok, i + 1)
            act.wait_ge(fo_ok, i)
            if i >= 2:
                act.wait_ge(out_done[i % 2], 16 * (i // 2))
            nc.scalar.activation(fo[:, i % 2, :], X[:, i, :], ACT.Square, accum_out=stat3[:, 0, i:i + 1]
                                 ).then_inc(ssq3_ok, 1)
            act.wait_ge(var3_ok, i + 1)
            nc.scalar.activation(stat3[:, 2, i:i + 1], stat3[:, 1, i:i + 1], ACT.Sqrt).then_inc(std3_ok, 1)

    @block.vector
    def _(dve):
        ch = Chain(dve, dve_chain)
        V_ = nc.vector
        ch.link(V_.memset(pt_ps[:, :], 0.0))
        dve.wait_ge(ssq_ok, 1)
        V_.tensor_scalar(stat[:, 1, :], stat[:, 0, :], 1.0 / D, EPS, ALU.mult, ALU.add).then_inc(var_ok, 1)
        dve.wait_ge(std_ok, 1)
        ch.link(V_.reciprocal(stat[:, 0, :], stat[:, 2, :]))
        for i in range(TT):
            V_.tensor_scalar(xn[:, i, :], X[:, i, :], stat[:, 0, i:i + 1], None, ALU.mult).then_inc(xn_ok, 1)
        V_.tensor_scalar(mn[:, :], msb[:, :], stat[0:META, 0, TT:TT + 1], None, ALU.mult).then_inc(xn_ok, 1)
        dve.wait_ge(prmT_ok, 1)
        tp = s_ps[:, 0, 0:104]
        V_.tensor_copy(PV[:, 0:5, :], tp[:, 0:40].rearrange("p (g b) -> p g b", b=8))
        V_.tensor_scalar(PV[:, 5:9, :], tp[:, 40:72].rearrange("p (g b) -> p g b", b=8), 0.5, None, ALU.mult)
        V_.tensor_copy(g12[:, :, :], tp[:, 88:104].rearrange("p (g b) -> p g b", b=8))
        ch.link(V_.tensor_copy(spt[:, 2, :], tp[:, 72:88]))
        lam = spt[:, 2, :]
        ch.link(V_.tensor_scalar(spt[:, 3, :], lam, -1.0, None, ALU.mult))
        V_.tensor_tensor(spt[:, 0, :], lam, spt[:, 3, :], ALU.max).then_inc(lam_abs_ok, 1)
        ch.link(V_.tensor_scalar(spt[:, 3, :], spt[:, 3, :], 0.0, None, ALU.max))
        dve.wait_ge(lam_exp_ok, 1)
        e_, s_, z_, p_ = spt[:, 1, :], spt[:, 4, :], spt[:, 5, :], spt[:, 6, :]
        ch.link(V_.tensor_scalar(s_, e_, 2.0, None, ALU.add))
        ch.link(V_.reciprocal(z_, s_))
        ch.link(V_.tensor_tensor(s_, e_, z_, ALU.mult))
        ch.link(V_.tensor_tensor(z_, s_, s_, ALU.mult))
        ch.link(V_.tensor_scalar(p_, z_, 2.0 / 19, None, ALU.mult))
        for k in range(8, 0, -1):
            ch.link(V_.scalar_tensor_tensor(p_, p_, 2.0 / (2 * k + 1), z_, ALU.add, ALU.mult))
        ch.link(V_.scalar_tensor_tensor(p_, p_, 2.0, s_, ALU.add, ALU.mult))
        ch.link(V_.tensor_tensor(p_, p_, spt[:, 3, :], ALU.add))
        p2 = p_.rearrange("p (g b) -> p g b", b=8)
        V_.tensor_scalar(PV[:, 9:11, :], p2, -4.0, None, ALU.mult)
        V_.tensor_scalar(PV[:, 11:13, :], p2, 4.0, None, ALU.mult).then_inc(par_ok, 1)

        def split_lo(phase, u, it=0):
            s, n = unit(phase, u, it)
            dve.wait_ge(w_hi_ok[s], n + 1)
            V_.tensor_tensor(w_lo[s][:, :, :], w_raw[s][:, :, :], w_hi[s][:, :, :].bitcast(F32), ALU.subtract
                             ).then_inc(w_lo_ok[s], 1)

        split_lo("kv", 0)
        split_lo("kv", 1)
        for k in range(KT):
            p = k % 2
            dve.wait_ge(nT_hi_ok, k + 1)
            V_.scalar_tensor_tensor(nT_lo[:, k, 0:400], pj[:, 2 * p, 0:400], g12[:, 0, k:k + 1],
                                    nT_hi[:, k, 0:400].bitcast(F32), ALU.mult, ALU.subtract)
            V_.scalar_tensor_tensor(nT_lo[:, k, 400:T], pj[:, 2 * p + 1, 0:P], g12[:, 0, k:k + 1],
                                    nT_hi[:, k, 400:T].bitcast(F32), ALU.mult, ALU.subtract).then_inc(nt_lo_ok, 1)

        for kv in range(KV):
            split_lo("kv", 2) if kv == 0 else None
            p = kv
            dve.wait_ge(k_hi_ok, kv + 1)
            two = lambda t: t.rearrange("p (h c) -> p h c", h=2)
            V_.tensor_tensor(two(kT_lo[:, kv, :]), pj[:, 2 * p:2 * p + 2, 0:HALF], two(kT_hi[:, kv, :]).bitcast(F32),
                             ALU.subtract).then_inc(k_lo_ok, 1)
        split_lo("kv", 3)
        split_lo("kv", 4)
        split_lo("kv", 5)
        ch.close()

        with dve.Fori(0, 4) as it:
            ch.body(it, 10)
            dve.wait_ge(cur_ok, it + 1)
            dve.wait_ge(pad_ok, 1)
            split_lo("mix", 2, it)
            for bb in range(2):
                dve.wait_ge(xr_ok, it * 2 + (bb + 1))
                ch.link(V_.tensor_scalar(xc[:, bb, :], xr[:, bb, 0:T], cur[:, 0, bb:bb + 1], cur[:, 4, bb:bb + 1],
                                         ALU.mult, ALU.add))
                for i in range(1, 4):
                    ins = V_.scalar_tensor_tensor(xc[:, bb, :], xr[:, bb, i:i + T], cur[:, i, bb:bb + 1],
                                                  xc[:, bb, :], ALU.mult, ALU.add)
                    ch.link(ins) if i < 3 else ins.then_inc(xc_ok, 1)
                split_lo("mix", 3 + bb, it)
            for bb in range(2):
                dve.wait_ge(xch_ok, it * 2 + (bb + 1))
                V_.tensor_tensor(xc_lo[:, bb, :], xc[:, bb, :], xc_hi[:, bb, :].bitcast(F32), ALU.subtract
                                 ).then_inc(xcl_ok, 1)
            split_lo("mix", 5, it)
            p = 0
            dve.wait_ge(qh_ok, it + 1)
            V_.scalar_tensor_tensor(qT_lo[:, :, :], pj[:, 2 * p:2 * p + 2, :], HD ** -0.5,
                                    qT_hi[:, :, :].bitcast(F32), ALU.mult, ALU.subtract).then_inc(q_ok, 1)

            def scores(a):
                hh, j = divmod(a, 4)
                w, o = S_W[j + 1], S_ND[j + 1]
                dve.wait_ge(s_full, it * 8 + (a + 1))
                dve.wait_ge(ndh_ok, it * 2 + (hh + 1))
                dve.wait_ge(pt_full, it * 10 + (PT_N[a - 2] if a >= 2 else 0))
                dve.sem_inc(flush, 1)
                V_.tensor_tensor_reduce(s_sb[a % 2][:, 0:w], ndh[:, o:o + w], s_ps[:, a % 2, 0:w], 1.0,
                                        cur[:, 14, hh:hh + 1], ALU.add, ALU.max, mx[:, hh, j:j + 1]
                                        ).then_inc(tt_ok, 1)
                dve.wait_ge(tt_ok, it * 8 + (a + 1))
                V_.tensor_scalar(nmax[:, hh, j:j + 1], mx[:, hh, j:j + 1], -1.0, None, ALU.mult).then_inc(neg_ok, 1)

            def evac_pt(a):
                nb = len(S_V[a % 4 + 1]) + 1
                dve.wait_ge(o_done, it * 8 + (a - 1 if a >= 2 else 0))
                dve.wait_ge(pt_full, it * 10 + PT_N[a])
                V_.tensor_copy(pt_sb[a % 2][:, 0:nb * P], pt_ps[:, 0:nb * P]).then_inc(pt_free, 1)

            def gate_in(i, bd):
                d, bb = divmod(bd, 2)
                o = META * d
                dve.wait_ge(thi_ok, it * 4 + (i + 1))
                V_.scalar_tensor_tensor(vb[:, bd, o:T], vb[:, bd, o:T], 1.0, xc[:, bb, o:T], ALU.add, ALU.mult
                                        ).then_inc(v_ok, 1)

            def one_minus(i, bd):
                o = META * (bd // 2)
                dve.wait_ge(a2_ok, it * 4 + (i + 1))
                V_.scalar_tensor_tensor(wb[:, bd, o:T], a2[i % 2][:, o:T], 1.0, wb[:, bd, o:T], ALU.add, ALU.mult
                                        ).then_inc(w_ok, 1)

            def normalise(hh):
                dve.wait_ge(es_ok, it * 2 + (hh + 1))
                dve.wait_ge(p_ok, it * 8 + 4 * (hh + 1))
                ch.link(V_.tensor_tensor(den[:, :], rsum[:, hh, :], esink[:, :], ALU.add))
                ch.link(V_.reciprocal(den[:, :], den[:, :]))
                dve.wait_ge(o_done, it * 8 + 4 * (hh + 1))
                dve.wait_ge(pt_full, it * 10 + (OT_N[0] if hh else 0))
                V_.tensor_tensor(o_sb[:, :, :], o_ps[:, :].rearrange("p (j d) -> p j d", d=P),
                                 den[:, :].unsqueeze(2).broadcast_to([P, TT, P]), ALU.mult).then_inc(onorm_ok, 1)

            scores(0)
            scores(1)
            gate_in(0, 0)
            evac_pt(0)
            scores(2)
            gate_in(1, 2)
            one_minus(0, 0)
            evac_pt(1)
            scores(3)
            one_minus(1, 2)
            evac_pt(2)
            scores(4)
            gate_in(2, 1)
            evac_pt(3)
            scores(5)
            gate_in(3, 3)
            split_lo("mix", 6, it)
            normalise(0)
            evac_pt(4)
            scores(6)
            one_minus(2, 1)
            evac_pt(5)
            one_minus(3, 3)
            scores(7)
            split_lo("mix", 7, it)
            evac_pt(6)
            evac_pt(7)
            normalise(1)
            for bd in range(4):
                d = bd // 2
                dve.wait_ge(u_ok, it * 4 + (bd + 1))
                fw = lambda t: t[:, bd, META:T][:, ::-1] if d else t[:, bd, :]
                V_.tensor_tensor_scan(fw(wb), fw(ab), fw(vb), 0.0, ALU.mult, ALU.add).then_inc(scan_ok, 1)
            split_lo("mix", 8, it)
        ch.close(4)

        dve.wait_ge(br_hi_ok, 1)
        V_.tensor_tensor(attn_lo[:, :, :], attn[:, :, :], attn_hi[:, :, :].bitcast(F32), ALU.subtract
                         ).then_inc(br_lo_ok, 1)
        dve.wait_ge(br_hi_ok, 2)
        V_.tensor_tensor(rec_lo[:, :, :], rec[:, :, :], rec_hi[:, :, :].bitcast(F32), ALU.subtract
                         ).then_inc(br_lo_ok, 1)
        with dve.Fori(0, KT) as m:
            split_lo("branch", 2, m)
            split_lo("branch", 3, m)
            split_lo("branch", 4, m)
            dve.wait_ge(gate_ok, m + 1)
            dve.wait_ge(ms_ok, m)
            p = 1
            made(dve, "branch", 3, m)
            V_.scalar_tensor_tensor(m2[:, :, :], g_sb[:, :, :], 1.0, pj[:, 2 * p:2 * p + 2, :], ALU.add, ALU.mult
                                    ).then_inc(m2_ok, 1)
            dve.wait_ge(mh_ok, m + 1)
            one = lambda t: t[:, bass.ds(m, 1), :].rearrange("p a t -> p (a t)")
            V_.scalar_tensor_tensor(one(mg_lo), ms[:, :], 0.5, one(mg_hi).bitcast(F32), ALU.mult, ALU.subtract
                                    ).then_inc(ml_ok, 1)
            split_lo("branch", 5, m)

        def out_run(it, last):
            c = dve.snap(it * 256) if not is_const(it) else it * 256
            for j in range(2):
                if not last:
                    split_lo("out", 2 + j, it)
            for j in range(2):
                dve.wait_ge(oT_full, it * 2 + (j + 1))
                dst = X[:, :, bass.ds(c + j * P, P)]
                V_.tensor_tensor(dst, dst, s_ps[:, j, :].rearrange("p (i c) -> p i c", c=P), ALU.add
                                 ).then_inc(h_ok, 1)

        with dve.Fori(0, 3) as it:
            out_run(it, False)
        out_run(3, True)

        dve.wait_ge(ssq2_ok, 1)
        V_.tensor_scalar(stat2[:, 1, :], stat2[:, 0, :], 1.0 / D, EPS, ALU.mult, ALU.add).then_inc(var2_ok, 1)
        dve.wait_ge(std2_ok, 1)
        ch.link(V_.reciprocal(stat2[:, 0, :], stat2[:, 2, :]))
        for i in range(TT):
            V_.tensor_scalar(xn2[:, i, :], X[:, i, :], stat2[:, 0, i:i + 1], None, ALU.mult).then_inc(xn2_ok, 1)

        dve.wait_ge(wrt_in, 64)
        dve.wait_ge(lg_ok, 1)
        ch.link(V_.tensor_tensor(lg[:, :, :], o_ps[:, 0:TT * (N_G + N_E)].rearrange("p (i c) -> p i c", c=N_G + N_E),
                                 bias_r[:, :].unsqueeze(1).broadcast_to([P, TT, N_G + N_E]), ALU.add))
        b4 = lambda t: t[:, :].unsqueeze(2).broadcast_to([P, TT, 4])
        ie = iota_e[:, :].unsqueeze(1).broadcast_to([P, TT, 4])

        def first_max(vals, top, onehot, a, b, col):
            ch.link(V_.tensor_reduce(top[:, :], vals, AX.X, ALU.max))
            ch.link(V_.tensor_tensor(a[:, :, :], vals, b4(top), ALU.is_equal))
            ch.link(V_.scalar_tensor_tensor(a[:, :, :], a[:, :, :], -8.0, ie, ALU.mult, ALU.add))
            ch.link(V_.tensor_reduce(col[:, :], a[:, :, :], AX.X, ALU.min))
            ch.link(V_.tensor_scalar(col[:, :], col[:, :], 8.0, None, ALU.add))
            ch.link(V_.tensor_tensor(onehot[:, :, :], ie, b4(col), ALU.is_equal))

        gl = lg[:, :, 0:N_G]
        first_max(gl, r1[0], g1h, t4[0], t4[1], r1[1])
        V_.tensor_tensor(gex[:, :, :], gl, b4(r1[0]), ALU.subtract).then_inc(gd_ok, 1)
        ge = g1h[:, :, :].unsqueeze(3).broadcast_to([P, TT, N_G, E_G])
        for i in range(TT):
            V_.tensor_tensor(e16[:, i], lg[:, i, N_G:].rearrange("p (g e) -> p g e", e=E_G), ge[:, i], ALU.mult)
        ch.link(V_.memset(r1[7][:, :], 0.0))
        ch.link(V_.tensor_reduce(e_in[:, :, :], e16[:, :, :, :].rearrange("p i g e -> p i e g"), AX.X, ALU.add))
        first_max(e_in[:, :, :], r1[1], o1h[0], t4[0], t4[1], r1[2])
        ch.link(V_.scalar_tensor_tensor(e_in[:, :, :], o1h[0][:, :, :], -3e38, e_in[:, :, :], ALU.mult, ALU.add))
        first_max(e_in[:, :, :], r1[2], o1h[1], t4[0], t4[1], r1[4])
        V_.tensor_tensor(r1[3][:, :], r1[2][:, :], r1[1][:, :], ALU.subtract).then_inc(ed_ok, 1)
        for k in range(2):
            for i in range(TT):
                V_.tensor_tensor(m16[k][:, i], ge[:, i], o1h[k][:, i, :].unsqueeze(1).broadcast_to([P, N_G, E_G]),
                                 ALU.mult)
        ch.link(V_.memset(r1[7][:, :], 0.0))
        V_.tensor_tensor(m16[2][:, :, :, :].rearrange("p i g e -> p (i g e)"),
                         m16[0][:, :, :, :].rearrange("p i g e -> p (i g e)"),
                         m16[1][:, :, :, :].rearrange("p i g e -> p (i g e)"), ALU.add).then_inc(m_ok, 1)
        dve.wait_ge(gexp_ok, 1)
        ch.link(V_.tensor_reduce(r1[5][:, :], gex[:, :, :], AX.X, ALU.add))
        dve.wait_ge(eexp_ok, 1)
        ch.link(V_.tensor_scalar(r1[6][:, :], r1[3][:, :], 1.0, None, ALU.add))
        ch.link(V_.tensor_tensor(r1[6][:, :], r1[6][:, :], r1[5][:, :], ALU.mult))
        ch.link(V_.reciprocal(slot_w[0][:, :], r1[6][:, :]))
        ch.link(V_.tensor_tensor(slot_w[1][:, :], slot_w[0][:, :], r1[3][:, :], ALU.mult))
        dve.wait_ge(rank_ok, 1)
        dve.wait_ge(iota_ok, 1)
        cnt = o_ps[:, 128:128 + N_E]
        ch.link(V_.tensor_scalar(nch[:, :], cnt, thr[:, 0:1], 1.0, ALU.is_gt, ALU.add))
        for k in range(1, 5):
            ch.link(V_.scalar_tensor_tensor(nch[:, :], cnt, thr[:, k:k + 1], nch[:, :], ALU.is_gt, ALU.add))
        ch.link(V_.memset(endf[:, 0:1], 0.0))
        ch.link(V_.memset(ctmp[:, :], 1.0))
        ch.link(V_.tensor_tensor_scan(endf[:, 1:N_E + 1], ctmp[:, :], nch[:, :], 0.0, ALU.mult, ALU.add))
        ch.link(V_.tensor_copy(ends[:, :], endf[:, :]))
        ch.link(V_.tensor_copy(rank[:, :, :], o_ps[:, 0:TT * N_E].rearrange("p (i e) -> p i e", e=N_E)))
        ch.link(V_.tensor_scalar(fl[:, :, :], rank[:, :, :], thr[:, 0:1], None, ALU.is_ge))
        for k in range(1, 5):
            ch.link(V_.scalar_tensor_tensor(fl[:, :, :], rank[:, :, :], thr[:, k:k + 1], fl[:, :, :],
                                            ALU.is_ge, ALU.add))
        ch.link(V_.scalar_tensor_tensor(rank[:, :, :], fl[:, :, :], -float(CHUNK), rank[:, :, :], ALU.mult, ALU.add))
        ch.link(V_.tensor_tensor(fl[:, :, :], fl[:, :, :],
                                 endf[:, 0:N_E].unsqueeze(1).broadcast_to([P, TT, N_E]), ALU.add))
        for k in range(2):
            mk = m16[k][:, :, :, :].rearrange("p i g e -> p i (g e)")
            ch.link(V_.tensor_tensor(pr[:, :, :], rank[:, :, :], mk, ALU.mult))
            ch.link(V_.tensor_reduce(prow[k][:, :], pr[:, :, :], AX.X, ALU.add))
            ch.link(V_.tensor_tensor(pr[:, :, :], fl[:, :, :], mk, ALU.mult))
            ch.link(V_.tensor_reduce(pch[k][:, :], pr[:, :, :], AX.X, ALU.add))
            V_.scalar_tensor_tensor(slot_i[k][:, :], pch[k][:, :], float(CHUNK), prow[k][:, :], ALU.mult, ALU.add)
            for i in range(TT):
                V_.tensor_scalar(roh[:, 4 * k + i, :], io_r[:, :], prow[k][:, i:i + 1], None, ALU.is_equal)
                last = V_.tensor_scalar(coh[:, 4 * k + i, :], io_c[:, :], pch[k][:, i:i + 1], tok[:, i:i + 1],
                                        ALU.is_equal, ALU.mult)
        last.then_inc(oh_ok, 1)
        dve.wait_ge(idxp_ok, 1)
        V_.tensor_copy(idx[:, :], o_ps[0:CHUNK, 160:160 + NIDX]).then_inc(route_ok, 1)

        def take_x(c):
            dve.wait_ge(xt_full, c + 1)
            dve.wait_ge(up_done, c)
            V_.tensor_tensor(xT[:, :, :].rearrange("p (h k) c -> p h k c", h=2),
                             pj[:, 2:4, 0:4 * CHUNK].rearrange("p h (k c) -> p h k c", c=CHUNK),
                             g12[:, 1, :].rearrange("p (h k) -> p h k", h=2).unsqueeze(3)
                             .broadcast_to([P, 2, 4, CHUNK]), ALU.mult).then_inc(xt_ok, 1)

        dve.wait_ge(route_ok, 1)
        total = dve.value_load(ends[0:1, N_E:N_E + 1], min_val=N_E, max_val=MAXC)
        dve.wait_ge(xt_full, 1)
        take_x(0)
        with dve.Fori(0, total) as c:
            dve.wait_ge(silu_ok, c + 1)
            dve.wait_ge(y_full, c)
            dve.wait_ge(up_done, c + 1)
            V_.tensor_tensor(hT[:, :, :].rearrange("p f c -> p (f c)"), sg[:, :, :].rearrange("p f c -> p (f c)"),
                             pj[:, 1, 0:FT * CHUNK], ALU.mult).then_inc(hid_ok, 1)
            take_x(c + 1)
            dve.wait_ge(y_out, c * 16)
            dve.wait_ge(y_full, c + 1)
            V_.tensor_copy(y_sb[:, 512:1024], s_ps[0:CHUNK, 1, :]).then_inc(y_evac_d, 1)

        dve.wait_ge(gfin_in, 16)
        for i in range(TT):
            for j in range(2):
                dve.wait_ge(f_in[2 * i + j], 16)
                ins = V_.scalar_tensor_tensor(X[:, i, :], F[j][:, i, :], slot_w[j][:, i:i + 1], X[:, i, :],
                                              ALU.mult, ALU.add)
                ch.link(ins) if j == 0 else ins.then_inc(hf_ok, 1)
            dve.wait_ge(ssq3_ok, i + 1)
            V_.tensor_scalar(stat3[:, 1, i:i + 1], stat3[:, 0, i:i + 1], 1.0 / D, EPS, ALU.mult, ALU.add
                             ).then_inc(var3_ok, 1)
            dve.wait_ge(std3_ok, i + 1)
            ch.link(V_.reciprocal(stat3[:, 0, i:i + 1], stat3[:, 2, i:i + 1]))
            V_.scalar_tensor_tensor(fo[:, i % 2, :], X[:, i, :], stat3[:, 0, i:i + 1], gfin[:, :],
                                    ALU.mult, ALU.mult).then_inc(fo_ok, 1)

    @block.tensor
    def _(pe):
        mm, tp = nc.tensor.matmul, nc.tensor.transpose
        pe.wait_ge(const_ok, 1)
        pe.wait_ge(prm_in, 128)
        tp(s_ps[:, 0, 0:104], prm[:, :], ident[0:104, 0:104]).then_inc(prmT_ok, 1)
        pe.wait_ge(xn_ok, TT + 1)
        for k in range(KT):
            p = k % 2
            if k >= 2:
                pe.wait_ge(nt_lo_ok, k - 1)
            c = slice(k * P, (k + 1) * P)
            tp(pj[:, 2 * p, 0:META], mn[:, c], ident[0:META, 0:META])
            for i in range(TT - 1):
                tp(pj[:, 2 * p, META + i * P:META + (i + 1) * P], xn[:, i, c], ident[:, :])
            tp(pj[:, 2 * p + 1, 0:P], xn[:, TT - 1, c], ident[:, :]).then_inc(nt_full, 1)

        def weights(phase, u, it=0):
            s, n = unit(phase, u, it)
            pe.wait_ge(w_lo_ok[s], n + 1)
            return s, (w_hi[s], w_lo[s])

        def project_T(phase, u, it, p):
            s, w = weights(phase, u, it)
            for k in range(KT):
                for n, (i, j) in enumerate(PASSES):
                    for h in range(2):
                        st, sp_ = k == 0 and n == 0, k == KT - 1 and n == 2
                        last = mm(pj[:, 2 * p + h, 0:HALF], w[i][:, k, :], NT[j][:, k, h * HALF:(h + 1) * HALF],
                                  start=st, stop=sp_)
            last.then_inc(w_used[s], 1)

        def project(phase, u, it, dst, act_parts, k0=0, k1=KT, off=0):
            s, w = unit(phase, u, it)[0], None
            if k0 == 0:
                weights(phase, u, it)
            w = (w_hi[s], w_lo[s])
            for k in range(k0, k1):
                for n, (i, j) in enumerate(PASSES):
                    last = mm(dst, w[i][:, k, :], act_parts[j][:, k, off:off + SEQ],
                              start=k == 0 and n == 0, stop=k == KT - 1 and n == 2)
            if k1 == KT:
                last.then_inc(w_used[s], 1)

        pe.wait_ge(nt_lo_ok, KT)
        for kv in range(KV):
            project_T("kv", kv, 0, kv)
        for c in range(2):
            p = c
            pe.wait_ge(k_lo_ok, c + 1)
            s, w = weights("kv", 2 + c)
            for t in range(TT + 1):
                dst = pj[:, 2 * p, (t - 1) * P:t * P] if t else pj[:, 2 * p + 1, 0:P]
                o = META + (t - 1) * P if t else 0
                for k in range(KT):
                    for n, (i, j) in enumerate(PASSES):
                        last = mm(dst, NT[j][:, k, o:o + P], w[i][:, k, :],
                                  start=k == 0 and n == 0, stop=k == KT - 1 and n == 2)
            last.then_inc(w_used[s], 1)
        pe.wait_ge(v_rows_ok, 2)

        with pe.Fori(0, 4) as it:
            kv = pe.snap(it // 2)
            pe.wait_ge(thi_ok, it * 4)
            project_T("mix", 0, it, 0)
            pe.wait_ge(gelu_ok, it)
            project_T("mix", 1, it, 1)
            pe.wait_ge(xr_ok, it * 2 + 1)
            project("mix", 2, it, pj[:, 0, :], NT, off=META)
            project("mix", 3, it, pj[:, 1, :], NT, off=META)
            QT, K = (qT_hi, qT_lo), (kT_hi, kT_lo)

            def scores(a):
                hh, j = divmod(a, 4)
                w, k0 = S_W[j + 1], S_K[j + 1]
                if a == 0:
                    pe.wait_ge(q_ok, it + 1)
                    pe.wait_ge(k_hi_ok, KV)
                pe.wait_ge(tt_ok, it * 8 + max(a - 1, 0))
                parts = ((0, 0, w),) if k0 == 16 else ((0, 0, 16), (16, k0, w - 16))
                for d0, s0, n_ in parts:
                    for n, (i, l) in enumerate(PASSES):
                        last = mm(s_ps[:, a % 2, d0:d0 + n_], QT[i][:, hh, j * P:(j + 1) * P],
                                  K[l][:, bass.ds(kv, 1), s0:s0 + n_].rearrange("p a t -> p (a t)"),
                                  start=n == 0, stop=n == 2)
                last.then_inc(s_full, 1)

            def transpose_p(a):
                hh, j = divmod(a, 4)
                pe.wait_ge(p_ok, it * 8 + (a + 1))
                pe.wait_ge(pt_free, it * 10 + (PT_N[a] - 1))
                nb = len(S_V[j + 1])
                tp(pt_ps[0:META, 0:P], s_sb[a % 2][:, 0:META], ident[:, :])
                for b in range(nb):
                    last = tp(pt_ps[:, (b + 1) * P:(b + 2) * P], s_sb[a % 2][:, META + b * P:META + (b + 1) * P],
                              ident[:, :])
                last.then_inc(pt_full, 1)

            def values(a):
                hh, j = divmod(a, 4)
                if j == 0:
                    pe.wait_ge(onorm_ok, it * 2 + hh)
                pe.wait_ge(pt_free, it * 10 + PT_N[a])
                dst = o_ps[:, j * P:(j + 1) * P]
                vs = lambda r, t: V[r, t, bass.ds(vo, P)]
                for b, t in enumerate(S_V[j + 1]):
                    mm(dst, pt_sb[a % 2][:, (b + 1) * P:(b + 2) * P], vs(slice(0, P), t), start=b == 0, stop=False)
                mm(dst, pt_sb[a % 2][0:META, 0:P], vs(slice(0, META), 0), start=False, stop=True
                   ).then_inc(o_done, 1)

            def transpose_o(hh):
                pe.wait_ge(onorm_ok, it * 2 + (hh + 1))
                pe.wait_ge(pt_free, it * 10 + (OT_N[hh] - 1))
                for j in range(TT):
                    last = tp(pt_ps[:, j * P:(j + 1) * P], o_sb[:, j, :], ident[:, :])
                last.then_inc(pt_full, 1)

            def lru(j, bb, d, which):
                s = unit("mix", 4, it)[0]
                w = (w_hi[s], w_lo[s])
                XC = (xc_hi, xc_lo)
                p = j % 2
                if d == 0:
                    for n_, (i, l) in enumerate(PASSES):
                        for h in range(2):
                            last = mm(pj[:, 2 * p + h, 0:HALF], w[i][:, 4 * which + bb, :],
                                      XC[l][:, bb, h * HALF:(h + 1) * HALF], start=n_ == 0, stop=n_ == 2)
                else:
                    for q in range(2):
                        for n_, (i, l) in enumerate(PASSES):
                            last = mm(pj[:, 2 * p + q, :], w[i][:, 4 * q + 2 + bb, :], XC[l][:, bb, META:T],
                                      start=n_ == 0, stop=n_ == 2)
                last.then_inc(lru_full if j < 8 else w_used[s], 1)

            vo = pe.snap(kv * P)
            scores(0)
            scores(1)
            weights("mix", 4, it)
            pe.wait_ge(xcl_ok, it * 2 + 2)
            pe.wait_ge(xr_ok, it * 2 + 2)
            lru(3, 0, 0, 0)
            pe.wait_ge(q_ok, it + 1)
            lru(4, 0, 0, 1)
            pe.wait_ge(tha_ok, it * 2 + 1)
            lru(5, 0, 1, 0)
            transpose_p(0)
            scores(2)
            pe.wait_ge(thi_ok, it * 4 + 1)
            lru(6, 1, 0, 0)
            values(0)
            transpose_p(1)
            scores(3)
            pe.wait_ge(thi_ok, it * 4 + 2)
            lru(7, 1, 0, 1)
            values(1)
            transpose_p(2)
            scores(4)
            pe.wait_ge(tha_ok, it * 2 + 2)
            lru(8, 1, 1, 0)
            values(2)
            transpose_p(3)
            scores(5)
            pe.wait_ge(thi_ok, it * 4 + 3)
            y0, y1 = pj[:, 2, :], pj[:, 3, :]
            project("mix", 5, it, y0, NT, 0, 4, META)
            values(3)
            transpose_p(4)
            scores(6)
            project("mix", 5, it, y0, NT, 4, KT, META)
            transpose_o(0)
            values(4)
            transpose_p(5)
            scores(7)
            project("mix", 6, it, y1, NT, 0, 4, META)
            values(5)
            transpose_p(6)
            project("mix", 6, it, y1, NT, 4, KT, META)
            values(6)
            transpose_p(7)
            values(7)
            transpose_o(1)

        REC, ATT, MG = (rec_hi, rec_lo), (attn_hi, attn_lo), (mg_hi, mg_lo)

        def branch_gates(m):
            pe.wait_ge(gate_ok, m)
            project("branch", 0, m, pj[:, 0, :], NT, off=META)
            project("branch", 1, m, pj[:, 1, :], NT, off=META)

        def branch_pair(m):
            pe.wait_ge(m2_ok, m)
            project("branch", 2, m, pj[:, 2, :], ATT)
            project("branch", 3, m, pj[:, 3, :], REC)

        pe.wait_ge(thi_ok, 16)
        pe.wait_ge(gelu_ok, 4)
        with pe.Fori(0, KT) as m:
            branch_gates(m)
            pe.wait_ge(br_lo_ok, 2)
            branch_pair(m)

        def out_run(it):
            for j in range(2):
                pe.wait_ge(oT_ok, it * 2)
                if j == 0:
                    pe.wait_ge(ml_ok, KT)
                project("out", j, it, pj[:, 2 * j, :], MG)
            for j in range(2):
                pe.wait_ge(h_ok, it * 2)
                pe.wait_ge(oT_ok, it * 2 + (j + 1))
                for i in range(TT):
                    last = tp(s_ps[:, j, i * P:(i + 1) * P], oT_sb[j][:, i * P:(i + 1) * P], ident[:, :])
                last.then_inc(oT_full, 1)

        with pe.Fori(0, 4) as it:
            out_run(it)

        pe.wait_ge(xn2_ok, TT)
        for k in range(KT):
            if k >= 4:
                pe.wait_ge(rt_free, k - 3)
            for i in range(TT):
                last = tp(pj[:, k % 4, i * P:(i + 1) * P], xn2[:, i, k * P:(k + 1) * P], ident[:, :])
            last.then_inc(rt_full, 1)
        pe.wait_ge(rt_free, KT)
        pe.wait_ge(wrt_in, 64)
        NC = N_G + N_E
        for i in range(TT):
            for k in range(KT):
                last = mm(o_ps[:, i * NC:(i + 1) * NC], n2T[:, k, i * P:(i + 1) * P], wrt[:, k, :],
                          start=k == 0, stop=k == KT - 1)
        last.then_inc(lg_ok, 1)
        pe.wait_ge(m_ok, 1)
        mk = lambda i: m16[2][:, i].rearrange("p g e -> p (g e)")
        for i in range(TT):
            for l in range(i + 1):
                mm(o_ps[:, i * N_E:(i + 1) * N_E], (tri if l == i else ones)[:, :], mk(l), start=l == 0, stop=l == i)
        for i in range(TT):
            last = mm(o_ps[:, 128:128 + N_E], ones[:, :], mk(i), start=i == 0, stop=i == TT - 1)
        last.then_inc(rank_ok, 1)
        pe.wait_ge(oh_ok, 1)
        for i in range(8):
            last = mm(o_ps[0:CHUNK, 160:160 + NIDX], roh[:, i, :], coh[:, i, :], start=i == 0, stop=i == 7)
        last.then_inc(idxp_ok, 1)
        pe.wait_ge(route_ok, 1)

        def take_rows(c):
            pe.wait_ge(xt_ok, c)
            pe.wait_ge(g_in, c * 16 + 16)
            for k in range(KT):
                last = tp(pj[:, 2 + k // 4, (k % 4) * CHUNK:(k % 4 + 1) * CHUNK], G[:, k * P:(k + 1) * P],
                          ident[0:CHUNK, 0:CHUNK])
            last.then_inc(xt_full, 1)

        take_rows(0)

        def expert(s, e, round_):
            lo = pe.value_load(ends[0:1, bass.ds(e, 1)], min_val=0, max_val=MAXC)
            hi = pe.value_load(ends[0:1, bass.ds(e + 1, 1)], min_val=1, max_val=MAXC)
            pe.wait_ge(e_gate_in[s], round_ * 16 + 16)
            pe.wait_ge(e_up_in[s], round_ * 16 + 16)
            pe.wait_ge(e_down_in[s], round_ * 16 + 16)
            pe.sem_inc(flush, 1)
            with pe.Fori(lo, hi) as c:
                pe.wait_ge(silu_ok, c)
                pe.wait_ge(xt_ok, c + 1)
                for m in range(FT):
                    for k in range(KT):
                        last = mm(pj[:, 0, m * CHUNK:(m + 1) * CHUNK], wg_sb[s][:, k, m * P:(m + 1) * P], xT[:, k, :],
                                  start=k == 0, stop=k == KT - 1)
                last.then_inc(gate_done, 1)
                pe.wait_ge(hid_ok, c)
                for m in range(FT):
                    for k in range(KT):
                        last = mm(pj[:, 1, m * CHUNK:(m + 1) * CHUNK], wu_sb[s][:, k, m * P:(m + 1) * P], xT[:, k, :],
                                  start=k == 0, stop=k == KT - 1)
                last.then_inc(up_done, 1)
                take_rows(c + 1)
                pe.wait_ge(hid_ok, c + 1)
                pe.wait_ge(y_evac_a, c)
                pe.wait_ge(y_evac_d, c)
                for n in range(2):
                    for k in range(FT):
                        last = mm(s_ps[0:CHUNK, n, :], hT[:, k, :], wd_sb[s][:, k, n * 512:(n + 1) * 512],
                                  start=k == 0, stop=k == FT - 1)
                last.then_inc(y_full, 1)

        with pe.Fori(0, 5) as r:
            for s in range(3):
                expert(s, pe.snap(r * 3 + s), r)
        expert(0, 15, 5)

    ctx.close()


_INS = ['x', 'meta_tokens', 'norm_mix_g', 'w_in', 'conv_w', 'conv_b', 'lru_w_a', 'lru_b_a', 'lru_w_x', 'lru_b_x',
        'lru_lambda', 'attn_sink', 'w_attn_branch', 'w_rec_branch', 'w_out', 'norm_ffn_g', 'w_group', 'b_group',
        'w_router', 'b_router', 'moe_w_gate', 'moe_w_up', 'moe_w_down', 'final_norm_g']
_OUTS = [((1, SEQ, D), 'float32')]


def kernel(**inputs):
    import numpy as _np
    import concourse.bacc as _bacc
    from concourse import mybir as _mybir
    from concourse.bass_utils import run_bass_kernel_spmd as _run

    nc = _bacc.Bacc("TRN2", target_bir_lowering=False, num_devices=1)
    arrays, args = {}, []
    for name in _INS:
        a = _np.ascontiguousarray(inputs[name])
        arrays[f"in_{name}_dram"] = a
        args.append(nc.dram_tensor(f"in_{name}_dram", a.shape, _mybir.dt.from_np(a.dtype), kind="ExternalInput").ap())
    for i, (shape, dtype) in enumerate(_OUTS):
        dt = _mybir.dt.from_np(_np.dtype(dtype))
        args.append(nc.dram_tensor(f"out_{i}_dram", shape, dt, kind="ExternalOutput").ap())
    block_program(nc, *args)
    r = _run(nc, [arrays], core_ids=[0])
    return r.results[0]["out_0_dram"]
```

```python
import concourse.bass as bass
from concourse import mybir
from contextlib import ExitStack

P = 128
D = 1024
KT = D // P
SEQ = 512
META = 16
T = META + SEQ
HALF = T // 2
TT = SEQ // P
HEADS = 8
KV = 2
HD = 128
N_E = 16
N_G = 4
E_G = N_E // N_G
FF = 512
FT = FF // P
CHUNK = 128
MAXR = SEQ // CHUNK
MAXO = (2 * SEQ - 1) // CHUNK + 1
MAXC = N_E + MAXO
NIDX = MAXC + 2
UNITS = 6
RAW = 2 * UNITS
CONV = 4
EPS = 1e-6
COL_Q, COL_K, COL_V, COL_X, COL_Y, COL_GA, COL_GR = 0, 1024, 1280, 1536, 2560, 3584, 4608

F32 = mybir.dt.float32
F32R = mybir.dt.float32r
I32 = mybir.dt.int32
ACT = mybir.ActivationFunctionType
ALU = mybir.AluOpType
AX = mybir.AxisListType

PHASES = ["kv", "mix", "branch", "out"]
UNIT_SLOTS = {"kv": [0, 1, 2, 1], "mix": [0, 1, 2, 0, 1, 2, 1], "branch": [0, 1, 2, 1], "out": [0, 1]}
RUNS = {"kv": 1, "mix": 4, "branch": 8, "out": 4}

def unit(phase, u, it=0):
    slots = UNIT_SLOTS[phase]
    if u >= len(slots):
        return unit(phase, u - len(slots), it + 1)
    s = slots[u]
    before = 0
    for q in PHASES[:PHASES.index(phase)]:
        before += RUNS[q] * UNIT_SLOTS[q].count(s)
    before += slots[:u].count(s)
    return s, it * slots.count(s) + before


def w_in_target(phase, u, it=0):
    s, n = unit(phase, u, it)
    lru_slot = UNIT_SLOTS["mix"][4]
    extra = 0
    if s == lru_slot:
        order = PHASES.index(phase) * 1
        if phase == "mix":
            run, at = it, u
            if u >= 7:
                run, at = it + 1, u - 7
            extra = run * 32 + (32 if at >= 4 else 0)
        elif order > PHASES.index("mix"):
            extra = RUNS["mix"] * 32
    return n * 32 + 32 + extra


def is_const(v):
    return isinstance(v, int)


class Chain:

    def __init__(self, eng, sem):
        self.eng, self.sem, self.base, self.it, self.per, self.n = eng, sem, 0, 0, 0, 0

    def body(self, it, per):
        self.it, self.per, self.n = it, per, 0

    def mark(self, ins):
        ins.then_inc(self.sem, 1)
        self.n += 1
        return self.n

    def need(self, n):
        self.eng.wait_ge(self.sem, self.it * self.per + (self.base + n))

    def link(self, ins):
        self.need(self.mark(ins))

    def close(self, runs=1):
        assert runs == 1 or self.n == self.per, (self.n, self.per)
        self.base += runs * self.n
        self.it, self.per, self.n = 0, 0, 0


def block_program(nc, x, meta_tokens, norm_mix_g, w_in, conv_w, conv_b, lru_w_a, lru_b_a, lru_w_x, lru_b_x,
                  lru_lambda, attn_sink, w_attn_branch, w_rec_branch, w_out, norm_ffn_g, w_group, b_group,
                  w_router, b_router, moe_w_gate, moe_w_up, moe_w_down, final_norm_g, out):
    ctx = ExitStack()
    KB = 1024
    X_AT = 16512
    CONST_AT = X_AT + 16 * KB
    R1 = CONST_AT + 7 * KB
    REST = R1 + 68 * KB
    TAIL = REST + 96 * KB
    END = nc.sbuf_usable_end
    assert X_AT >= nc.sbuf_base

    class Region:

        def __init__(self, at, end):
            self.at, self.end = at, end

        def put(self, name, shape, dt=F32):
            size = 4
            for n in shape[1:]:
                size *= n
            t = nc.alloc_sbuf_tensor_at(name, shape, dt, offset=self.at)
            self.at += (size + 31) // 32 * 32
            assert self.at <= self.end, (name, self.at - self.end)
            return t

    X = Region(X_AT, CONST_AT).put("resid", [P, TT, D])
    cr = Region(CONST_AT, R1)
    ident = cr.put("ident", [P, P])
    nd_at = cr.at
    nd = cr.put("neg_dist", [P, 944])
    tri = cr.put("tri", [P, P])
    ones = cr.put("ones", [P, P])
    g12 = cr.put("g12", [P, 2, KT])
    stat = cr.put("norm_stat", [P, 3, TT + 1])
    stat2 = cr.put("norm_stat2", [P, 4, TT])
    stat3 = cr.put("norm_stat3", [P, 3, TT])
    thr = cr.put("chunk_thresholds", [P, MAXR - 1])
    even = cr.put("even_numbers", [P, MAXO // 2])
    iota_e = cr.put("iota_e", [P, 2, E_G])
    tok = cr.put("token_ids", [P, TT])
    bias_r = cr.put("router_bias", [P, N_G + N_E])
    wr = Region(R1, R1 + 36 * KB)
    w_raw = [wr.put(f"w_raw{s}", [P, KT, P]) for s in range(3)]
    w_hi = [wr.put(f"w_hi{s}", [P, KT, P], F32R) for s in range(3)]
    w_lo = [wr.put(f"w_lo{s}", [P, KT, P], F32R) for s in range(3)]
    n2t_hi = nc.alloc_sbuf_tensor_at("n2t_hi", [P, 2, SEQ], F32R, offset=R1 + 20 * KB)
    n2t_lo = nc.alloc_sbuf_tensor_at("n2t_lo", [P, 2, SEQ], F32R, offset=R1 + 32 * KB)
    lgT = nc.alloc_sbuf_tensor_at("logitsT", [N_G + N_E, SEQ], F32, offset=R1 + 8 * KB)
    mr = Region(R1 + 36 * KB, REST)
    kT_hi = mr.put("kT_hi", [P, KV, T], F32R)
    kT_lo = mr.put("kT_lo", [P, KV, T], F32R)
    V = mr.put("v_rows", [P, TT + 1, KV * HD])
    qT_hi = mr.put("qT_hi", [P, 2, SEQ], F32R)
    qT_lo = mr.put("qT_lo", [P, 2, SEQ], F32R)
    pt_sb = [mr.put(f"pt_sb{i}", [P, 4 * P]) for i in range(2)]
    o_sb = mr.put("o_sb", [P, TT, P])
    ndh = mr.put("neg_dist_h", [P, 944])
    rr = Region(REST, END)
    nT_hi = rr.put("nT_hi", [P, KT, T], F32R)
    nT_lo = rr.put("nT_lo", [P, KT, T], F32R)
    rec_at = rr.at
    rec = rr.put("rec", [P, KT, SEQ])
    attn = rr.put("attn", [P, KT, SEQ])
    PV = rr.put("par", [P, 15, 8])
    cur = rr.put("par_now", [P, 15, 2])
    nmax = rr.put("neg_max", [P, 2, TT])
    mx = rr.put("row_max", [P, 2, TT])
    rsum = rr.put("row_sum", [P, 2, TT])
    esink = rr.put("exp_sink", [P, TT])
    den = rr.put("denom", [P, TT])
    mix_at = rr.at
    ab = rr.put("lru_a", [P, 4, T])
    wb = rr.put("lru_w", [P, 4, T])
    vb = rr.put("lru_v", [P, 4, T])
    xr = rr.put("xr_pad", [P, 2, T + 4])
    xc = rr.put("xc", [P, 2, T])
    xc_hi = rr.put("xc_hi", [P, 2, T], F32R)
    xc_lo = rr.put("xc_lo", [P, 2, T], F32R)
    s_sb = [rr.put(f"s_sb{i}", [P, 400]) for i in range(2)]
    a2 = [rr.put(f"lru_a2_{i}", [P, T]) for i in range(2)]
    nr = Region(mix_at, END)
    xn = nr.put("xn_rows", [P, TT, D])
    msb = nr.put("meta_rows", [META, D])
    mn = nr.put("meta_n", [META, D])
    junk = nr.put("square_junk", [P, D])
    prm = nr.put("prm_rows", [104, P])
    spt = nr.put("softplus_tmp", [P, 8, 16])
    lo_r = Region(rec_at, mix_at)
    rec_lo = lo_r.put("rec_lo", [P, KT, SEQ], F32R)
    attn_lo = lo_r.put("attn_lo", [P, KT, SEQ], F32R)
    br = Region(mix_at, END)
    rec_hi = br.put("rec_hi", [P, KT, SEQ], F32R)
    attn_hi = br.put("attn_hi", [P, KT, SEQ], F32R)
    g_sb = br.put("gates", [P, 2, SEQ])
    m2 = br.put("gated", [P, 2, SEQ])
    ms = br.put("gated_sum", [P, SEQ])
    gr_ = Region(R1 + 36 * KB, REST)
    mg_hi = gr_.put("mergeT_hi", [P, KT, SEQ], F32R)
    mg_lo = gr_.put("mergeT_lo", [P, KT, SEQ], F32R)
    tr = Region(TAIL, END)
    xn2 = tr.put("xn2_rows", [P, TT, D])
    tail2 = tr.at
    oT_sb = [tr.put(f"oT_sb{i}", [P, SEQ]) for i in range(2)]
    rt = Region(tail2, END)
    lg = rt.put("logits", [P, TT, N_G + N_E])
    g1h = rt.put("group_onehot", [P, TT, N_G])
    gex = rt.put("group_exp", [P, TT, N_G])
    e_in = rt.put("e_in_group", [P, TT, E_G])
    e16 = rt.put("e_masked", [P, TT, N_G, E_G])
    o1h = [rt.put(f"expert_onehot{i}", [P, TT, E_G]) for i in range(2)]
    t4 = rt.put("tmp4", [P, TT, E_G])
    gtop, etop1, etop2, pick, ediff, gsum, wden = (
        rt.put(n, [P, TT]) for n in ("group_top", "expert_top1", "expert_top2", "picked", "expert_diff",
                                     "group_sum", "weight_den"))
    slot_w = [rt.put(f"pair_weight{i}", [P, TT]) for i in range(2)]
    slot_i = rt.put("pair_slot", [P, 2 * TT], I32)
    idx = rt.put("chunk_rows", [CHUNK, NIDX], I32)
    idx_now = [rt.put(f"chunk_rows_now{i}", [CHUNK, 1], I32) for i in range(2)]
    silu_warm = rt.put("silu_warm", [P, 1])
    table = rt.put("chunk_table", [P, MAXC + 3], I32)
    mz = Region(R1 + 48 * KB, REST)
    masks = mz.put("masks_by_choice", [P, 2, TT, N_G, E_G])
    both = mz.put("masks", [P, TT + 1, N_E])
    past = mz.put("masks_before", [P, TT + 1, N_E])
    tablef = mz.put("chunk_tablef", [P, MAXC + 3])
    nch = mz.put("n_overflow", [P, N_E])
    oend = mz.put("overflow_end", [P, N_E])
    obase = mz.put("overflow_base", [P, N_E])
    over9 = mz.put("overflow_past", [P, MAXO + 1, N_E])
    npair = mz.put("pairs_over", [P, MAXO // 2])
    pr = mz.put("pair_tmp", [P, 2 * TT, N_E])
    pex, pob, prk, pf1, pfl, pch, prow = (
        mz.put(n, [P, 2 * TT]) for n in ("pair_expert", "pair_base", "pair_rank", "pair_over", "pair_fold",
                                         "pair_chunk", "pair_row"))
    roh = mz.put("row_onehot", [P, 2 * TT, CHUNK], F32R)
    ceq = mz.put("chunk_equal", [P, 2 * TT, NIDX])
    coh = mz.put("chunk_onehot", [P, 2 * TT, NIDX], F32R)
    io_r = mz.put("iota_rows", [P, CHUNK])
    one16 = mz.put("one16", [P, N_E])
    assert mz.at <= R1 + 64 * KB
    er = Region(REST, TAIL)
    e_raw = [er.put(f"e_raw{s}", [P, 2048]) for s in range(RAW)]
    pre = Region(er.at - 16 * KB, er.at)
    wrt_hi = pre.put("router_w_hi", [P, KT, P], F32R)
    wrt_lo = pre.put("router_w_lo", [P, KT, P], F32R)
    g2row = pre.put("ffn_gain_rows", [P, D])
    ec = Region(R1, R1 + 64 * KB)
    e_hi, e_lo = [], []
    for s in range(CONV):
        e_hi.append(ec.put(f"e_hi{s}", [P, 2048], F32R))
        e_lo.append(ec.put(f"e_lo{s}", [P, 2048], F32R))
    eh = Region(R1 + 64 * KB, REST)
    hid = eh.put("chunk_hidden", [CHUNK, FF])
    hT_hi = eh.put("chunk_hT_hi", [P, FT, CHUNK], F32R)
    hT_lo = rt.put("chunk_hT_lo", [P, FT, CHUNK], F32R)
    er2 = Region(TAIL, TAIL + 16 * KB)
    G = [er2.put("chunk_rows_x0", [CHUNK, D]), nc.alloc_sbuf_tensor_at("chunk_rows_x1", [CHUNK, D], F32, offset=nd_at)]
    y_sb = er2.put("chunk_y", [CHUNK, D])
    xT_hi = er2.put("chunk_xT_hi", [P, KT, CHUNK], F32R)
    xT_lo = er2.put("chunk_xT_lo", [P, KT, CHUNK], F32R)
    fr = Region(REST, REST + 48 * KB)
    F = [fr.put(f"pair_rows{i}", [P, TT, D]) for i in range(2)]
    fo = fr.put("final_rows", [P, 2, D])
    gfin = fr.put("final_gain", [P, D])
    wrt = cr.put("router_w", [P, KT, N_G + N_E])

    n2_dram = nc.dram_tensor("n2_rows", [SEQ, D], F32, kind="Internal").ap()
    y_dram = nc.dram_tensor("y_rows", [MAXC * CHUNK, D], F32, kind="Internal").ap()

    pj = ctx.enter_context(nc.psum_tensor("pj", [P, 4, 512], F32))
    s_ps = ctx.enter_context(nc.psum_tensor("s_ps", [P, 2, 512], F32))
    pt_ps = ctx.enter_context(nc.psum_tensor("pt_ps", [P, 512], F32))
    o_ps = ctx.enter_context(nc.psum_tensor("o_ps", [P, 512], F32))

    v_ps = (pt_ps, o_ps)
    ht_ps = (pt_ps, o_ps)

    def sem(name):
        return ctx.enter_context(nc.semaphore(name))

    def sems(name, n):
        return [sem(f"{name}{i}") for i in range(n)]

    x_in = sems("x_in", TT)
    meta_in = sem("meta_in")
    prm_in = sem("prm_in")
    wrt_in = sem("wrt_in")
    gfin_in = sem("gfin_in")
    act_chain, dve_chain, pool_chain = sem("act_chain"), sem("dve_chain"), sem("pool_chain")
    const_ok = sem("const_ok")
    ssq_ok, var_ok, std_ok, xn_ok = sem("ssq_ok"), sem("var_ok"), sem("std_ok"), sem("xn_ok")
    prm_ok = sem("prm_ok")
    prmT_ok, lam_abs_ok, lam_exp_ok, par_ok = sem("prmT_ok"), sem("lam_abs_ok"), sem("lam_exp_ok"), sem("par_ok")
    nT_hi_ok = sem("nT_hi_ok")
    w_in_ok, w_hi_ok, w_lo_ok, w_used = sems("w_in_ok", 3), sems("w_hi_ok", 3), sems("w_lo_ok", 3), sems("w_used", 3)
    nt_full, nt_lo_ok = sem("nt_full"), sem("nt_lo_ok")
    k_hi_ok, k_lo_ok, v_rows_ok = sem("k_hi_ok"), sem("k_lo_ok"), sem("v_rows_ok")
    lru_full, tha_ok = sem("lru_full"), sem("tha_ok")
    cur_ok, xr_ok, xc_ok, xch_ok, xcl_ok = sem("cur_ok"), sem("xr_ok"), sem("xc_ok"), sem("xch_ok"), sem("xcl_ok")
    qh_ok, q_ok = sem("qh_ok"), sem("q_ok")
    s_full, tt_ok, neg_ok, p_ok = sem("s_full"), sem("tt_ok"), sem("neg_ok"), sem("p_ok")
    pt_full, pt_free, o_done, onorm_ok, es_ok, ndh_ok = (sem("pt_full"), sem("pt_free"), sem("o_done"),
                                                         sem("onorm_ok"), sem("es_ok"), sem("ndh_ok"))
    thi_ok, a_ok, a2_ok, w_ok, v_ok, sq_ok, u_ok, scan_ok, gelu_ok, rec_ok = (
        sem(n) for n in ("thi_ok", "a_ok", "a2_ok", "w_ok", "v_ok", "sq_ok", "u_ok", "scan_ok", "gelu_ok", "rec_ok"))
    br_hi_ok, br_lo_ok = sem("br_hi_ok"), sem("br_lo_ok")
    gate_ok, m2_ok, ms_ok, mh_ok, ml_ok = (sem(n) for n in ("gate_ok", "m2_ok", "ms_ok", "mh_ok", "ml_ok"))
    oT_ok, oT_full, h_ok = sem("oT_ok"), sem("oT_full"), sem("h_ok")
    ssq2_ok, var2_ok, std2_ok, xn2_ok = sem("ssq2_ok"), sem("var2_ok"), sem("std2_ok"), sem("xn2_ok")
    n2_out, rt_full, lg_ok = sem("n2_out"), sem("rt_full"), sem("lg_ok")
    wrt0_ok, wrt_hi_ok, wrt_ok = sem("wrt0_ok"), sem("wrt_hi_ok"), sem("wrt_ok")
    n2h_ok, n2l_ok, lg_mm, lgT_ok = (sem(n) for n in ("n2h_ok", "n2l_ok", "lg_mm", "lgT_ok"))
    table_ok = sem("table_ok")
    gd_ok, gexp_ok, ed_ok, eexp_ok, m_ok, rank_ok, oh_ok, idxp_ok, route_ok = (
        sem(n) for n in ("gd_ok", "gexp_ok", "ed_ok", "eexp_ok", "m_ok", "rank_ok", "oh_ok", "idxp_ok", "route_ok"))
    iota_ok, idx_ok = sem("iota_ok"), sem("idx_ok")
    g2_in = sem("g2_in")
    rstd_ok, mn_ok, gain_ok, vT_ok, v_full = (sem(n) for n in ("rstd_ok", "mn_ok", "gain_ok", "vT_ok", "v_full"))
    ew_in = sems("ew_in", RAW)
    e_hi_ok, e_lo_ok, e_used = sem("e_hi_ok"), sem("e_lo_ok"), sem("e_used")
    g_in, xt_full = sems("g_in", 2), sems("xt_full", 2)
    x_hi_ok, x_lo_ok, silu_ok, hid_ok, ht_full, h_hi_ok, h_lo_ok, y_ok, y_out = (
        sem(n) for n in ("x_hi_ok", "x_lo_ok", "silu_ok", "hid_ok", "ht_full", "h_hi_ok",
                         "h_lo_ok", "y_ok", "y_out"))
    f_in = sems("f_in", TT)
    out_done = sems("out_done", 2)
    ssq3_ok, var3_ok, std3_ok, hf_ok, fo_ok = (
        sem(n) for n in ("ssq3_ok", "var3_ok", "std3_ok", "hf_ok", "fo_ok"))
    flush = sem("flush")
    pad_ok, zero_ok, y_zeroed = sem("pad_ok"), sem("zero_ok"), sem("y_zeroed")

    def nt_ps(k, h):
        return (pj[:, 0, :], pj[:, 1, :], pj[:, 2, :], pj[:, 3, :], s_ps[:, 0, :], s_ps[:, 1, :])[2 * (k % 3) + h]

    def made(eng, phase, u, it=0):
        s, n = unit(phase, u, it)
        eng.wait_ge(w_used[s], n + 1)

    block = ctx.enter_context(nc.Block())

    w_in_v = w_in[0].rearrange("(k p) c -> p k c", p=P)
    wa_v = w_attn_branch[0].rearrange("(k p) c -> p k c", p=P)
    wr_v = w_rec_branch[0].rearrange("(k p) c -> p k c", p=P)
    wo_v = w_out[0].rearrange("(k p) c -> p k c", p=P)
    lwa_v = lru_w_a[0].rearrange("r b d e -> d r b e")
    lwx_v = lru_w_x[0].rearrange("r b d e -> d r b e")

    PASSES = ((0, 0), (0, 1), (1, 0))
    PASSES_X = ((0, 0), (0, 1), (1, 0))
    NT = (nT_hi, nT_lo)
    S_W = {1: 272, 2: 400, 3: 400, 4: 272}
    S_ND = {1: 0, 2: 272, 3: 272, 4: 672}
    S_K = {1: 16, 2: 16, 3: 144, 4: 272}
    S_V = {1: (1, 2), 2: (1, 2, 3), 3: (2, 3, 4), 4: (3, 4)}
    PT_N = {a: (a + 1 if a <= 4 else a + 2) for a in range(8)}
    OT_N = {0: 6, 1: 10}

    @block.sync
    def _(sp):
        for i in range(TT):
            sp.dma_start(X[:, i, :], x[0, i * P:(i + 1) * P, :]).then_inc(x_in[i], 16)
            if i == 0:
                sp.dma_start(msb[:, :], meta_tokens[:, :]).then_inc(meta_in, 16)

        rows = lambda v: v.rearrange("(b c) -> b c", c=P)
        sp.dma_start(prm[0:32, :], conv_w[0].rearrange("i (b c) -> (i b) c", c=P)).then_inc(prm_in, 16)
        sp.dma_start(prm[32:40, :], rows(conv_b[0])).then_inc(prm_in, 16)
        sp.dma_start(prm[40:56, :], lru_b_a[0].rearrange("r (b c) -> (r b) c", c=P)).then_inc(prm_in, 16)
        sp.dma_start(prm[56:72, :], lru_b_x[0].rearrange("r (b c) -> (r b) c", c=P)).then_inc(prm_in, 16)
        sp.dma_start(prm[72:88, :], lru_lambda[0].rearrange("r (b c) -> (r b) c", c=P)).then_inc(prm_in, 16)
        sp.dma_start(prm[88:96, :], rows(norm_mix_g[0])).then_inc(prm_in, 16)
        sp.dma_start(prm[96:104, :], rows(norm_ffn_g[0])).then_inc(prm_in, 16)
        sp.dma_start(PV[:, 14, :], attn_sink[0].partition_broadcast(P)).then_inc(prm_in, 16)

        def load_unit(phase, u, it, src):
            s, n = unit(phase, u, it)
            if not (is_const(n) and n == 0):
                sp.wait_ge(w_lo_ok[s], n)
                sp.sem_inc(flush, 1)
            for h in range(2):
                sp.dma_start(w_raw[s][:, 4 * h:4 * h + 4, :], src(h)).then_inc(w_in_ok[s], 16)

        def cols(view, c):
            return lambda h: view[:, 4 * h:4 * h + 4, bass.ds(c, P)]

        for u, c in enumerate((COL_K, COL_K + P, COL_V, COL_V + P)):
            load_unit("kv", u, 0, cols(w_in_v, c))
        sp.dma_start(wrt[:, :, 0:N_G], w_group[0].rearrange("(k p) g -> p k g", p=P)).then_inc(wrt_in, 16)
        sp.dma_start(wrt[:, :, N_G:N_G + N_E], w_router[0].rearrange("(k p) g -> p k g", p=P)).then_inc(wrt_in, 16)
        sp.dma_start(bias_r[:, 0:N_G], b_group[0].partition_broadcast(P)).then_inc(wrt_in, 16)
        sp.dma_start(bias_r[:, N_G:N_G + N_E], b_router[0].partition_broadcast(P)).then_inc(wrt_in, 16)
        sp.wait_ge(zero_ok, 1)
        for c in range(N_E, MAXC):
            sp.dma_start(y_dram[c * CHUNK:(c + 1) * CHUNK, :].rearrange("p (a t) -> p a t", a=2),
                         rec[0:CHUNK, 0:2, :]).then_inc(y_zeroed, 16)
        with sp.Fori(0, 4) as it:
            c = sp.snap(it * 256)
            b = sp.snap(it * 2)
            load_unit("mix", 0, it, cols(w_in_v, c + COL_X))
            load_unit("mix", 1, it, cols(w_in_v, c + (COL_X + P)))
            load_unit("mix", 2, it, cols(w_in_v, c + COL_Q))
            load_unit("mix", 3, it, cols(w_in_v, c + (COL_Q + P)))
            s, n = unit("mix", 4, it)
            sp.wait_ge(w_lo_ok[s], n)
            sp.sem_inc(flush, 1)
            for h, view in enumerate((lwa_v, lwx_v)):
                for r in range(2):
                    sp.dma_start(w_raw[s][:, 4 * h + 2 * r:4 * h + 2 * r + 2, :],
                                 view[:, r, bass.ds(b, 2), :]).then_inc(w_in_ok[s], 16)
            load_unit("mix", 5, it, cols(w_in_v, c + COL_Y))
            load_unit("mix", 6, it, cols(w_in_v, c + (COL_Y + P)))
        with sp.Fori(0, 8) as m:
            c = sp.snap(m * 128)
            load_unit("branch", 0, m, cols(w_in_v, c + COL_GA))
            load_unit("branch", 1, m, cols(w_in_v, c + COL_GR))
            load_unit("branch", 2, m, cols(wa_v, c))
            load_unit("branch", 3, m, cols(wr_v, c))
        def load_expert_unit(s, e):
            which, h = divmod(s % UNITS, 2)
            view = (moe_w_gate, moe_w_up, moe_w_down)[which][0, bass.ds(e, 1)].rearrange(
                "a (k p) f -> p (a k) f", p=P)
            n = (4, 4, 2)[which]
            sp.dma_start(e_raw[s][:, :].rearrange("p (k f) -> p k f", k=n), view[:, n * h:n * (h + 1), :]
                         ).then_inc(ew_in[s], 16)

        for it in range(4):
            load_unit("out", 0, it, cols(wo_v, it * 256))
            load_unit("out", 1, it, cols(wo_v, it * 256 + P))
            if it == 0:
                made(sp, "branch", 3, KT - 1)
                sp.wait_ge(ml_ok, KT)
                sp.dma_start(g2row[:, :], norm_ffn_g[0].partition_broadcast(P)).then_inc(g2_in, 16)
            for s in range(3 * it, min(3 * it + 3, RAW - 2)):
                load_expert_unit(s, s // UNITS)
        for i in range(TT):
            sp.wait_ge(xn2_ok, i + 1)
            sp.dma_start(n2_dram[i * P:(i + 1) * P, :], xn2[:, i, :]).then_inc(n2_out, 16)
        sp.wait_ge(lg_mm, KT)
        load_expert_unit(RAW - 2, 1)
        load_expert_unit(RAW - 1, 1)
        for s in range(CONV - 1):
            sp.wait_ge(e_lo_ok, s + 1)
            load_expert_unit(s, 2)
        sp.wait_ge(table_ok, 1)
        more = sp.value_load(table[0:1, MAXC + 2:MAXC + 3], min_val=N_E // 2 - 1, max_val=MAXC // 2 - 1)
        with sp.Fori(0, more) as q:
            for n, c in ((CONV - 1, 2), (UNITS, 3), (RAW, 4)):
                e = sp.value_load(table[0:1, bass.ds(q * 2 + c, 1)], min_val=0, max_val=N_E - 1)
                for j in range(n, {CONV - 1: UNITS, UNITS: RAW, RAW: RAW + CONV - 1}[n]):
                    sp.wait_ge(e_lo_ok, q * RAW + (j + 1))
                    sp.sem_inc(flush, 1)
                    load_expert_unit(j % RAW, e)
        sp.wait_ge(e_lo_ok, more * RAW + (RAW + CONV - 1))
        sp.sem_inc(flush, 1)
        sp.dma_start(gfin[:, :], final_norm_g.partition_broadcast(P)).then_inc(gfin_in, 16)
        for i in range(TT):
            sp.wait_ge(fo_ok, i + 1)
            sp.dma_start(out[0, i * P:(i + 1) * P, :], fo[:, i % 2, :]).then_inc(out_done[i % 2], 16)
        sp.wait_ge(out_done[0], 16 * TT // 2)
        sp.wait_ge(out_done[1], 16 * TT // 2)

    @block.gpsimd
    def _(pool):
        ch = Chain(pool, pool_chain)
        nc.gpsimd.memset(rec[0:CHUNK, 0:2, :], 0.0).then_inc(zero_ok, 1)
        nc.gpsimd.memset(ones[:, :], 1.0)
        nc.gpsimd.memset(stat[:, :, :], 1.0)
        for h in range(HEADS):
            nc.gpsimd.memset(PV[:, 13, h:h + 1], 2.0 ** (-8.0 * (h + 1) / HEADS))
        for k in range(MAXR - 1):
            nc.gpsimd.memset(thr[:, k:k + 1], float(CHUNK * (k + 1)))
        nc.gpsimd.iota(even[:, :], pattern=[[2, MAXO // 2]], base=0, channel_multiplier=0,
                       allow_small_or_imprecise_dtypes=True)
        for i in range(2):
            nc.gpsimd.iota(iota_e[:, i, :], pattern=[[1, E_G]], base=-8 * i, channel_multiplier=0,
                           allow_small_or_imprecise_dtypes=True)
        nc.gpsimd.iota(tok[:, :], pattern=[[P, TT]], base=0, channel_multiplier=1,
                       allow_small_or_imprecise_dtypes=True)
        nc.gpsimd.memset(nd[:, 0:16], 0.0)
        nc.gpsimd.memset(nd[:, 272:288], 0.0)
        nc.gpsimd.memset(nd[:, 672:688], 0.0)
        ch.link(nc.gpsimd.iota(nd[:, 288:672], pattern=[[1, 384]], base=-P, channel_multiplier=-1,
                               allow_small_or_imprecise_dtypes=True))
        ch.link(nc.gpsimd.affine_select(out=ident[:, :], in_=ones[:, :], compare_op=ALU.is_equal, fill=0.0, base=0,
                                        pattern=[[-1, P]], channel_multiplier=1))
        nc.gpsimd.affine_select(out=tri[:, :], in_=ones[:, :], compare_op=ALU.is_gt, fill=0.0, base=0,
                                pattern=[[1, P]], channel_multiplier=-1).then_inc(const_ok, 1)
        ch.link(nc.gpsimd.tensor_scalar(ndh[:, 0:384], nd[:, 288:672], -1.0, None, ALU.mult))
        ch.link(nc.gpsimd.affine_select(out=nd[:, 288:672], in_=nd[:, 288:672], compare_op=ALU.is_gt, fill=0.0,
                                        base=P, pattern=[[-1, 384]], channel_multiplier=1))
        ch.link(nc.gpsimd.affine_select(out=ndh[:, 0:384], in_=ndh[:, 0:384], compare_op=ALU.is_ge, fill=0.0,
                                        base=-P, pattern=[[1, 384]], channel_multiplier=-1))
        ch.link(nc.gpsimd.tensor_tensor(nd[:, 288:672], nd[:, 288:672], ndh[:, 0:384], ALU.add))
        ch.link(nc.gpsimd.affine_select(out=nd[:, 288:672], in_=nd[:, 288:672], compare_op=ALU.is_ge, fill=-1e32,
                                        base=0, pattern=[[1, 384]], channel_multiplier=-1))
        ch.link(nc.gpsimd.affine_select(out=nd[:, 288:672], in_=nd[:, 288:672], compare_op=ALU.is_ge, fill=-1e32,
                                        base=256, pattern=[[-1, 384]], channel_multiplier=1))
        nc.gpsimd.tensor_copy(nd[:, 16:272], nd[:, 288 + 128:672])
        ch.link(nc.gpsimd.tensor_copy(nd[:, 688:944], nd[:, 288:288 + 256]))
        ch.close()
        pool.wait_ge(nt_lo_ok, KT)
        pool.wait_ge(par_ok, 1)
        nc.gpsimd.memset(xr[:, :, 0:2], 0.0)
        nc.gpsimd.memset(xr[:, :, T + 2:T + 4], 0.0).then_inc(pad_ok, 1)

        with pool.Fori(0, 4) as it:
            ch.body(it, 2)

            def head_bias(hh):
                pool.wait_ge(cur_ok, it + 1)
                pool.wait_ge(tt_ok, it * 8 + 4 * hh)
                pool.sem_inc(flush, 1)
                nc.gpsimd.tensor_scalar(ndh[:, :], nd[:, :], cur[:, 13, hh:hh + 1], None, ALU.mult
                                        ).then_inc(ndh_ok, 1)

            def square_a(i, bd):
                o = 0 if bd < 2 else META
                pool.wait_ge(a_ok, it * 4 + (i + 1))
                if i >= 2:
                    pool.wait_ge(w_ok, it * 4 + (i - 1))
                nc.gpsimd.tensor_tensor(a2[i % 2][:, o:T], ab[:, bd, o:T], ab[:, bd, o:T], ALU.mult
                                        ).then_inc(a2_ok, 1)

            head_bias(0)
            square_a(0, 0)
            square_a(1, 2)
            head_bias(1)
            square_a(2, 1)
            square_a(3, 3)
            pool.wait_ge(v_ok, it * 4 + 4)
            for d in range(2):
                o = META * d
                pool.wait_ge(sq_ok, it * 2 + (d + 1))
                for bb in range(2):
                    bd = 2 * d + bb
                    nc.gpsimd.tensor_tensor(vb[:, bd, o:T], vb[:, bd, o:T], wb[:, bd, o:T], ALU.mult
                                            ).then_inc(u_ok, 1)
            r = pool.snap(it * 2)
            marks = []
            for bb in range(2):
                pool.wait_ge(scan_ok, it * 4 + (3 + bb))
                marks.append(ch.mark(nc.gpsimd.tensor_tensor(a2[bb][:, 0:SEQ], wb[:, bb, META:T],
                                                             wb[:, 2 + bb, META:T], ALU.add)))
            pool.wait_ge(gelu_ok, it + 1)
            for bb in range(2):
                ch.need(marks[bb])
                nc.gpsimd.sem_inc(flush, 1)
                dst = rec[:, bass.ds(r + bb, 1), :].rearrange("p a t -> p (a t)")
                nc.gpsimd.tensor_tensor(dst, dst, a2[bb][:, 0:SEQ], ALU.mult).then_inc(rec_ok, 1)
        ch.close(4)

        with pool.Fori(0, KT) as m:
            pool.wait_ge(ml_ok, m)
            pool.wait_ge(m2_ok, m + 1)
            nc.gpsimd.tensor_tensor(ms[:, :], m2[:, 0, :], m2[:, 1, :], ALU.add).then_inc(ms_ok, 1)

        made(pool, "branch", 3, KT - 1)
        nc.gpsimd.memset(wrt_hi[:, :, :].bitcast(F32), 0.0)
        nc.gpsimd.memset(wrt_lo[:, :, :].bitcast(F32), 0.0).then_inc(wrt0_ok, 1)
        made(pool, "out", 1, 3)
        nc.gpsimd.memset(past[:, 0, :], 0.0)
        nc.gpsimd.memset(both[:, TT, :], 0.0)
        nc.gpsimd.memset(one16[:, :], 1.0)
        nc.gpsimd.iota(io_r[:, :], pattern=[[1, CHUNK]], base=0, channel_multiplier=0,
                       allow_small_or_imprecise_dtypes=True).then_inc(iota_ok, 1)
        for j in range(CONV - 1):
            pool.wait_ge(e_hi_ok, j + 1)
            nc.gpsimd.tensor_tensor(e_lo[j][:, :], e_raw[j][:, :], e_hi[j][:, :].bitcast(F32), ALU.subtract
                                    ).then_inc(e_lo_ok, 1)
        pool.wait_ge(n2_out, 16 * TT)
        pool.wait_ge(route_ok, 1)

        def gather(p, h):
            pool.wait_ge(g_in[h], p * 16)
            pool.sem_inc(flush, 1)
            nc.gpsimd.tensor_copy(idx_now[h][:, :], idx[:, bass.ds(p * 2 + h, 1)]).then_inc(idx_ok, 1)
            pool.wait_ge(idx_ok, p * 2 + (h + 1))
            pool.wait_ge(xt_full[h], p * 2)
            pool.sem_inc(flush, 1)
            pool.indirect_dma_start(G[h][:, :], None, n2_dram[:, :],
                                    bass.IndirectOffsetOnAxis(ap=idx_now[h][:, :], axis=0)).then_inc(g_in[h], 16)

        pairs = pool.value_load(table[0:1, MAXC + 1:MAXC + 2], min_val=N_E // 2, max_val=MAXC // 2)
        with pool.Fori(0, pairs) as p:
            for h in range(2):
                gather(p, h)
        gather(pairs, 0)
        pool.wait_ge(e_lo_ok, pairs * RAW + (CONV - 1))
        pool.wait_ge(y_out, pairs * 32)
        pool.sem_inc(flush, 1)
        for i in range(TT):
            for j in range(2):
                pool.indirect_dma_start(F[j][:, i, :], None, y_dram[:, :],
                                        bass.IndirectOffsetOnAxis(ap=slot_i[:, TT * j + i:TT * j + i + 1], axis=0)
                                        ).then_inc(f_in[i], 16)

    @block.scalar
    def _(act):
        ch = Chain(act, act_chain)
        act.wait_ge(const_ok, 1)
        for i in range(TT):
            act.wait_ge(x_in[i], 16)
            ch.link(nc.scalar.activation(junk[:, :], X[:, i, :], ACT.Square, accum_out=stat[:, 0, i:i + 1]))
        act.wait_ge(meta_in, 16)
        nc.scalar.activation(junk[0:META, :], msb[:, :], ACT.Square,
                             accum_out=stat[0:META, 0, TT:TT + 1]).then_inc(ssq_ok, 1)
        act.wait_ge(var_ok, 1)
        nc.scalar.activation(stat[:, 2, :], stat[:, 1, :], ACT.Sqrt).then_inc(std_ok, 1)
        act.wait_ge(rstd_ok, 1)
        nc.scalar.activation(mn[:, :], msb[:, :], ACT.Copy, scale=stat[0:META, 0, TT:TT + 1]).then_inc(mn_ok, 1)

        def split_hi(phase, u, it=0):
            s, n = unit(phase, u, it)
            act.wait_ge(w_in_ok[s], w_in_target(phase, u, it))
            if not (is_const(n) and n == 0):
                act.wait_ge(w_used[s], n)
            nc.scalar.activation(w_hi[s][:, :, :], w_raw[s][:, :, :], ACT.Copy).then_inc(w_hi_ok[s], 1)

        split_hi("kv", 0)
        split_hi("kv", 1)
        for k in range(KT):
            act.wait_ge(nt_full, k + 1)
            if k == 0:
                act.wait_ge(gain_ok, 1)
            nc.scalar.activation(nT_hi[:, k, 0:400], nt_ps(k, 0)[:, 0:400], ACT.Copy, scale=g12[:, 0, k:k + 1])
            nc.scalar.activation(nT_hi[:, k, 400:T], nt_ps(k, 1)[:, 0:P], ACT.Copy, scale=g12[:, 0, k:k + 1]
                                 ).then_inc(nT_hi_ok, 1)
        act.wait_ge(lam_abs_ok, 1)
        nc.scalar.activation(spt[:, 1, :], spt[:, 0, :], ACT.Exp, scale=-1.0).then_inc(lam_exp_ok, 1)

        for kv in range(KV):
            split_hi("kv", kv + 2) if kv == 0 else None
            p = kv
            made(act, "kv", kv)
            nc.scalar.activation(kT_hi[:, kv, :].rearrange("p (h c) -> p h c", h=2), pj[:, 2 * p:2 * p + 2, 0:HALF],
                                 ACT.Copy).then_inc(k_hi_ok, 1)
        split_hi("kv", 3)
        split_hi("kv", 4)
        for c in range(2):
            made(act, "kv", 2 + c)
            nc.scalar.activation(a2[c][:, :].rearrange("p (h c) -> p h c", h=2), pj[:, 2 * c:2 * c + 2, 0:HALF],
                                 ACT.Copy).then_inc(vT_ok, 1)
        split_hi("kv", 5)
        for c in range(2):
            act.wait_ge(v_full, c + 1)
            nc.scalar.activation(V[:, 1:TT + 1, c * P:(c + 1) * P],
                                 v_ps[c][:, :].rearrange("p (t c) -> p t c", c=P), ACT.Copy)
            nc.scalar.activation(V[0:META, 0, c * P:(c + 1) * P], s_ps[0:META, c, 0:P], ACT.Copy
                                 ).then_inc(v_rows_ok, 1)
        ch.close()

        act.wait_ge(y_zeroed, 16 * (MAXC - N_E))
        with act.Fori(0, 4) as it:
            ch.body(it, 6)
            r = act.snap(it * 2)
            act.wait_ge(par_ok, 1)
            act.wait_ge(tt_ok, it * 8)
            act.sem_inc(flush, 1)
            nc.scalar.activation(cur[:, :, :], PV[:, :, bass.ds(r, 2)], ACT.Copy).then_inc(cur_ok, 1)
            act.wait_ge(cur_ok, it + 1)
            split_hi("mix", 2, it)
            for bb in range(2):
                p = bb
                act.wait_ge(xc_ok, it * 2)
                made(act, "mix", bb, it)
                nc.scalar.activation(xr[:, bb, 2:T + 2].rearrange("p (h c) -> p h c", h=2),
                                     pj[:, 2 * p:2 * p + 2, 0:HALF], ACT.Copy).then_inc(xr_ok, 1)
                split_hi("mix", 3 + bb, it)
            s4, n4 = unit("mix", 4, it)
            for bb in range(2):
                act.wait_ge(xc_ok, it * 2 + (bb + 1))
                act.wait_ge(w_used[s4], n4)
                nc.scalar.activation(xc_hi[:, bb, :], xc[:, bb, :], ACT.Copy).then_inc(xch_ok, 1)
            split_hi("mix", 5, it)
            for hh in range(2):
                made(act, "mix", 2 + hh, it)
                if hh == 0:
                    act.wait_ge(s_full, it * 8)
                nc.scalar.activation(qT_hi[:, hh, :], pj[:, hh, :], ACT.Copy, scale=HD ** -0.5).then_inc(qh_ok, 1)

            def lru_a(j, bd):
                d, bb = divmod(bd, 2)
                o = META * d
                act.wait_ge(scan_ok, it * 4)
                act.wait_ge(rec_ok, it * 2)
                p = j % 2
                if j == 8:
                    made(act, "mix", 4, it)
                else:
                    act.wait_ge(lru_full, it * 5 + (j - 2))
                if d == 0:
                    two = lambda t: t.rearrange("p (h c) -> p h c", h=2)
                    nc.scalar.activation(two(ab[:, bd, :]), pj[:, 2 * p:2 * p + 2, 0:HALF], ACT.Tanh,
                                         bias=cur[:, 5, bb:bb + 1], scale=0.5).then_inc(tha_ok, 1)
                    return None
                q = ch.mark(nc.scalar.activation(ab[:, bd, o:T], pj[:, 2 * p, :], ACT.Tanh,
                                                 bias=cur[:, 6, bb:bb + 1], scale=0.5))
                nc.scalar.activation(vb[:, bd, o:T], pj[:, 2 * p + 1, :], ACT.Tanh, bias=cur[:, 8, bb:bb + 1],
                                     scale=0.5).then_inc(thi_ok, 1)
                return q

            def lru_x(j, bb):
                p = j % 2
                act.wait_ge(lru_full, it * 5 + (j - 2))
                nc.scalar.activation(vb[:, bb, :].rearrange("p (h c) -> p h c", h=2), pj[:, 2 * p:2 * p + 2, 0:HALF],
                                     ACT.Tanh, bias=cur[:, 7, bb:bb + 1], scale=0.5).then_inc(thi_ok, 1)

            def lru_decay(q, bd):
                d, bb = divmod(bd, 2)
                o = META * d
                if q is None:
                    act.wait_ge(tha_ok, it * 2 + (bb + 1))
                else:
                    ch.need(q)
                q2 = ch.mark(nc.scalar.activation(wb[:, bd, o:T], ab[:, bd, o:T], ACT.Tanh,
                                                  bias=cur[:, 11 + d, bb:bb + 1], scale=cur[:, 11 + d, bb:bb + 1]))
                ch.need(q2)
                nc.scalar.activation(ab[:, bd, o:T], ab[:, bd, o:T], ACT.Exp,
                                     bias=cur[:, 9 + d, bb:bb + 1], scale=cur[:, 9 + d, bb:bb + 1]).then_inc(a_ok, 1)

            def exps(a):
                hh, j = divmod(a, 4)
                act.wait_ge(neg_ok, it * 8 + (a + 1))
                if a < 4:
                    act.wait_ge(onorm_ok, it * 2)
                w = S_W[j + 1]
                nc.scalar.activation(s_sb[a % 2][:, 0:w], s_sb[a % 2][:, 0:w], ACT.Exp, bias=nmax[:, hh, j:j + 1],
                                     accum_out=rsum[:, hh, j:j + 1]).then_inc(p_ok, 1)

            def exp_sink(hh):
                act.wait_ge(onorm_ok, it * 2 + hh)
                nc.scalar.activation(esink[:, :], nmax[:, hh, :], ACT.Exp, bias=cur[:, 14, hh:hh + 1]
                                     ).then_inc(es_ok, 1)

            def evac_o(hh):
                act.wait_ge(pt_full, it * 10 + OT_N[hh])
                act.sem_inc(flush, 1)
                nc.scalar.activation(attn[:, bass.ds(r + hh, 1), :].rearrange("p a t -> p (a t)"), pt_ps[:, :],
                                     ACT.Copy).then_inc(pt_free, 1)

            q0 = lru_a(3, 0)
            lru_x(4, 0)
            exps(0)
            q1 = lru_a(5, 2)
            lru_decay(q0, 0)
            exps(1)
            lru_decay(q1, 2)
            q2 = lru_a(6, 1)
            exps(2)
            lru_x(7, 1)
            exps(3)
            exp_sink(0)
            q3 = lru_a(8, 3)
            split_hi("mix", 6, it)
            exps(4)
            lru_decay(q2, 1)
            lru_decay(q3, 3)
            exps(5)
            split_hi("mix", 7, it)
            exps(6)
            evac_o(0)
            exps(7)
            exp_sink(1)
            act.wait_ge(w_ok, it * 4 + 4)
            for d in range(2):
                o = META * d
                nc.scalar.activation(wb[:, 2 * d:2 * d + 2, o:T], wb[:, 2 * d:2 * d + 2, o:T], ACT.Sqrt, scale=0.25
                                     ).then_inc(sq_ok, 1)
            p = 1
            made(act, "mix", 6, it)
            act.sem_inc(flush, 1)
            nc.scalar.activation(rec[:, bass.ds(r, 2), :], pj[:, 2 * p:2 * p + 2, :], ACT.Gelu_apprx_tanh
                                 ).then_inc(gelu_ok, 1)
            act.wait_ge(gelu_ok, it + 1)
            evac_o(1)
            split_hi("mix", 8, it)
        ch.close(4)

        act.wait_ge(o_done, 32)
        act.wait_ge(onorm_ok, 8)
        act.wait_ge(pt_free, 40)
        act.wait_ge(rec_ok, KT)
        nc.scalar.activation(attn_hi[:, :, :], attn[:, :, :], ACT.Copy).then_inc(br_hi_ok, 1)
        nc.scalar.activation(rec_hi[:, :, :], rec[:, :, :], ACT.Copy).then_inc(br_hi_ok, 1)
        with act.Fori(0, KT) as m:
            split_hi("branch", 2, m)
            p = 0
            act.wait_ge(m2_ok, m)
            made(act, "branch", 1, m)
            nc.scalar.activation(g_sb[:, :, :], pj[:, 2 * p:2 * p + 2, :], ACT.Tanh, scale=0.5
                                 ).then_inc(gate_ok, 1)
            split_hi("branch", 3, m)
            split_hi("branch", 4, m)
            act.wait_ge(ms_ok, m + 1)
            act.sem_inc(flush, 1)
            nc.scalar.activation(mg_hi[:, bass.ds(m, 1), :].rearrange("p a t -> p (a t)"), ms[:, :], ACT.Copy,
                                 scale=0.5).then_inc(mh_ok, 1)
            split_hi("branch", 5, m)

        def split_unit_hi(j, p):
            n = j if p is None else p * RAW + j
            at = (1 if p is None else p + 1) if j < RAW else p + 2
            act.wait_ge(ew_in[j % RAW], at * 16)
            if p is not None:
                act.wait_ge(e_used, n - (CONV - 1))
            nc.scalar.activation(e_hi[j % CONV][:, :], e_raw[j % RAW][:, :], ACT.Copy).then_inc(e_hi_ok, 1)

        def n2_hi(k):
            act.wait_ge(rt_full, k + 1)
            if k >= 2:
                act.wait_ge(lg_mm, k - 1)
            nc.scalar.activation(n2t_hi[:, k % 2, :], pj[:, 2 * (k % 2) + 1, :], ACT.Copy, scale=g12[:, 1, k:k + 1]
                                 ).then_inc(n2h_ok, 1)

        def sum_squares(i, c0, c1, col):
            nc.scalar.activation(xn2[:, i, c0:c1], X[:, i, c0:c1], ACT.Square, accum_out=stat2[:, col, i:i + 1]
                                 ).then_inc(ssq2_ok, 1)

        for it in range(4):
            if it == 3:
                act.wait_ge(h_ok, 6)
                for i in range(TT):
                    sum_squares(i, 0, 6 * P, 0)
            for j in range(2):
                if it:
                    act.wait_ge(oT_full, it * 2 + j - 1)
                made(act, "out", j, it)
                nc.scalar.activation(oT_sb[j][:, :], pj[:, 2 * j, :], ACT.Copy).then_inc(oT_ok, 1)
                if it < 3:
                    split_hi("out", 2 + j, it)
                if it == 0 and j == 0:
                    act.wait_ge(wrt0_ok, 1)
                    act.wait_ge(wrt_in, 64)
                    nc.scalar.activation(wrt_hi[:, :, 0:N_G + N_E], wrt[:, :, :], ACT.Copy).then_inc(wrt_hi_ok, 1)
                if it and j == 0:
                    n2_hi(2 * it - 2)
                    n2_hi(2 * it - 1)
        n2_hi(KT - 2)
        act.wait_ge(h_ok, KT)
        n2_hi(KT - 1)
        for i in range(TT):
            sum_squares(i, 6 * P, KT * P, 3)
        act.wait_ge(var2_ok, 1)
        nc.scalar.activation(stat2[:, 2, :], stat2[:, 1, :], ACT.Sqrt).then_inc(std2_ok, 1)
        act.wait_ge(lg_mm, KT)
        nc.scalar.activation(lgT[:, :], o_ps[0:N_G + N_E, :], ACT.Copy).then_inc(lgT_ok, 1)
        act.wait_ge(lg_ok, 1)
        for j in range(CONV - 1):
            split_unit_hi(j, None)
        act.wait_ge(gd_ok, 1)
        nc.scalar.activation(gex[:, :, :], gex[:, :, :], ACT.Exp).then_inc(gexp_ok, 1)
        act.wait_ge(ed_ok, 1)
        nc.scalar.activation(ediff[:, :], ediff[:, :], ACT.Exp).then_inc(eexp_ok, 1)

        def x_hi_half(p, odd, h):
            act.wait_ge(xt_full[odd], p * 2 + (h + 1))
            nc.scalar.activation(xT_hi[:, 4 * h:4 * h + 4, :],
                                 pj[:, 2 + h, :].rearrange("p (k c) -> p k c", c=P), ACT.Copy).then_inc(x_hi_ok, 1)

        def chunk(p, h):
            c, u, m = p * 2 + h, h * UNITS, p * 4 + 2 * h
            split_unit_hi(u + 3, p)
            split_unit_hi(u + 4, p)
            act.wait_ge(e_used, p * RAW + (u + 2))
            act.wait_ge(ht_full, m)
            nc.scalar.activation(hid[:, :], pj[:, 0, :], ACT.Silu).then_inc(silu_ok, 1)
            split_unit_hi(u + 5, p)

            def h_hi(half):
                act.wait_ge(ht_full, m + (half + 1))
                nc.scalar.activation(hT_hi[:, 2 * half:2 * half + 2, :],
                                     ht_ps[half][:, 0:2 * P].rearrange("p (k c) -> p k c", c=P),
                                     ACT.Copy).then_inc(h_hi_ok, 1)

            split_unit_hi(u + 6, p)
            h_hi(0)
            x_hi_half(p + h, 1 - h, 0)
            h_hi(1)
            x_hi_half(p + h, 1 - h, 1)
            split_unit_hi(u + 7, p)
            split_unit_hi(u + 8, p)
            row = act.snap(c * CHUNK)
            act.wait_ge(y_out, c * 16)
            act.wait_ge(e_used, p * RAW + (u + 6))
            nc.scalar.activation(y_sb[:, :].rearrange("p (h d) -> p h d", h=2), s_ps[:, :, :], ACT.Copy
                                 ).then_inc(y_ok, 1)
            act.wait_ge(y_ok, c + 1)
            act.dma_start(y_dram[bass.ds(row, CHUNK), :], y_sb[:, :]).then_inc(y_out, 16)

        x_hi_half(0, 0, 0)
        x_hi_half(0, 0, 1)
        pairs = act.value_load(table[0:1, MAXC + 1:MAXC + 2], min_val=N_E // 2, max_val=MAXC // 2)
        with act.Fori(0, pairs) as p:
            nc.scalar.activation(silu_warm[:, :], ident[:, 0:1], ACT.Silu)
            for h in range(2):
                chunk(p, h)

        for i in range(TT):
            act.wait_ge(hf_ok, i + 1)
            act.wait_ge(fo_ok, i)
            if i >= 2:
                act.wait_ge(out_done[i % 2], 16 * (i // 2))
            nc.scalar.activation(fo[:, i % 2, :], X[:, i, :], ACT.Square, accum_out=stat3[:, 0, i:i + 1]
                                 ).then_inc(ssq3_ok, 1)
            act.wait_ge(var3_ok, i + 1)
            nc.scalar.activation(stat3[:, 2, i:i + 1], stat3[:, 1, i:i + 1], ACT.Sqrt).then_inc(std3_ok, 1)

    @block.vector
    def _(dve):
        ch = Chain(dve, dve_chain)
        V_ = nc.vector
        ch.link(V_.memset(pt_ps[:, :], 0.0))
        dve.wait_ge(ssq_ok, 1)
        V_.tensor_scalar(stat[:, 1, :], stat[:, 0, :], 1.0 / D, EPS, ALU.mult, ALU.add).then_inc(var_ok, 1)
        dve.wait_ge(std_ok, 1)
        V_.reciprocal(stat[:, 0, :], stat[:, 2, :]).then_inc(rstd_ok, 1)
        dve.wait_ge(rstd_ok, 1)
        for i in range(TT):
            V_.tensor_scalar(xn[:, i, :], X[:, i, :], stat[:, 0, i:i + 1], None, ALU.mult).then_inc(xn_ok, 1)
        dve.wait_ge(prmT_ok, 1)
        tp = s_ps[:, 0, 0:104]
        V_.tensor_copy(g12[:, :, :], tp[:, 88:104].rearrange("p (g b) -> p g b", b=8)).then_inc(gain_ok, 1)
        V_.tensor_copy(PV[:, 0:5, :], tp[:, 0:40].rearrange("p (g b) -> p g b", b=8))
        V_.tensor_scalar(PV[:, 5:9, :], tp[:, 40:72].rearrange("p (g b) -> p g b", b=8), 0.5, None, ALU.mult)
        V_.tensor_copy(spt[:, 2, :], tp[:, 72:88]).then_inc(prm_ok, 1)
        dve.wait_ge(prm_ok, 1)

        def split_lo(phase, u, it=0):
            s, n = unit(phase, u, it)
            dve.wait_ge(w_hi_ok[s], n + 1)
            V_.tensor_tensor(w_lo[s][:, :, :], w_raw[s][:, :, :], w_hi[s][:, :, :].bitcast(F32), ALU.subtract
                             ).then_inc(w_lo_ok[s], 1)

        split_lo("kv", 0)
        for k in range(KT):
            if k == 4:
                split_lo("kv", 1)
            dve.wait_ge(nT_hi_ok, k + 1)
            V_.scalar_tensor_tensor(nT_lo[:, k, 0:400], nt_ps(k, 0)[:, 0:400], g12[:, 0, k:k + 1],
                                    nT_hi[:, k, 0:400].bitcast(F32), ALU.mult, ALU.subtract)
            V_.scalar_tensor_tensor(nT_lo[:, k, 400:T], nt_ps(k, 1)[:, 0:P], g12[:, 0, k:k + 1],
                                    nT_hi[:, k, 400:T].bitcast(F32), ALU.mult, ALU.subtract).then_inc(nt_lo_ok, 1)

        lam = spt[:, 2, :]
        ch.link(V_.tensor_scalar(spt[:, 3, :], lam, -1.0, None, ALU.mult))
        V_.tensor_tensor(spt[:, 0, :], lam, spt[:, 3, :], ALU.max).then_inc(lam_abs_ok, 1)
        ch.link(V_.tensor_scalar(spt[:, 3, :], spt[:, 3, :], 0.0, None, ALU.max))

        def softplus():
            dve.wait_ge(lam_exp_ok, 1)
            e_, s_, z_, p_ = spt[:, 1, :], spt[:, 4, :], spt[:, 5, :], spt[:, 6, :]
            ch.link(V_.tensor_scalar(s_, e_, 2.0, None, ALU.add))
            ch.link(V_.reciprocal(z_, s_))
            ch.link(V_.tensor_tensor(s_, e_, z_, ALU.mult))
            ch.link(V_.tensor_tensor(z_, s_, s_, ALU.mult))
            ch.link(V_.tensor_scalar(p_, z_, 2.0 / 19, None, ALU.mult))
            for k in range(8, 0, -1):
                ch.link(V_.scalar_tensor_tensor(p_, p_, 2.0 / (2 * k + 1), z_, ALU.add, ALU.mult))
            ch.link(V_.scalar_tensor_tensor(p_, p_, 2.0, s_, ALU.add, ALU.mult))
            ch.link(V_.tensor_tensor(p_, p_, spt[:, 3, :], ALU.add))
            p2 = p_.rearrange("p (g b) -> p g b", b=8)
            V_.tensor_scalar(PV[:, 9:11, :], p2, -4.0, None, ALU.mult)
            V_.tensor_scalar(PV[:, 11:13, :], p2, 4.0, None, ALU.mult).then_inc(par_ok, 1)

        for kv in range(KV):
            if kv == 0:
                split_lo("kv", 2)
            p = kv
            dve.wait_ge(k_hi_ok, kv + 1)
            two = lambda t: t.rearrange("p (h c) -> p h c", h=2)
            V_.tensor_tensor(two(kT_lo[:, kv, :]), pj[:, 2 * p:2 * p + 2, 0:HALF], two(kT_hi[:, kv, :]).bitcast(F32),
                             ALU.subtract).then_inc(k_lo_ok, 1)
        split_lo("kv", 3)
        split_lo("kv", 4)
        softplus()
        split_lo("kv", 5)
        ch.close()

        with dve.Fori(0, 4) as it:
            ch.body(it, 10)
            dve.wait_ge(cur_ok, it + 1)
            dve.wait_ge(pad_ok, 1)
            split_lo("mix", 2, it)
            for bb in range(2):
                dve.wait_ge(xr_ok, it * 2 + (bb + 1))
                ch.link(V_.tensor_scalar(xc[:, bb, :], xr[:, bb, 0:T], cur[:, 0, bb:bb + 1], cur[:, 4, bb:bb + 1],
                                         ALU.mult, ALU.add))
                for i in range(1, 4):
                    ins = V_.scalar_tensor_tensor(xc[:, bb, :], xr[:, bb, i:i + T], cur[:, i, bb:bb + 1],
                                                  xc[:, bb, :], ALU.mult, ALU.add)
                    ch.link(ins) if i < 3 else ins.then_inc(xc_ok, 1)
                split_lo("mix", 3 + bb, it)
            for bb in range(2):
                dve.wait_ge(xch_ok, it * 2 + (bb + 1))
                V_.tensor_tensor(xc_lo[:, bb, :], xc[:, bb, :], xc_hi[:, bb, :].bitcast(F32), ALU.subtract
                                 ).then_inc(xcl_ok, 1)
            split_lo("mix", 5, it)
            for hh in range(2):
                dve.wait_ge(qh_ok, it * 2 + (hh + 1))
                V_.scalar_tensor_tensor(qT_lo[:, hh, :], pj[:, hh, :], HD ** -0.5, qT_hi[:, hh, :].bitcast(F32),
                                        ALU.mult, ALU.subtract).then_inc(q_ok, 1)

            def scores(a):
                hh, j = divmod(a, 4)
                w, o = S_W[j + 1], S_ND[j + 1]
                dve.wait_ge(s_full, it * 8 + (a + 1))
                dve.wait_ge(ndh_ok, it * 2 + (hh + 1))
                dve.wait_ge(pt_full, it * 10 + (PT_N[a - 2] if a >= 2 else 0))
                dve.sem_inc(flush, 1)
                V_.tensor_tensor_reduce(s_sb[a % 2][:, 0:w], ndh[:, o:o + w], s_ps[:, a % 2, 0:w], 1.0,
                                        cur[:, 14, hh:hh + 1], ALU.add, ALU.max, mx[:, hh, j:j + 1]
                                        ).then_inc(tt_ok, 1)
                dve.wait_ge(tt_ok, it * 8 + (a + 1))
                V_.tensor_scalar(nmax[:, hh, j:j + 1], mx[:, hh, j:j + 1], -1.0, None, ALU.mult).then_inc(neg_ok, 1)

            def evac_pt(a):
                nb = len(S_V[a % 4 + 1]) + 1
                dve.wait_ge(o_done, it * 8 + (a - 1 if a >= 2 else 0))
                dve.wait_ge(pt_full, it * 10 + PT_N[a])
                V_.tensor_copy(pt_sb[a % 2][:, 0:nb * P], pt_ps[:, 0:nb * P]).then_inc(pt_free, 1)

            def gate_in(i, bd):
                d, bb = divmod(bd, 2)
                o = META * d
                dve.wait_ge(thi_ok, it * 4 + (i + 1))
                V_.scalar_tensor_tensor(vb[:, bd, o:T], vb[:, bd, o:T], 1.0, xc[:, bb, o:T], ALU.add, ALU.mult
                                        ).then_inc(v_ok, 1)

            def one_minus(i, bd):
                o = META * (bd // 2)
                dve.wait_ge(a2_ok, it * 4 + (i + 1))
                V_.scalar_tensor_tensor(wb[:, bd, o:T], a2[i % 2][:, o:T], 1.0, wb[:, bd, o:T], ALU.add, ALU.mult
                                        ).then_inc(w_ok, 1)

            def normalise(hh):
                dve.wait_ge(es_ok, it * 2 + (hh + 1))
                dve.wait_ge(p_ok, it * 8 + 4 * (hh + 1))
                ch.link(V_.tensor_tensor(den[:, :], rsum[:, hh, :], esink[:, :], ALU.add))
                ch.link(V_.reciprocal(den[:, :], den[:, :]))
                dve.wait_ge(o_done, it * 8 + 4 * (hh + 1))
                dve.wait_ge(pt_full, it * 10 + (OT_N[0] if hh else 0))
                V_.tensor_tensor(o_sb[:, :, :], o_ps[:, :].rearrange("p (j d) -> p j d", d=P),
                                 den[:, :].unsqueeze(2).broadcast_to([P, TT, P]), ALU.mult).then_inc(onorm_ok, 1)

            scores(0)
            scores(1)
            gate_in(0, 0)
            evac_pt(0)
            scores(2)
            gate_in(1, 2)
            one_minus(0, 0)
            evac_pt(1)
            scores(3)
            one_minus(1, 2)
            evac_pt(2)
            scores(4)
            gate_in(2, 1)
            evac_pt(3)
            scores(5)
            gate_in(3, 3)
            split_lo("mix", 6, it)
            normalise(0)
            evac_pt(4)
            scores(6)
            one_minus(2, 1)
            evac_pt(5)
            one_minus(3, 3)
            scores(7)
            split_lo("mix", 7, it)
            evac_pt(6)
            evac_pt(7)
            normalise(1)
            for bd in range(4):
                d = bd // 2
                dve.wait_ge(u_ok, it * 4 + (bd + 1))
                fw = lambda t: t[:, bd, META:T][:, ::-1] if d else t[:, bd, :]
                V_.tensor_tensor_scan(fw(wb), fw(ab), fw(vb), 0.0, ALU.mult, ALU.add).then_inc(scan_ok, 1)
            split_lo("mix", 8, it)
        ch.close(4)

        dve.wait_ge(br_hi_ok, 1)
        V_.tensor_tensor(attn_lo[:, :, :], attn[:, :, :], attn_hi[:, :, :].bitcast(F32), ALU.subtract
                         ).then_inc(br_lo_ok, 1)
        dve.wait_ge(br_hi_ok, 2)
        V_.tensor_tensor(rec_lo[:, :, :], rec[:, :, :], rec_hi[:, :, :].bitcast(F32), ALU.subtract
                         ).then_inc(br_lo_ok, 1)
        with dve.Fori(0, KT) as m:
            split_lo("branch", 2, m)
            split_lo("branch", 3, m)
            split_lo("branch", 4, m)
            dve.wait_ge(gate_ok, m + 1)
            dve.wait_ge(ms_ok, m)
            p = 1
            made(dve, "branch", 3, m)
            V_.scalar_tensor_tensor(m2[:, :, :], g_sb[:, :, :], 1.0, pj[:, 2 * p:2 * p + 2, :], ALU.add, ALU.mult
                                    ).then_inc(m2_ok, 1)
            dve.wait_ge(mh_ok, m + 1)
            one = lambda t: t[:, bass.ds(m, 1), :].rearrange("p a t -> p (a t)")
            V_.scalar_tensor_tensor(one(mg_lo), ms[:, :], 0.5, one(mg_hi).bitcast(F32), ALU.mult, ALU.subtract
                                    ).then_inc(ml_ok, 1)
            split_lo("branch", 5, m)

        def n2_lo(k):
            dve.wait_ge(n2h_ok, k + 1)
            V_.scalar_tensor_tensor(n2t_lo[:, k % 2, :], pj[:, 2 * (k % 2) + 1, :], g12[:, 1, k:k + 1],
                                    n2t_hi[:, k % 2, :].bitcast(F32), ALU.mult, ALU.subtract).then_inc(n2l_ok, 1)

        for it in range(4):
            if it < 3:
                split_lo("out", 2, it)
            if it == 0:
                dve.wait_ge(wrt_hi_ok, 1)
                V_.tensor_tensor(wrt_lo[:, :, 0:N_G + N_E], wrt[:, :, :], wrt_hi[:, :, 0:N_G + N_E].bitcast(F32),
                                 ALU.subtract).then_inc(wrt_ok, 1)
            else:
                n2_lo(2 * it - 2)
                n2_lo(2 * it - 1)
            if it < 3:
                split_lo("out", 3, it)
            for j in range(2):
                dve.wait_ge(oT_full, it * 2 + (j + 1))
                dst = X[:, :, (2 * it + j) * P:(2 * it + j + 1) * P]
                V_.tensor_tensor(dst, dst, s_ps[:, j, :].rearrange("p (i c) -> p i c", c=P), ALU.add
                                 ).then_inc(h_ok, 1)
        n2_lo(KT - 2)
        n2_lo(KT - 1)

        dve.wait_ge(ssq2_ok, 2 * TT)
        ch.link(V_.tensor_tensor(stat2[:, 0, :], stat2[:, 0, :], stat2[:, 3, :], ALU.add))
        V_.tensor_scalar(stat2[:, 1, :], stat2[:, 0, :], 1.0 / D, EPS, ALU.mult, ALU.add).then_inc(var2_ok, 1)
        dve.wait_ge(std2_ok, 1)
        ch.link(V_.reciprocal(stat2[:, 0, :], stat2[:, 2, :]))

        dve.wait_ge(g2_in, 16)
        for i in range(TT):
            V_.scalar_tensor_tensor(xn2[:, i, :], X[:, i, :], stat2[:, 0, i:i + 1], g2row[:, :], ALU.mult, ALU.mult
                                    ).then_inc(xn2_ok, 1)

        NC = N_G + N_E
        dve.wait_ge(lg_ok, 1)
        lp = pt_ps[:, 0:TT * NC].rearrange("p (i c) -> p i c", c=NC)
        ch.link(V_.tensor_tensor(lg[:, :, :], lp, stat2[:, 0, :].unsqueeze(2).broadcast_to([P, TT, NC]), ALU.mult))
        ch.link(V_.tensor_tensor(lg[:, :, :], lg[:, :, :], bias_r[:, :].unsqueeze(1).broadcast_to([P, TT, NC]),
                                 ALU.add))
        b4 = lambda t: t[:, :].unsqueeze(2).broadcast_to([P, TT, 4])
        ie, ie8 = (iota_e[:, i, :].unsqueeze(1).broadcast_to([P, TT, 4]) for i in range(2))

        def first_max(vals, top, onehot):
            ch.link(V_.tensor_reduce(top[:, :], vals, AX.X, ALU.max))
            ch.link(V_.tensor_tensor(t4[:, :, :], vals, b4(top), ALU.is_equal))
            ch.link(V_.scalar_tensor_tensor(t4[:, :, :], t4[:, :, :], -8.0, ie, ALU.mult, ALU.add))
            ch.link(V_.tensor_reduce(pick[:, :], t4[:, :, :], AX.X, ALU.min))
            ch.link(V_.tensor_tensor(onehot[:, :, :], ie8, b4(pick), ALU.is_equal))

        gl = lg[:, :, 0:N_G]
        first_max(gl, gtop, g1h)
        V_.tensor_tensor(gex[:, :, :], gl, b4(gtop), ALU.subtract).then_inc(gd_ok, 1)
        ge = g1h[:, :, :].unsqueeze(3).broadcast_to([P, TT, N_G, E_G])
        for i in range(TT):
            last = ch.mark(V_.tensor_tensor(e16[:, i], lg[:, i, N_G:].rearrange("p (g e) -> p g e", e=E_G), ge[:, i],
                                            ALU.mult))
        ch.need(last)
        ch.link(V_.tensor_reduce(e_in[:, :, :], e16[:, :, :, :].rearrange("p i g e -> p i e g"), AX.X, ALU.add))
        first_max(e_in[:, :, :], etop1, o1h[0])
        ch.link(V_.scalar_tensor_tensor(e_in[:, :, :], o1h[0][:, :, :], -3e38, e_in[:, :, :], ALU.mult, ALU.add))
        first_max(e_in[:, :, :], etop2, o1h[1])
        for k in range(2):
            for i in range(TT):
                last = ch.mark(V_.tensor_tensor(masks[:, k, i], ge[:, i],
                                                o1h[k][:, i, :].unsqueeze(1).broadcast_to([P, N_G, E_G]), ALU.mult))
        ch.need(last)
        dve.wait_ge(iota_ok, 1)
        flat = lambda k: masks[:, k].rearrange("p i g e -> p (i g e)")
        ch.link(V_.tensor_tensor(both[:, 0:TT, :].rearrange("p i e -> p (i e)"), flat(0), flat(1), ALU.add))
        for i in range(TT):
            ins = V_.tensor_tensor(past[:, i + 1, :], past[:, i, :], both[:, i, :], ALU.add)
            ch.link(ins) if i < TT - 1 else ins.then_inc(m_ok, 1)
        V_.tensor_tensor(ediff[:, :], etop2[:, :], etop1[:, :], ALU.subtract).then_inc(ed_ok, 1)
        m01 = masks[:, :, :, :, :].rearrange("p k i g e -> p (k i) (g e)")
        per = lambda t: t.unsqueeze(1).broadcast_to([P, 2 * TT, N_E])
        ch.link(V_.tensor_tensor(pr[:, :, :], m01, per(io_r[:, 0:N_E]), ALU.mult))
        ch.link(V_.tensor_reduce(pex[:, :], pr[:, :, :], AX.X, ALU.add))
        dve.wait_ge(rank_ok, 1)
        cnt = o_ps[:, TT * N_E:(TT + 1) * N_E]
        ch.link(V_.tensor_scalar(nch[:, :], cnt, thr[:, 0:1], None, ALU.is_gt))
        for k in range(1, MAXR - 1):
            ch.link(V_.scalar_tensor_tensor(nch[:, :], cnt, thr[:, k:k + 1], nch[:, :], ALU.is_gt, ALU.add))
        ch.link(V_.tensor_tensor_scan(oend[:, :], one16[:, :], nch[:, :], 0.0, ALU.mult, ALU.add))
        ch.link(V_.tensor_tensor(obase[:, :], oend[:, :], nch[:, :], ALU.subtract))
        ch.link(V_.scalar_tensor_tensor(obase[:, :], obase[:, :], N_E - 1.0, io_r[:, 0:N_E], ALU.add, ALU.subtract))
        ch.link(V_.tensor_tensor(pr[:, :, :], m01, per(obase[:, :]), ALU.mult))
        ch.link(V_.tensor_reduce(pob[:, :], pr[:, :, :], AX.X, ALU.add))
        ch.link(V_.tensor_tensor(pr[:, :, :].rearrange("p (k i) e -> p k (i e)", k=2),
                                 m01.rearrange("p (k i) e -> p k (i e)", k=2),
                                 o_ps[:, 0:TT * N_E].unsqueeze(1).broadcast_to([P, 2, TT * N_E]), ALU.mult))
        ch.link(V_.tensor_reduce(prk[:, :], pr[:, :, :], AX.X, ALU.add))
        ch.link(V_.tensor_scalar(pf1[:, :], prk[:, :], thr[:, 0:1], None, ALU.is_ge))
        ch.link(V_.scalar_tensor_tensor(pfl[:, :], prk[:, :], thr[:, 1:2], pf1[:, :], ALU.is_ge, ALU.add))
        for k in range(2, MAXR - 1):
            ch.link(V_.scalar_tensor_tensor(pfl[:, :], prk[:, :], thr[:, k:k + 1], pfl[:, :], ALU.is_ge, ALU.add))
        ch.link(V_.scalar_tensor_tensor(prow[:, :], pfl[:, :], -float(CHUNK), prk[:, :], ALU.mult, ALU.add))
        last = ch.mark(V_.tensor_tensor(roh[:, :, :], io_r[:, :].unsqueeze(1).broadcast_to([P, 2 * TT, CHUNK]),
                                        prow[:, :].unsqueeze(2).broadcast_to([P, 2 * TT, CHUNK]), ALU.is_equal))
        ch.link(V_.tensor_tensor(pf1[:, :], pf1[:, :], pob[:, :], ALU.mult))
        ch.link(V_.tensor_tensor(pch[:, :], pex[:, :], pfl[:, :], ALU.add))
        ch.link(V_.tensor_tensor(pch[:, :], pch[:, :], pf1[:, :], ALU.add))
        ch.link(V_.tensor_tensor(ceq[:, :, :], io_r[:, 0:NIDX].unsqueeze(1).broadcast_to([P, 2 * TT, NIDX]),
                                 pch[:, :].unsqueeze(2).broadcast_to([P, 2 * TT, NIDX]), ALU.is_equal))
        V_.tensor_tensor(coh[:, :, :].rearrange("p (k i) c -> p k i c", k=2),
                         ceq[:, :, :].rearrange("p (k i) c -> p k i c", k=2),
                         tok[:, :].unsqueeze(1).unsqueeze(3).broadcast_to([P, 2, TT, NIDX]), ALU.mult
                         ).then_inc(oh_ok, 1)
        last = ch.mark(V_.tensor_copy(tablef[:, 0:N_E], io_r[:, 0:N_E]))
        ch.link(V_.tensor_tensor(over9[:, :, :], io_r[:, 0:MAXO + 1].unsqueeze(2).broadcast_to([P, MAXO + 1, N_E]),
                                 oend[:, :].unsqueeze(1).broadcast_to([P, MAXO + 1, N_E]), ALU.is_ge))
        ch.link(V_.tensor_tensor(npair[:, :], oend[:, N_E - 1:N_E].broadcast_to([P, MAXO // 2]), even[:, :],
                                 ALU.is_gt))
        ch.link(V_.tensor_reduce(tablef[:, N_E:MAXC + 1], over9[:, :, :], AX.X, ALU.add))
        ch.link(V_.tensor_scalar(tablef[:, N_E:MAXC + 1], tablef[:, N_E:MAXC + 1], N_E - 1.0, None, ALU.min))
        ch.link(V_.tensor_reduce(tablef[:, MAXC + 1:MAXC + 2], npair[:, :], AX.X, ALU.add))
        ch.link(V_.tensor_scalar(tablef[:, MAXC + 2:MAXC + 3], tablef[:, MAXC + 1:MAXC + 2], N_E // 2 - 1.0, None,
                                 ALU.add))
        ch.link(V_.tensor_scalar(tablef[:, MAXC + 1:MAXC + 2], tablef[:, MAXC + 1:MAXC + 2], N_E // 2 + 0.0, None,
                                 ALU.add))
        V_.tensor_copy(table[:, :], tablef[:, :]).then_inc(table_ok, 1)
        ch.link(V_.scalar_tensor_tensor(slot_i[:, :], pch[:, :], float(CHUNK), prow[:, :], ALU.mult, ALU.add))
        dve.wait_ge(idxp_ok, 1)
        dve.wait_ge(table_ok, 1)
        V_.tensor_copy(idx[:, :], o_ps[0:CHUNK, 128:128 + NIDX]).then_inc(route_ok, 1)
        dve.wait_ge(gexp_ok, 1)
        ch.link(V_.tensor_reduce(gsum[:, :], gex[:, :, :], AX.X, ALU.add))
        dve.wait_ge(eexp_ok, 1)
        ch.link(V_.tensor_scalar(wden[:, :], ediff[:, :], 1.0, None, ALU.add))
        ch.link(V_.tensor_tensor(wden[:, :], wden[:, :], gsum[:, :], ALU.mult))
        ch.link(V_.reciprocal(slot_w[0][:, :], wden[:, :]))
        ch.link(V_.tensor_tensor(slot_w[1][:, :], slot_w[0][:, :], ediff[:, :], ALU.mult))

        def split_unit_lo(j, p):
            n = j if p is None else p * RAW + j
            dve.wait_ge(e_hi_ok, n + 1)
            V_.tensor_tensor(e_lo[j % CONV][:, :], e_raw[j % RAW][:, :], e_hi[j % CONV][:, :].bitcast(F32),
                             ALU.subtract).then_inc(e_lo_ok, 1)

        def x_lo_half(m, h):
            dve.wait_ge(x_hi_ok, m + 1)
            V_.tensor_tensor(xT_lo[:, 4 * h:4 * h + 4, :], pj[:, 2 + h, :].rearrange("p (k c) -> p k c", c=P),
                             xT_hi[:, 4 * h:4 * h + 4, :].bitcast(F32), ALU.subtract).then_inc(x_lo_ok, 1)

        def chunk(p, h):
            u, m = h * UNITS, p * 4 + 2 * h
            for j in range(3):
                split_unit_lo(u + 3 + j, p)
            dve.wait_ge(silu_ok, p * 2 + (h + 1))
            dve.wait_ge(e_used, p * RAW + (u + 4))
            for half in range(2):
                f = slice(half * 256, (half + 1) * 256)
                V_.tensor_tensor(hid[:, f], hid[:, f], pj[:, 1, f], ALU.mult).then_inc(hid_ok, 1)

            def h_lo(half):
                dve.wait_ge(h_hi_ok, m + (half + 1))
                V_.tensor_tensor(hT_lo[:, 2 * half:2 * half + 2, :],
                                 ht_ps[half][:, 0:2 * P].rearrange("p (k c) -> p k c", c=P),
                                 hT_hi[:, 2 * half:2 * half + 2, :].bitcast(F32), ALU.subtract).then_inc(h_lo_ok, 1)

            h_lo(0)
            x_lo_half(m + 2, 0)
            h_lo(1)
            x_lo_half(m + 3, 1)
            for j in range(3):
                split_unit_lo(u + 6 + j, p)

        x_lo_half(0, 0)
        x_lo_half(1, 1)
        dve.wait_ge(e_lo_ok, CONV - 1)
        pairs = dve.value_load(table[0:1, MAXC + 1:MAXC + 2], min_val=N_E // 2, max_val=MAXC // 2)
        with dve.Fori(0, pairs) as p:
            for h in range(2):
                chunk(p, h)

        dve.wait_ge(gfin_in, 16)
        for i in range(TT):
            dve.wait_ge(f_in[i], 32)
            for j in range(2):
                ins = V_.scalar_tensor_tensor(X[:, i, :], F[j][:, i, :], slot_w[j][:, i:i + 1], X[:, i, :],
                                              ALU.mult, ALU.add)
                ch.link(ins) if j == 0 else ins.then_inc(hf_ok, 1)
            dve.wait_ge(ssq3_ok, i + 1)
            V_.tensor_scalar(stat3[:, 1, i:i + 1], stat3[:, 0, i:i + 1], 1.0 / D, EPS, ALU.mult, ALU.add
                             ).then_inc(var3_ok, 1)
            dve.wait_ge(std3_ok, i + 1)
            ch.link(V_.reciprocal(stat3[:, 0, i:i + 1], stat3[:, 2, i:i + 1]))
            V_.scalar_tensor_tensor(fo[:, i % 2, :], X[:, i, :], stat3[:, 0, i:i + 1], gfin[:, :],
                                    ALU.mult, ALU.mult).then_inc(fo_ok, 1)

    @block.tensor
    def _(pe):
        mm, tp = nc.tensor.matmul, nc.tensor.transpose
        pe.wait_ge(const_ok, 1)
        pe.wait_ge(prm_in, 128)
        tp(s_ps[:, 0, 0:104], prm[:, :], ident[0:104, 0:104]).then_inc(prmT_ok, 1)
        pe.wait_ge(mn_ok, 1)
        pe.wait_ge(xn_ok, TT)
        for k in range(KT):
            if k >= 3:
                pe.wait_ge(nt_lo_ok, k - 2)
            elif k == 2:
                pe.wait_ge(prm_ok, 1)
            c = slice(k * P, (k + 1) * P)
            tp(nt_ps(k, 0)[:, 0:META], mn[:, c], ident[0:META, 0:META])
            for i in range(TT - 1):
                tp(nt_ps(k, 0)[:, META + i * P:META + (i + 1) * P], xn[:, i, c], ident[:, :])
            tp(nt_ps(k, 1)[:, 0:P], xn[:, TT - 1, c], ident[:, :]).then_inc(nt_full, 1)

        def weights(phase, u, it=0):
            s, n = unit(phase, u, it)
            pe.wait_ge(w_lo_ok[s], n + 1)
            return s, (w_hi[s], w_lo[s])

        def project_T(phase, u, it, p):
            s, w = weights(phase, u, it)
            for k in range(KT):
                for n, (i, j) in enumerate(PASSES):
                    for h in range(2):
                        st, sp_ = k == 0 and n == 0, k == KT - 1 and n == 2
                        last = mm(pj[:, 2 * p + h, 0:HALF], w[i][:, k, :], NT[j][:, k, h * HALF:(h + 1) * HALF],
                                  start=st, stop=sp_)
            last.then_inc(w_used[s], 1)

        def project(phase, u, it, dst, act_parts, k0=0, k1=KT, off=0):
            s, w = unit(phase, u, it)[0], None
            if k0 == 0:
                weights(phase, u, it)
            w = (w_hi[s], w_lo[s])
            for k in range(k0, k1):
                for n, (i, j) in enumerate(PASSES):
                    last = mm(dst, w[i][:, k, :], act_parts[j][:, k, off:off + SEQ],
                              start=k == 0 and n == 0, stop=k == KT - 1 and n == 2)
            if k1 == KT:
                last.then_inc(w_used[s], 1)

        pe.wait_ge(nt_lo_ok, KT)
        for kv in range(KV):
            project_T("kv", kv, 0, kv)
        for c in range(2):
            pe.wait_ge(k_lo_ok, c + 1)
            project_T("kv", 2 + c, 0, c)
        for c in range(2):
            pe.wait_ge(vT_ok, c + 1)
            tp(s_ps[0:META, c, 0:P], a2[c][:, 0:META], ident[:, :])
            for t in range(TT):
                last = tp(v_ps[c][:, t * P:(t + 1) * P], a2[c][:, META + t * P:META + (t + 1) * P], ident[:, :])
            last.then_inc(v_full, 1)

        with pe.Fori(0, 4) as it:
            kv = pe.snap(it // 2)
            pe.wait_ge(thi_ok, it * 4)
            project_T("mix", 0, it, 0)
            pe.wait_ge(gelu_ok, it)
            project_T("mix", 1, it, 1)
            pe.wait_ge(xr_ok, it * 2 + 1)
            project("mix", 2, it, pj[:, 0, :], NT, off=META)
            project("mix", 3, it, pj[:, 1, :], NT, off=META)
            QT, K = (qT_hi, qT_lo), (kT_hi, kT_lo)

            def scores(a):
                hh, j = divmod(a, 4)
                w, k0 = S_W[j + 1], S_K[j + 1]
                if a in (0, 4):
                    pe.wait_ge(q_ok, it * 2 + (hh + 1))
                pe.wait_ge(tt_ok, it * 8 + max(a - 1, 0))
                parts = ((0, 0, w),) if k0 == 16 else ((0, 0, 16), (16, k0, w - 16))
                for d0, s0, n_ in parts:
                    for n, (i, l) in enumerate(PASSES):
                        last = mm(s_ps[:, a % 2, d0:d0 + n_], QT[i][:, hh, j * P:(j + 1) * P],
                                  K[l][:, bass.ds(kv, 1), s0:s0 + n_].rearrange("p a t -> p (a t)"),
                                  start=n == 0, stop=n == 2)
                last.then_inc(s_full, 1)

            def transpose_p(a):
                hh, j = divmod(a, 4)
                pe.wait_ge(p_ok, it * 8 + (a + 1))
                pe.wait_ge(pt_free, it * 10 + (PT_N[a] - 1))
                nb = len(S_V[j + 1])
                tp(pt_ps[0:META, 0:P], s_sb[a % 2][:, 0:META], ident[:, :])
                for b in range(nb):
                    last = tp(pt_ps[:, (b + 1) * P:(b + 2) * P], s_sb[a % 2][:, META + b * P:META + (b + 1) * P],
                              ident[:, :])
                last.then_inc(pt_full, 1)

            def values(a):
                hh, j = divmod(a, 4)
                if j == 0:
                    pe.wait_ge(onorm_ok, it * 2 + hh)
                pe.wait_ge(pt_free, it * 10 + PT_N[a])
                dst = o_ps[:, j * P:(j + 1) * P]
                vs = lambda r, t: V[r, t, bass.ds(vo, P)]
                for b, t in enumerate(S_V[j + 1]):
                    mm(dst, pt_sb[a % 2][:, (b + 1) * P:(b + 2) * P], vs(slice(0, P), t), start=b == 0, stop=False)
                mm(dst, pt_sb[a % 2][0:META, 0:P], vs(slice(0, META), 0), start=False, stop=True
                   ).then_inc(o_done, 1)

            def transpose_o(hh):
                pe.wait_ge(onorm_ok, it * 2 + (hh + 1))
                pe.wait_ge(pt_free, it * 10 + (OT_N[hh] - 1))
                for j in range(TT):
                    last = tp(pt_ps[:, j * P:(j + 1) * P], o_sb[:, j, :], ident[:, :])
                last.then_inc(pt_full, 1)

            def lru(j, bb, d, which):
                s = unit("mix", 4, it)[0]
                w = (w_hi[s], w_lo[s])
                XC = (xc_hi, xc_lo)
                p = j % 2
                if d == 0:
                    for n_, (i, l) in enumerate(PASSES):
                        for h in range(2):
                            last = mm(pj[:, 2 * p + h, 0:HALF], w[i][:, 4 * which + bb, :],
                                      XC[l][:, bb, h * HALF:(h + 1) * HALF], start=n_ == 0, stop=n_ == 2)
                else:
                    for q in range(2):
                        for n_, (i, l) in enumerate(PASSES):
                            last = mm(pj[:, 2 * p + q, :], w[i][:, 4 * q + 2 + bb, :], XC[l][:, bb, META:T],
                                      start=n_ == 0, stop=n_ == 2)
                last.then_inc(lru_full if j < 8 else w_used[s], 1)

            vo = pe.snap(kv * P)
            weights("mix", 4, it)
            pe.wait_ge(xcl_ok, it * 2 + 2)
            pe.wait_ge(xr_ok, it * 2 + 2)
            lru(3, 0, 0, 0)
            pe.wait_ge(v_rows_ok, 2)
            scores(0)
            scores(1)
            pe.wait_ge(q_ok, it * 2 + 2)
            lru(4, 0, 0, 1)
            pe.wait_ge(tha_ok, it * 2 + 1)
            lru(5, 0, 1, 0)
            transpose_p(0)
            scores(2)
            pe.wait_ge(thi_ok, it * 4 + 1)
            lru(6, 1, 0, 0)
            values(0)
            transpose_p(1)
            scores(3)
            pe.wait_ge(thi_ok, it * 4 + 2)
            lru(7, 1, 0, 1)
            values(1)
            transpose_p(2)
            scores(4)
            pe.wait_ge(tha_ok, it * 2 + 2)
            lru(8, 1, 1, 0)
            values(2)
            transpose_p(3)
            scores(5)
            pe.wait_ge(thi_ok, it * 4 + 3)
            y0, y1 = pj[:, 2, :], pj[:, 3, :]
            project("mix", 5, it, y0, NT, 0, 4, META)
            values(3)
            transpose_p(4)
            scores(6)
            project("mix", 5, it, y0, NT, 4, KT, META)
            transpose_o(0)
            values(4)
            transpose_p(5)
            scores(7)
            project("mix", 6, it, y1, NT, 0, 4, META)
            values(5)
            transpose_p(6)
            values(6)
            transpose_p(7)
            project("mix", 6, it, y1, NT, 4, KT, META)
            values(7)
            transpose_o(1)

        REC, ATT, MG = (rec_hi, rec_lo), (attn_hi, attn_lo), (mg_hi, mg_lo)

        def branch_gates(m):
            pe.wait_ge(gate_ok, m)
            project("branch", 0, m, pj[:, 0, :], NT, off=META)
            project("branch", 1, m, pj[:, 1, :], NT, off=META)

        def branch_pair(m):
            pe.wait_ge(m2_ok, m)
            project("branch", 2, m, pj[:, 2, :], ATT)
            project("branch", 3, m, pj[:, 3, :], REC)

        pe.wait_ge(thi_ok, 16)
        pe.wait_ge(gelu_ok, 4)
        with pe.Fori(0, KT) as m:
            branch_gates(m)
            pe.wait_ge(br_lo_ok, 2)
            branch_pair(m)

        def h_rows_T(k):
            pe.wait_ge(h_ok, k + 1)
            if k >= 2:
                pe.wait_ge(n2l_ok, k - 1)
            for i in range(TT):
                last = tp(pj[:, 2 * (k % 2) + 1, i * P:(i + 1) * P], X[:, i, k * P:(k + 1) * P], ident[:, :])
            last.then_inc(rt_full, 1)

        def logits(k):
            pe.wait_ge(n2l_ok, k + 1)
            for n, (i, j) in enumerate(PASSES):
                last = mm(o_ps[:, :], (wrt_hi, wrt_lo)[i][:, k, :], (n2t_hi, n2t_lo)[j][:, k % 2, :],
                          start=k == 0 and n == 0, stop=k == KT - 1 and n == 2)
            last.then_inc(lg_mm, 1)

        def back(it, j):
            if it:
                pe.wait_ge(h_ok, it * 2 - 1 + j)
            pe.wait_ge(oT_ok, it * 2 + (j + 1))
            for i in range(TT):
                last = tp(s_ps[:, j, i * P:(i + 1) * P], oT_sb[j][:, i * P:(i + 1) * P], ident[:, :])
            last.then_inc(oT_full, 1)

        for it in range(4):
            if it:
                pe.wait_ge(oT_ok, it * 2 - 1)
            else:
                pe.wait_ge(ml_ok, KT)
            project("out", 0, it, pj[:, 0, :], MG)
            if it:
                h_rows_T(2 * it - 2)
                h_rows_T(2 * it - 1)
                pe.wait_ge(oT_ok, it * 2)
            project("out", 1, it, pj[:, 2, :], MG)
            back(it, 0)
            if it:
                if it == 1:
                    pe.wait_ge(wrt_ok, 1)
                logits(2 * it - 2)
                logits(2 * it - 1)
            back(it, 1)
        h_rows_T(KT - 2)
        h_rows_T(KT - 1)
        logits(KT - 2)
        logits(KT - 1)

        NC = N_G + N_E
        pe.wait_ge(lgT_ok, 1)
        for i in range(TT):
            last = tp(pt_ps[:, i * NC:(i + 1) * NC], lgT[:, i * P:(i + 1) * P], ident[0:NC, 0:NC])
        last.then_inc(lg_ok, 1)
        pe.wait_ge(m_ok, 1)
        rk = o_ps[:, 0:(TT + 1) * N_E]
        mm(rk, tri[:, :], both[:, :, :].rearrange("p i e -> p (i e)"), start=True, stop=False)
        mm(rk, ones[:, :], past[:, :, :].rearrange("p i e -> p (i e)"), start=False, stop=True).then_inc(rank_ok, 1)
        pe.wait_ge(oh_ok, 1)
        for i in range(2 * TT):
            last = mm(o_ps[0:CHUNK, 128:128 + NIDX], roh[:, i, :], coh[:, i, :], start=i == 0, stop=i == 2 * TT - 1)
        last.then_inc(idxp_ok, 1)
        pe.wait_ge(route_ok, 1)

        def x_rows(odd, h):
            for k in range(4 * h, 4 * h + 4):
                last = tp(pj[:, 2 + h, (k % 4) * CHUNK:(k % 4 + 1) * CHUNK], G[odd][:, k * P:(k + 1) * P],
                          ident[:, :])
            last.then_inc(xt_full[odd], 1)

        XT, HT = (xT_hi, xT_lo), (hT_hi, hT_lo)

        def half_product(dst, act_parts, u, p):
            s = u % CONV
            pe.wait_ge(e_lo_ok, p * RAW + (u + 1))
            for k in range(4):
                for n, (i, j) in enumerate(PASSES_X):
                    last = mm(dst, act_parts[i][:, 4 * (u % 2) + k, :], (e_hi, e_lo)[j][s][:, k * FF:(k + 1) * FF],
                              start=u % 2 == 0 and k == 0 and n == 0, stop=u % 2 == 1 and k == 3 and n == 2)
            last.then_inc(e_used, 1)

        def chunk(p, h):
            c, u, m = p * 2 + h, h * UNITS, p * 4 + 2 * h
            pe.wait_ge(x_lo_ok, m + 2)
            pe.wait_ge(silu_ok, c)
            half_product(pj[:, 0, :], XT, u, p)
            half_product(pj[:, 0, :], XT, u + 1, p)
            pe.wait_ge(hid_ok, m)
            half_product(pj[:, 1, :], XT, u + 2, p)
            half_product(pj[:, 1, :], XT, u + 3, p)

            def h_rows(half):
                pe.wait_ge(hid_ok, m + (half + 1))
                for k in range(2 * half, 2 * half + 2):
                    last = tp(ht_ps[half][:, (k % 2) * P:(k % 2 + 1) * P], hid[:, k * P:(k + 1) * P], ident[:, :])
                last.then_inc(ht_full, 1)

            pe.wait_ge(g_in[1 - h], p * 16 + (h + 1) * 16)
            x_rows(1 - h, 0)
            h_rows(0)
            x_rows(1 - h, 1)
            h_rows(1)
            for half in range(2):
                v = u + 4 + half
                s = v % CONV
                pe.wait_ge(h_lo_ok, m + (half + 1))
                pe.wait_ge(e_lo_ok, p * RAW + (v + 1))
                if half == 0:
                    pe.wait_ge(y_ok, c)
                for k in range(2):
                    for n, (i, j) in enumerate(PASSES_X):
                        for d in range(2):
                            last = mm(s_ps[:, d, :], HT[i][:, 2 * half + k, :],
                                      (e_hi, e_lo)[j][s][:, k * D + d * 512:k * D + (d + 1) * 512],
                                      start=half == 0 and k == 0 and n == 0, stop=half == 1 and k == 1 and n == 2)
                last.then_inc(e_used, 1)

        pe.wait_ge(g_in[0], 16)
        x_rows(0, 0)
        x_rows(0, 1)
        pairs = pe.value_load(table[0:1, MAXC + 1:MAXC + 2], min_val=N_E // 2, max_val=MAXC // 2)
        pe.sem_inc(flush, 1)
        with pe.Fori(0, pairs) as p:
            for h in range(2):
                chunk(p, h)

    ctx.close()


_INS = ['x', 'meta_tokens', 'norm_mix_g', 'w_in', 'conv_w', 'conv_b', 'lru_w_a', 'lru_b_a', 'lru_w_x', 'lru_b_x',
        'lru_lambda', 'attn_sink', 'w_attn_branch', 'w_rec_branch', 'w_out', 'norm_ffn_g', 'w_group', 'b_group',
        'w_router', 'b_router', 'moe_w_gate', 'moe_w_up', 'moe_w_down', 'final_norm_g']
_OUTS = [((1, SEQ, D), 'float32')]


def kernel(**inputs):
    import numpy as _np
    import concourse.bacc as _bacc
    from concourse import mybir as _mybir
    from concourse.bass_utils import run_bass_kernel_spmd as _run

    nc = _bacc.Bacc("TRN2", target_bir_lowering=False, num_devices=1)
    arrays, args = {}, []
    for name in _INS:
        a = _np.ascontiguousarray(inputs[name])
        arrays[f"in_{name}_dram"] = a
        args.append(nc.dram_tensor(f"in_{name}_dram", a.shape, _mybir.dt.from_np(a.dtype), kind="ExternalInput").ap())
    for i, (shape, dtype) in enumerate(_OUTS):
        dt = _mybir.dt.from_np(_np.dtype(dtype))
        args.append(nc.dram_tensor(f"out_{i}_dram", shape, dt, kind="ExternalOutput").ap())
    block_program(nc, *args)
    r = _run(nc, [arrays], core_ids=[0])
    return r.results[0]["out_0_dram"]
```

```python
import concourse.bass as bass
from concourse import mybir
from contextlib import ExitStack

P = 128
D = 1024
KT = D // P
SEQ = 512
META = 16
T = META + SEQ
HALF = T // 2
TT = SEQ // P
HEADS = 8
KV = 2
HD = 128
N_E = 16
N_G = 4
E_G = N_E // N_G
FF = 512
FT = FF // P
CHUNK = 128
MAXR = SEQ // CHUNK
MAXO = (2 * SEQ - 1) // CHUNK + 1
MAXC = N_E + MAXO
NIDX = MAXC + 2
UNITS = 6
RAW = 2 * UNITS
CONV = 4
EPS = 1e-6
COL_Q, COL_K, COL_V, COL_X, COL_Y, COL_GA, COL_GR = 0, 1024, 1280, 1536, 2560, 3584, 4608

F32 = mybir.dt.float32
F32R = mybir.dt.float32r
I32 = mybir.dt.int32
ACT = mybir.ActivationFunctionType
ALU = mybir.AluOpType
AX = mybir.AxisListType

PHASES = ["kv", "mix", "branch", "out"]
UNIT_SLOTS = {"kv": [0, 1, 2, 1], "mix": [0, 1, 2, 0, 1, 2, 1], "branch": [0, 1, 2, 1], "out": [0, 1]}
RUNS = {"kv": 1, "mix": 4, "branch": 8, "out": 4}

def unit(phase, u, it=0):
    slots = UNIT_SLOTS[phase]
    if u >= len(slots):
        return unit(phase, u - len(slots), it + 1)
    s = slots[u]
    before = 0
    for q in PHASES[:PHASES.index(phase)]:
        before += RUNS[q] * UNIT_SLOTS[q].count(s)
    before += slots[:u].count(s)
    return s, it * slots.count(s) + before


def w_in_target(phase, u, it=0):
    s, n = unit(phase, u, it)
    lru_slot = UNIT_SLOTS["mix"][4]
    extra = 0
    if s == lru_slot:
        order = PHASES.index(phase)
        if phase == "mix":
            run, at = it, u
            if u >= 7:
                run, at = it + 1, u - 7
            extra = run * 32 + (32 if at >= 4 else 0)
        elif order > PHASES.index("mix"):
            extra = RUNS["mix"] * 32
    return n * 32 + 32 + extra


def is_const(v):
    return isinstance(v, int)


def after(eng, sem, v):
    if not (is_const(v) and v == 0):
        eng.wait_ge(sem, v)


class Chain:

    def __init__(self, eng, sem):
        self.eng, self.sem, self.base, self.it, self.per, self.n = eng, sem, 0, 0, 0, 0

    def body(self, it, per):
        self.it, self.per, self.n = it, per, 0

    def mark(self, ins):
        ins.then_inc(self.sem, 1)
        self.n += 1
        return self.n

    def need(self, n):
        self.eng.wait_ge(self.sem, self.it * self.per + (self.base + n))

    def link(self, ins):
        self.need(self.mark(ins))

    def close(self, runs=1):
        assert runs == 1 or self.n == self.per, (self.n, self.per)
        self.base += runs * self.n
        self.it, self.per, self.n = 0, 0, 0


def block_program(nc, x, meta_tokens, norm_mix_g, w_in, conv_w, conv_b, lru_w_a, lru_b_a, lru_w_x, lru_b_x,
                  lru_lambda, attn_sink, w_attn_branch, w_rec_branch, w_out, norm_ffn_g, w_group, b_group,
                  w_router, b_router, moe_w_gate, moe_w_up, moe_w_down, final_norm_g, out):
    ctx = ExitStack()
    KB = 1024
    X_AT = 16512
    CONST_AT = X_AT + 16 * KB
    R1 = CONST_AT + 7 * KB
    REST = R1 + 68 * KB
    TAIL = REST + 96 * KB
    END = nc.sbuf_usable_end
    assert X_AT >= nc.sbuf_base

    class Region:

        def __init__(self, at, end):
            self.at, self.end = at, end

        def put(self, name, shape, dt=F32):
            size = 4
            for n in shape[1:]:
                size *= n
            t = nc.alloc_sbuf_tensor_at(name, shape, dt, offset=self.at)
            self.at += (size + 31) // 32 * 32
            assert self.at <= self.end, (name, self.at - self.end)
            return t

    X = Region(X_AT, CONST_AT).put("resid", [P, TT, D])
    cr = Region(CONST_AT, R1)
    ident = cr.put("ident", [P, P])
    nd_at = cr.at
    nd = cr.put("neg_dist", [P, 944])
    tri = cr.put("tri", [P, P])
    ones = cr.put("ones", [P, P])
    g12 = cr.put("g12", [P, 2, KT])
    stat = cr.put("norm_stat", [P, 3, TT + 1])
    stat2 = cr.put("norm_stat2", [P, 4, TT])
    stat3 = cr.put("norm_stat3", [P, 3, TT])
    thr = cr.put("chunk_thresholds", [P, MAXR - 1])
    even = cr.put("even_numbers", [P, MAXO // 2])
    iota_e = cr.put("iota_e", [P, 2, E_G])
    tok = cr.put("token_ids", [P, TT])
    bias_r = cr.put("router_bias", [P, N_G + N_E])
    wr = Region(R1, R1 + 36 * KB)
    w_raw = [wr.put(f"w_raw{s}", [P, KT, P]) for s in range(3)]
    w_hi = [wr.put(f"w_hi{s}", [P, KT, P], F32R) for s in range(3)]
    w_lo = [wr.put(f"w_lo{s}", [P, KT, P], F32R) for s in range(3)]
    n2t_hi = nc.alloc_sbuf_tensor_at("n2t_hi", [P, 2, SEQ], F32R, offset=R1 + 20 * KB)
    n2t_lo = nc.alloc_sbuf_tensor_at("n2t_lo", [P, 2, SEQ], F32R, offset=R1 + 32 * KB)
    lgT = nc.alloc_sbuf_tensor_at("logitsT", [N_G + N_E, SEQ], F32, offset=R1 + 8 * KB)
    mr = Region(R1 + 36 * KB, REST)
    kT_hi = mr.put("kT_hi", [P, KV, T], F32R)
    kT_lo = mr.put("kT_lo", [P, KV, T], F32R)
    V = mr.put("v_rows", [P, TT + 1, KV * HD])
    qT_hi = mr.put("qT_hi", [P, 2, SEQ], F32R)
    qT_lo = mr.put("qT_lo", [P, 2, SEQ], F32R)
    pt_sb = [mr.put(f"pt_sb{i}", [P, 4 * P]) for i in range(2)]
    o_sb = mr.put("o_sb", [P, TT, P])
    ndh = mr.put("neg_dist_h", [P, 944])
    rr = Region(REST, END)
    nT_hi = rr.put("nT_hi", [P, KT, T], F32R)
    nT_lo = rr.put("nT_lo", [P, KT, T], F32R)
    rec_at = rr.at
    rec = rr.put("rec", [P, KT, SEQ])
    attn = rr.put("attn", [P, KT, SEQ])
    PV = rr.put("par", [P, 15, 8])
    cur = rr.put("par_now", [P, 15, 2])
    nmax = rr.put("neg_max", [P, 2, TT])
    mx = rr.put("row_max", [P, 2, TT])
    rsum = rr.put("row_sum", [P, 2, TT])
    esink = rr.put("exp_sink", [P, TT])
    den = rr.put("denom", [P, TT])
    mix_at = rr.at
    ab = rr.put("lru_a", [P, 4, T])
    wb = rr.put("lru_w", [P, 4, T])
    vb = rr.put("lru_v", [P, 4, T])
    xr = rr.put("xr_pad", [P, 2, T + 4])
    xc = rr.put("xc", [P, 2, T])
    xc_hi = rr.put("xc_hi", [P, 2, T], F32R)
    xc_lo = rr.put("xc_lo", [P, 2, T], F32R)
    s_sb = [rr.put(f"s_sb{i}", [P, 400]) for i in range(2)]
    a2 = [rr.put(f"lru_a2_{i}", [P, T]) for i in range(2)]
    nr = Region(mix_at, END)
    xn = nr.put("xn_rows", [P, TT, D])
    msb = nr.put("meta_rows", [META, D])
    mn = nr.put("meta_n", [META, D])
    junk = nr.put("square_junk", [P, D])
    prm = nr.put("prm_rows", [104, P])
    spt = nr.put("softplus_tmp", [P, 8, 16])
    lo_r = Region(rec_at, mix_at)
    rec_lo = lo_r.put("rec_lo", [P, KT, SEQ], F32R)
    attn_lo = lo_r.put("attn_lo", [P, KT, SEQ], F32R)
    br = Region(mix_at, END)
    rec_hi = br.put("rec_hi", [P, KT, SEQ], F32R)
    br.at += KB
    attn_hi = br.put("attn_hi", [P, KT, SEQ], F32R)
    g_sb = br.put("gates", [P, 2, SEQ])
    m2 = br.put("gated", [P, 2, SEQ])
    ms = br.put("gated_sum", [P, SEQ])
    mgr = Region(R1 + 36 * KB, REST)
    mg_hi = mgr.put("mergeT_hi", [P, KT, SEQ], F32R)
    mg_lo = mgr.put("mergeT_lo", [P, KT, SEQ], F32R)
    tr = Region(TAIL, END)
    xn2 = tr.put("xn2_rows", [P, TT, D])
    tail2 = tr.at
    oT_sb = [tr.put(f"oT_sb{i}", [P, SEQ]) for i in range(2)]
    rt = Region(tail2, END)
    lg = rt.put("logits", [P, TT, N_G + N_E])
    g1h = rt.put("group_onehot", [P, TT, N_G])
    gex = rt.put("group_exp", [P, TT, N_G])
    e_in = rt.put("e_in_group", [P, TT, E_G])
    e16 = rt.put("e_masked", [P, TT, N_G, E_G])
    o1h = [rt.put(f"expert_onehot{i}", [P, TT, E_G]) for i in range(2)]
    t4 = rt.put("tmp4", [P, TT, E_G])
    gtop, etop1, etop2, pick, ediff, gsum, wden = (
        rt.put(n, [P, TT]) for n in ("group_top", "expert_top1", "expert_top2", "picked", "expert_diff",
                                     "group_sum", "weight_den"))
    slot_w = [rt.put(f"pair_weight{i}", [P, TT]) for i in range(2)]
    slot_i = rt.put("pair_slot", [P, 2 * TT], I32)
    idx = rt.put("chunk_rows", [CHUNK, NIDX], I32)
    idx_now = [rt.put(f"chunk_rows_now{i}", [CHUNK, 1], I32) for i in range(2)]
    silu_warm = rt.put("silu_warm", [P, 1])
    table = rt.put("chunk_table", [P, MAXC + 3], I32)
    mz = Region(R1 + 48 * KB, REST)
    masks = mz.put("masks_by_choice", [P, 2, TT, N_G, E_G])
    both = mz.put("masks", [P, TT + 1, N_E])
    past = mz.put("masks_before", [P, TT + 1, N_E])
    tablef = mz.put("chunk_tablef", [P, MAXC + 3])
    nch = mz.put("n_overflow", [P, N_E])
    oend = mz.put("overflow_end", [P, N_E])
    obase = mz.put("overflow_base", [P, N_E])
    over9 = mz.put("overflow_past", [P, MAXO + 1, N_E])
    npair = mz.put("pairs_over", [P, MAXO // 2])
    pr = mz.put("pair_tmp", [P, 2 * TT, N_E])
    pex, pob, prk, pf1, pfl, pch, prow = (
        mz.put(n, [P, 2 * TT]) for n in ("pair_expert", "pair_base", "pair_rank", "pair_over", "pair_fold",
                                         "pair_chunk", "pair_row"))
    roh = mz.put("row_onehot", [P, 2 * TT, CHUNK], F32R)
    ceq = mz.put("chunk_equal", [P, 2 * TT, NIDX])
    coh = mz.put("chunk_onehot", [P, 2 * TT, NIDX], F32R)
    io_r = mz.put("iota_rows", [P, CHUNK])
    one16 = mz.put("one16", [P, N_E])
    assert mz.at <= R1 + 64 * KB
    er = Region(REST, TAIL)
    e_raw = [er.put(f"e_raw{s}", [P, 2048]) for s in range(RAW)]
    pre = Region(er.at - 16 * KB, er.at)
    wrt_hi = pre.put("router_w_hi", [P, KT, P], F32R)
    wrt_lo = pre.put("router_w_lo", [P, KT, P], F32R)
    g2row = pre.put("ffn_gain_rows", [P, D])
    ec = Region(R1, R1 + 64 * KB)
    e_hi, e_lo = [], []
    for s in range(CONV):
        e_hi.append(ec.put(f"e_hi{s}", [P, 2048], F32R))
        e_lo.append(ec.put(f"e_lo{s}", [P, 2048], F32R))
    eh = Region(R1 + 64 * KB, REST)
    hid = eh.put("chunk_hidden", [CHUNK, FF])
    hT_hi = eh.put("chunk_hT_hi", [P, FT, CHUNK], F32R)
    hT_lo = rt.put("chunk_hT_lo", [P, FT, CHUNK], F32R)
    er2 = Region(TAIL, TAIL + 16 * KB)
    G = [er2.put("chunk_rows_x0", [CHUNK, D]), nc.alloc_sbuf_tensor_at("chunk_rows_x1", [CHUNK, D], F32, offset=nd_at)]
    y_sb = er2.put("chunk_y", [CHUNK, D])
    xT_hi = er2.put("chunk_xT_hi", [P, KT, CHUNK], F32R)
    xT_lo = er2.put("chunk_xT_lo", [P, KT, CHUNK], F32R)
    fr = Region(REST, REST + 52 * KB)
    F = [fr.put(f"pair_rows{i}", [P, TT, D]) for i in range(2)]
    fo = fr.put("final_rows", [P, TT, D])
    gfin = fr.put("final_gain", [P, D])
    wrt = cr.put("router_w", [P, KT, N_G + N_E])

    n2_dram = nc.dram_tensor("n2_rows", [SEQ, D], F32, kind="Internal").ap()
    y_dram = nc.dram_tensor("y_rows", [MAXC * CHUNK, D], F32, kind="Internal").ap()

    pj = ctx.enter_context(nc.psum_tensor("pj", [P, 4, 512], F32))
    s_ps = ctx.enter_context(nc.psum_tensor("s_ps", [P, 2, 512], F32))
    pt_ps = ctx.enter_context(nc.psum_tensor("pt_ps", [P, 512], F32))
    o_ps = ctx.enter_context(nc.psum_tensor("o_ps", [P, 512], F32))

    v_ps = (pt_ps, o_ps)
    ht_ps = (pt_ps, o_ps)

    def sem(name):
        return ctx.enter_context(nc.semaphore(name))

    def sems(name, n):
        return [sem(f"{name}{i}") for i in range(n)]

    x_in = sems("x_in", TT)
    meta_in = sem("meta_in")
    prm_in = sem("prm_in")
    wrt_in = sem("wrt_in")
    gfin_in = sem("gfin_in")
    act_chain, dve_chain, pool_chain = sem("act_chain"), sem("dve_chain"), sem("pool_chain")
    const_ok = sem("const_ok")
    NORM2_SSQ = 1
    ssq_ok, var_ok, std_ok, xn_ok = sem("ssq_ok"), sem("var_ok"), sem("std_ok"), sem("xn_ok")
    prm_ok = sem("prm_ok")
    prmT_ok, lam_abs_ok, lam_exp_ok, par_ok = sem("prmT_ok"), sem("lam_abs_ok"), sem("lam_exp_ok"), sem("par_ok")
    nT_hi_ok = sem("nT_hi_ok")
    w_in_ok, w_hi_ok, w_lo_ok, w_used = sems("w_in_ok", 3), sems("w_hi_ok", 3), sems("w_lo_ok", 3), sems("w_used", 3)
    nt_full, nt_lo_ok = sem("nt_full"), sem("nt_lo_ok")
    k_hi_ok, k_lo_ok, v_rows_ok = sem("k_hi_ok"), sem("k_lo_ok"), sem("v_rows_ok")
    lru_full, tha_ok = sem("lru_full"), sem("tha_ok")
    cur_ok, xr_ok, xc_ok, xch_ok, xcl_ok = sem("cur_ok"), sem("xr_ok"), sem("xc_ok"), sem("xch_ok"), sem("xcl_ok")
    qh_ok, q_ok = sem("qh_ok"), sem("q_ok")
    s_full, tt_ok, neg_ok, p_ok = sem("s_full"), sem("tt_ok"), sem("neg_ok"), sem("p_ok")
    pt_full, pt_free, o_done, onorm_ok, es_ok, ndh_ok = (sem("pt_full"), sem("pt_free"), sem("o_done"),
                                                         sem("onorm_ok"), sem("es_ok"), sem("ndh_ok"))
    thi_ok, a_ok, a2_ok, w_ok, v_ok, sq_ok, u_ok, scan_ok, gelu_ok, rec_ok = (
        sem(n) for n in ("thi_ok", "a_ok", "a2_ok", "w_ok", "v_ok", "sq_ok", "u_ok", "scan_ok", "gelu_ok", "rec_ok"))
    br_hi_ok, br_lo_ok = sem("br_hi_ok"), sem("br_lo_ok")
    gate_ok, m2_ok, ms_ok, mh_ok, ml_ok = (sem(n) for n in ("gate_ok", "m2_ok", "ms_ok", "mh_ok", "ml_ok"))
    oT_ok, oT_full, h_ok = sem("oT_ok"), sem("oT_full"), sem("h_ok")
    xn2_ok = sem("xn2_ok")
    n2_out, rt_full, lg_ok = sem("n2_out"), sem("rt_full"), sem("lg_ok")
    wrt0_ok, wrt_hi_ok, wrt_ok = sem("wrt0_ok"), sem("wrt_hi_ok"), sem("wrt_ok")
    n2h_ok, n2l_ok, lg_mm, lgT_ok = (sem(n) for n in ("n2h_ok", "n2l_ok", "lg_mm", "lgT_ok"))
    table_ok, xs_ok, xn2_last_ok = sem("table_ok"), sem("xs_ok"), sem("xn2_last_ok")
    gd_ok, gexp_ok, ed_ok, eexp_ok, m_ok, rank_ok, oh_ok, idxp_ok, route_ok = (
        sem(n) for n in ("gd_ok", "gexp_ok", "ed_ok", "eexp_ok", "m_ok", "rank_ok", "oh_ok", "idxp_ok", "route_ok"))
    iota_ok, idx_ok = sem("iota_ok"), sem("idx_ok")
    g2_in = sem("g2_in")
    rstd_ok, mn_ok, gain_ok, vT_ok, v_full = (sem(n) for n in ("rstd_ok", "mn_ok", "gain_ok", "vT_ok", "v_full"))
    ew_in = sems("ew_in", RAW)
    e_hi_ok, e_lo_ok, e_used = sem("e_hi_ok"), sem("e_lo_ok"), sem("e_used")
    g_in, xt_full = sems("g_in", 2), sems("xt_full", 2)
    x_hi_ok, x_lo_ok, silu_ok, hid_ok, ht_full, h_hi_ok, h_lo_ok, y_ok, y_out = (
        sem(n) for n in ("x_hi_ok", "x_lo_ok", "silu_ok", "hid_ok", "ht_full", "h_hi_ok",
                         "h_lo_ok", "y_ok", "y_out"))
    f_in = sems("f_in", TT)
    out_done = sem("out_done")
    hf_ok, fs_ok, fo_ok, fo_last_ok = (sem(n) for n in ("hf_ok", "fs_ok", "fo_ok", "fo_last_ok"))
    flush = sem("flush")
    pad_ok, zero_ok, y_zeroed = sem("pad_ok"), sem("zero_ok"), sem("y_zeroed")

    def nt_ps(k, h):
        return (pj[:, 0, :], pj[:, 1, :], pj[:, 2, :], pj[:, 3, :], s_ps[:, 0, :], s_ps[:, 1, :])[2 * (k % 3) + h]

    def kv_ps(kv):
        return (s_ps[:, 0:2, 0:HALF], pj[:, 2:4, 0:HALF])[kv]

    def made(eng, phase, u, it=0):
        s, n = unit(phase, u, it)
        eng.wait_ge(w_used[s], n + 1)

    def unit_split(eng, j, p=0):
        eng.wait_ge(e_lo_ok, p * RAW + (j + 1))

    block = ctx.enter_context(nc.Block())

    w_in_v = w_in[0].rearrange("(k p) c -> p k c", p=P)
    wa_v = w_attn_branch[0].rearrange("(k p) c -> p k c", p=P)
    wr_v = w_rec_branch[0].rearrange("(k p) c -> p k c", p=P)
    wo_v = w_out[0].rearrange("(k p) c -> p k c", p=P)
    lwa_v = lru_w_a[0].rearrange("r b d e -> d r b e")
    lwx_v = lru_w_x[0].rearrange("r b d e -> d r b e")

    PASSES = ((0, 0), (0, 1), (1, 0))
    NT = (nT_hi, nT_lo)
    S_W = {1: 272, 2: 400, 3: 400, 4: 272}
    S_ND = {1: 0, 2: 272, 3: 272, 4: 672}
    S_K = {1: 16, 2: 16, 3: 144, 4: 272}
    S_V = {1: (1, 2), 2: (1, 2, 3), 3: (2, 3, 4), 4: (3, 4)}
    PT_N = {a: (a + 1 if a <= 4 else a + 2) for a in range(8)}
    OT_N = {0: 6, 1: 10}

    @block.sync
    def _(sp):
        for i in range(TT):
            sp.dma_start(X[:, i, :], x[0, i * P:(i + 1) * P, :]).then_inc(x_in[i], 16)
            if i == 0:
                sp.dma_start(msb[:, :], meta_tokens[:, :]).then_inc(meta_in, 16)

        rows = lambda v: v.rearrange("(b c) -> b c", c=P)
        sp.dma_start(prm[0:32, :], conv_w[0].rearrange("i (b c) -> (i b) c", c=P)).then_inc(prm_in, 16)
        sp.dma_start(prm[32:40, :], rows(conv_b[0])).then_inc(prm_in, 16)
        sp.dma_start(prm[40:56, :], lru_b_a[0].rearrange("r (b c) -> (r b) c", c=P)).then_inc(prm_in, 16)
        sp.dma_start(prm[56:72, :], lru_b_x[0].rearrange("r (b c) -> (r b) c", c=P)).then_inc(prm_in, 16)
        sp.dma_start(prm[72:88, :], lru_lambda[0].rearrange("r (b c) -> (r b) c", c=P)).then_inc(prm_in, 16)
        sp.dma_start(prm[88:96, :], rows(norm_mix_g[0])).then_inc(prm_in, 16)
        sp.dma_start(prm[96:104, :], rows(norm_ffn_g[0])).then_inc(prm_in, 16)
        sp.dma_start(PV[:, 14, :], attn_sink[0].partition_broadcast(P)).then_inc(prm_in, 16)

        def load_unit(phase, u, it, src):
            s, n = unit(phase, u, it)
            if not (is_const(n) and n == 0):
                sp.wait_ge(w_lo_ok[s], n)
                sp.sem_inc(flush, 1)
            for h in range(2):
                sp.dma_start(w_raw[s][:, 4 * h:4 * h + 4, :], src(h)).then_inc(w_in_ok[s], 16)

        def cols(view, c):
            return lambda h: view[:, 4 * h:4 * h + 4, bass.ds(c, P)]

        for u, c in enumerate((COL_K, COL_K + P, COL_V, COL_V + P)):
            load_unit("kv", u, 0, cols(w_in_v, c))
        sp.dma_start(wrt[:, :, 0:N_G], w_group[0].rearrange("(k p) g -> p k g", p=P)).then_inc(wrt_in, 16)
        sp.dma_start(wrt[:, :, N_G:N_G + N_E], w_router[0].rearrange("(k p) g -> p k g", p=P)).then_inc(wrt_in, 16)
        sp.dma_start(bias_r[:, 0:N_G], b_group[0].partition_broadcast(P)).then_inc(wrt_in, 16)
        sp.dma_start(bias_r[:, N_G:N_G + N_E], b_router[0].partition_broadcast(P)).then_inc(wrt_in, 16)
        sp.wait_ge(zero_ok, 1)
        for c in range(N_E, MAXC):
            sp.dma_start(y_dram[c * CHUNK:(c + 1) * CHUNK, :].rearrange("p (a t) -> p a t", a=2),
                         rec[0:CHUNK, 0:2, :]).then_inc(y_zeroed, 16)
        with sp.Fori(0, 4) as it:
            c = sp.snap(it * 256)
            b = sp.snap(it * 2)
            load_unit("mix", 0, it, cols(w_in_v, c + COL_X))
            load_unit("mix", 1, it, cols(w_in_v, c + (COL_X + P)))
            load_unit("mix", 2, it, cols(w_in_v, c + COL_Q))
            load_unit("mix", 3, it, cols(w_in_v, c + (COL_Q + P)))
            s, n = unit("mix", 4, it)
            sp.wait_ge(w_lo_ok[s], n)
            sp.sem_inc(flush, 1)
            for h, view in enumerate((lwa_v, lwx_v)):
                for r in range(2):
                    sp.dma_start(w_raw[s][:, 4 * h + 2 * r:4 * h + 2 * r + 2, :],
                                 view[:, r, bass.ds(b, 2), :]).then_inc(w_in_ok[s], 16)
            load_unit("mix", 5, it, cols(w_in_v, c + COL_Y))
            load_unit("mix", 6, it, cols(w_in_v, c + (COL_Y + P)))
        with sp.Fori(0, 8) as m:
            c = sp.snap(m * 128)
            load_unit("branch", 0, m, cols(w_in_v, c + COL_GA))
            load_unit("branch", 1, m, cols(w_in_v, c + COL_GR))
            load_unit("branch", 2, m, cols(wa_v, c))
            load_unit("branch", 3, m, cols(wr_v, c))
        def load_expert_unit(s, e):
            which, h = divmod(s % UNITS, 2)
            view = (moe_w_gate, moe_w_up, moe_w_down)[which][0, bass.ds(e, 1)].rearrange(
                "a (k p) f -> p (a k) f", p=P)
            n = (4, 4, 2)[which]
            sp.dma_start(e_raw[s][:, :].rearrange("p (k f) -> p k f", k=n), view[:, n * h:n * (h + 1), :]
                         ).then_inc(ew_in[s], 16)

        def out_units(it):
            load_unit("out", 0, it, cols(wo_v, it * 256))
            load_unit("out", 1, it, cols(wo_v, it * 256 + P))

        out_units(0)
        out_units(1)
        made(sp, "branch", 3, KT - 1)
        sp.wait_ge(ml_ok, KT)
        sp.dma_start(g2row[:, :], norm_ffn_g[0].partition_broadcast(P)).then_inc(g2_in, 16)
        for it in range(2, 4):
            for s in range(3 * (it - 2), 3 * (it - 1)):
                load_expert_unit(s, s // UNITS)
            out_units(it)
        for s in range(UNITS, RAW - 2):
            load_expert_unit(s, s // UNITS)
        for i in range(TT):
            if i == TT - 1:
                sp.wait_ge(xn2_last_ok, 1)
            else:
                sp.wait_ge(xn2_ok, i + 1)
            sp.dma_start(n2_dram[i * P:(i + 1) * P, :], xn2[:, i, :]).then_inc(n2_out, 16)
        sp.wait_ge(lg_mm, KT)
        load_expert_unit(RAW - 2, 1)
        load_expert_unit(RAW - 1, 1)
        for s in range(CONV - 1):
            unit_split(sp, s)
            load_expert_unit(s, 2)
        sp.wait_ge(table_ok, 1)
        more = sp.value_load(table[0:1, MAXC + 2:MAXC + 3], min_val=N_E // 2 - 1, max_val=MAXC // 2 - 1)
        with sp.Fori(0, more) as q:
            for n, c in ((CONV - 1, 2), (UNITS, 3), (RAW, 4)):
                e = sp.value_load(table[0:1, bass.ds(q * 2 + c, 1)], min_val=0, max_val=N_E - 1)
                for j in range(n, {CONV - 1: UNITS, UNITS: RAW, RAW: RAW + CONV - 1}[n]):
                    unit_split(sp, j, q)
                    sp.sem_inc(flush, 1)
                    load_expert_unit(j % RAW, e)
        for j in range(CONV - 1):
            unit_split(sp, RAW + j, more)
            sp.sem_inc(flush, 1)
        sp.sem_inc(flush, 1)
        sp.dma_start(gfin[:, :], final_norm_g.partition_broadcast(P)).then_inc(gfin_in, 16)
        for i in range(TT):
            if i >= TT - 2:
                sp.wait_ge(fo_last_ok, i - (TT - 2) + 1)
            else:
                sp.wait_ge(fo_ok, i + 1)
            sp.dma_start(out[0, i * P:(i + 1) * P, :], fo[:, i, :]).then_inc(out_done, 16)
        sp.wait_ge(out_done, 16 * TT)

    @block.gpsimd
    def _(pool):
        ch = Chain(pool, pool_chain)
        nc.gpsimd.memset(rec[0:CHUNK, 0:2, :], 0.0).then_inc(zero_ok, 1)
        nc.gpsimd.memset(ones[:, :], 1.0)
        nc.gpsimd.memset(stat[:, :, :], 1.0)
        for h in range(HEADS):
            nc.gpsimd.memset(PV[:, 13, h:h + 1], 2.0 ** (-8.0 * (h + 1) / HEADS))
        for k in range(MAXR - 1):
            nc.gpsimd.memset(thr[:, k:k + 1], float(CHUNK * (k + 1)))
        nc.gpsimd.iota(even[:, :], pattern=[[2, MAXO // 2]], base=0, channel_multiplier=0,
                       allow_small_or_imprecise_dtypes=True)
        for i in range(2):
            nc.gpsimd.iota(iota_e[:, i, :], pattern=[[1, E_G]], base=-8 * i, channel_multiplier=0,
                           allow_small_or_imprecise_dtypes=True)
        nc.gpsimd.iota(tok[:, :], pattern=[[P, TT]], base=0, channel_multiplier=1,
                       allow_small_or_imprecise_dtypes=True)
        nc.gpsimd.memset(nd[:, 0:16], 0.0)
        nc.gpsimd.memset(nd[:, 272:288], 0.0)
        nc.gpsimd.memset(nd[:, 672:688], 0.0)
        ch.link(nc.gpsimd.iota(nd[:, 288:672], pattern=[[1, 384]], base=-P, channel_multiplier=-1,
                               allow_small_or_imprecise_dtypes=True))
        ch.link(nc.gpsimd.affine_select(out=ident[:, :], in_=ones[:, :], compare_op=ALU.is_equal, fill=0.0, base=0,
                                        pattern=[[-1, P]], channel_multiplier=1))
        nc.gpsimd.affine_select(out=tri[:, :], in_=ones[:, :], compare_op=ALU.is_gt, fill=0.0, base=0,
                                pattern=[[1, P]], channel_multiplier=-1).then_inc(const_ok, 1)
        ch.link(nc.gpsimd.tensor_scalar(ndh[:, 0:384], nd[:, 288:672], -1.0, None, ALU.mult))
        ch.link(nc.gpsimd.affine_select(out=nd[:, 288:672], in_=nd[:, 288:672], compare_op=ALU.is_gt, fill=0.0,
                                        base=P, pattern=[[-1, 384]], channel_multiplier=1))
        ch.link(nc.gpsimd.affine_select(out=ndh[:, 0:384], in_=ndh[:, 0:384], compare_op=ALU.is_ge, fill=0.0,
                                        base=-P, pattern=[[1, 384]], channel_multiplier=-1))
        ch.link(nc.gpsimd.tensor_tensor(nd[:, 288:672], nd[:, 288:672], ndh[:, 0:384], ALU.add))
        ch.link(nc.gpsimd.affine_select(out=nd[:, 288:672], in_=nd[:, 288:672], compare_op=ALU.is_ge, fill=-1e32,
                                        base=0, pattern=[[1, 384]], channel_multiplier=-1))
        ch.link(nc.gpsimd.affine_select(out=nd[:, 288:672], in_=nd[:, 288:672], compare_op=ALU.is_ge, fill=-1e32,
                                        base=256, pattern=[[-1, 384]], channel_multiplier=1))
        nc.gpsimd.tensor_copy(nd[:, 16:272], nd[:, 288 + 128:672])
        ch.link(nc.gpsimd.tensor_copy(nd[:, 688:944], nd[:, 288:288 + 256]))
        ch.close()
        s0 = unit("kv", 0)[0]
        pool.wait_ge(w_hi_ok[s0], 1)
        nc.gpsimd.tensor_tensor(w_lo[s0][:, :, :], w_raw[s0][:, :, :], w_hi[s0][:, :, :].bitcast(F32), ALU.subtract
                                ).then_inc(w_lo_ok[s0], 1)
        pool.wait_ge(nt_lo_ok, KT)
        pool.wait_ge(par_ok, 1)
        nc.gpsimd.memset(xr[:, :, 0:2], 0.0)
        nc.gpsimd.memset(xr[:, :, T + 2:T + 4], 0.0).then_inc(pad_ok, 1)

        with pool.Fori(0, 4) as it:
            ch.body(it, 2)

            def head_bias(hh):
                pool.wait_ge(cur_ok, it + 1)
                pool.wait_ge(tt_ok, it * 8 + 4 * hh)
                pool.sem_inc(flush, 1)
                nc.gpsimd.tensor_scalar(ndh[:, :], nd[:, :], cur[:, 13, hh:hh + 1], None, ALU.mult
                                        ).then_inc(ndh_ok, 1)

            def square_a(i, bd):
                o = 0 if bd < 2 else META
                pool.wait_ge(a_ok, it * 4 + (i + 1))
                if i >= 2:
                    pool.wait_ge(w_ok, it * 4 + (i - 1))
                nc.gpsimd.tensor_tensor(a2[i % 2][:, o:T], ab[:, bd, o:T], ab[:, bd, o:T], ALU.mult
                                        ).then_inc(a2_ok, 1)

            head_bias(0)
            square_a(0, 0)
            square_a(1, 2)
            head_bias(1)
            square_a(2, 1)
            square_a(3, 3)
            pool.wait_ge(v_ok, it * 4 + 4)
            for d in range(2):
                o = META * d
                pool.wait_ge(sq_ok, it * 2 + (d + 1))
                for bb in range(2):
                    bd = 2 * d + bb
                    nc.gpsimd.tensor_tensor(vb[:, bd, o:T], vb[:, bd, o:T], wb[:, bd, o:T], ALU.mult
                                            ).then_inc(u_ok, 1)
            r = pool.snap(it * 2)
            marks = []
            for bb in range(2):
                pool.wait_ge(scan_ok, it * 4 + (3 + bb))
                marks.append(ch.mark(nc.gpsimd.tensor_tensor(a2[bb][:, 0:SEQ], wb[:, bb, META:T],
                                                             wb[:, 2 + bb, META:T], ALU.add)))
            pool.wait_ge(gelu_ok, it + 1)
            for bb in range(2):
                ch.need(marks[bb])
                nc.gpsimd.sem_inc(flush, 1)
                dst = rec[:, bass.ds(r + bb, 1), :].rearrange("p a t -> p (a t)")
                nc.gpsimd.tensor_tensor(dst, dst, a2[bb][:, 0:SEQ], ALU.mult).then_inc(rec_ok, 1)
        ch.close(4)

        with pool.Fori(0, KT) as m:
            pool.wait_ge(ml_ok, m)
            pool.wait_ge(m2_ok, m + 1)
            nc.gpsimd.tensor_tensor(ms[:, :], m2[:, 0, :], m2[:, 1, :], ALU.add).then_inc(ms_ok, 1)

        made(pool, "branch", 3, KT - 1)
        nc.gpsimd.memset(wrt_hi[:, :, :].bitcast(F32), 0.0)
        nc.gpsimd.memset(wrt_lo[:, :, :].bitcast(F32), 0.0).then_inc(wrt0_ok, 1)
        made(pool, "out", 1, 3)
        nc.gpsimd.memset(past[:, 0, :], 0.0)
        nc.gpsimd.memset(both[:, TT, :], 0.0)
        nc.gpsimd.memset(one16[:, :], 1.0)
        nc.gpsimd.iota(io_r[:, :], pattern=[[1, CHUNK]], base=0, channel_multiplier=0,
                       allow_small_or_imprecise_dtypes=True).then_inc(iota_ok, 1)

        pool.wait_ge(g2_in, 16)
        for i in range(TT - 1):
            pool.wait_ge(xs_ok, i + 1)
            nc.gpsimd.tensor_tensor(xn2[:, i, :], xn2[:, i, :], g2row[:, :], ALU.mult).then_inc(xn2_ok, 1)
        pool.wait_ge(n2_out, 16 * TT)
        pool.wait_ge(route_ok, 1)

        def gather(p, h):
            after(pool, g_in[h], p * 16)
            pool.sem_inc(flush, 1)
            nc.gpsimd.tensor_copy(idx_now[h][:, :], idx[:, bass.ds(p * 2 + h, 1)]).then_inc(idx_ok, 1)
            pool.wait_ge(idx_ok, p * 2 + (h + 1))
            after(pool, xt_full[h], p * 2)
            pool.sem_inc(flush, 1)
            pool.indirect_dma_start(G[h][:, :], None, n2_dram[:, :],
                                    bass.IndirectOffsetOnAxis(ap=idx_now[h][:, :], axis=0)).then_inc(g_in[h], 16)

        pairs = pool.value_load(table[0:1, MAXC + 1:MAXC + 2], min_val=N_E // 2, max_val=MAXC // 2)
        for h in range(2):
            gather(0, h)
        with pool.Fori(0, pairs) as p:
            for h in range(2):
                gather(p + 1, h)
        for j in range(CONV - 1):
            unit_split(pool, j, pairs)
            pool.sem_inc(flush, 1)
        pool.wait_ge(y_out, pairs * 32)
        pool.sem_inc(flush, 1)
        for i in range(TT):
            for j in range(2):
                pool.indirect_dma_start(F[j][:, i, :], None, y_dram[:, :],
                                        bass.IndirectOffsetOnAxis(ap=slot_i[:, TT * j + i:TT * j + i + 1], axis=0)
                                        ).then_inc(f_in[i], 16)
        pool.wait_ge(gfin_in, 16)
        for i in range(TT - 2):
            pool.wait_ge(fs_ok, i + 1)
            nc.gpsimd.tensor_tensor(fo[:, i, :], fo[:, i, :], gfin[:, :], ALU.mult).then_inc(fo_ok, 1)

    @block.scalar
    def _(act):
        ch = Chain(act, act_chain)

        def warm_sqrt(where):
            nc.scalar.activation(where, ones[:, 0:TT], ACT.Sqrt)

        act.wait_ge(const_ok, 1)
        warm_sqrt(stat[:, 2, 0:TT])
        for i in range(TT):
            act.wait_ge(x_in[i], 16)
            ins = nc.scalar.activation(junk[:, :], X[:, i, :], ACT.Square, accum_out=stat[:, 0, i:i + 1])
            ch.link(ins) if i < TT - 1 else ins.then_inc(ssq_ok, 1)
            if i == 0:
                act.wait_ge(meta_in, 16)
                ch.link(nc.scalar.activation(junk[0:META, :], msb[:, :], ACT.Square,
                                             accum_out=stat[0:META, 0, TT:TT + 1]))
        act.wait_ge(var_ok, 1)
        nc.scalar.activation(stat[:, 2, :], stat[:, 1, :], ACT.Sqrt).then_inc(std_ok, 1)
        act.wait_ge(rstd_ok, 1)
        nc.scalar.activation(mn[:, :], msb[:, :], ACT.Copy, scale=stat[0:META, 0, TT:TT + 1]).then_inc(mn_ok, 1)

        def split_hi(phase, u, it=0):
            s, n = unit(phase, u, it)
            act.wait_ge(w_in_ok[s], w_in_target(phase, u, it))
            if not (is_const(n) and n == 0):
                act.wait_ge(w_used[s], n)
            nc.scalar.activation(w_hi[s][:, :, :], w_raw[s][:, :, :], ACT.Copy).then_inc(w_hi_ok[s], 1)

        split_hi("kv", 0)
        for k in range(KT):
            act.wait_ge(nt_full, k + 1)
            if k == 0:
                act.wait_ge(gain_ok, 1)
            nc.scalar.activation(nT_hi[:, k, 0:400], nt_ps(k, 0)[:, 0:400], ACT.Copy, scale=g12[:, 0, k:k + 1])
            nc.scalar.activation(nT_hi[:, k, 400:T], nt_ps(k, 1)[:, 0:P], ACT.Copy, scale=g12[:, 0, k:k + 1]
                                 ).then_inc(nT_hi_ok, 1)
        split_hi("kv", 1)
        act.wait_ge(lam_abs_ok, 1)
        nc.scalar.activation(spt[:, 1, :], spt[:, 0, :], ACT.Exp, scale=-1.0).then_inc(lam_exp_ok, 1)

        for kv in range(KV):
            if kv == 0:
                split_hi("kv", 2)
            made(act, "kv", kv)
            nc.scalar.activation(kT_hi[:, kv, :].rearrange("p (h c) -> p h c", h=2), kv_ps(kv), ACT.Copy
                                 ).then_inc(k_hi_ok, 1)
        split_hi("kv", 3)
        split_hi("kv", 4)
        for c in range(2):
            made(act, "kv", 2 + c)
            nc.scalar.activation(a2[c][:, :].rearrange("p (h c) -> p h c", h=2), pj[:, 2 * c:2 * c + 2, 0:HALF],
                                 ACT.Copy).then_inc(vT_ok, 1)
        split_hi("kv", 5)
        for c in range(2):
            act.wait_ge(v_full, c + 1)
            nc.scalar.activation(V[:, 1:TT + 1, c * P:(c + 1) * P],
                                 v_ps[c][:, :].rearrange("p (t c) -> p t c", c=P), ACT.Copy)
            nc.scalar.activation(V[0:META, 0, c * P:(c + 1) * P], s_ps[0:META, c, 0:P], ACT.Copy
                                 ).then_inc(v_rows_ok, 1)
        ch.close()

        act.wait_ge(y_zeroed, 16 * (MAXC - N_E))
        with act.Fori(0, 4) as it:
            ch.body(it, 6)
            r = act.snap(it * 2)
            act.wait_ge(par_ok, 1)
            act.wait_ge(tt_ok, it * 8)
            act.sem_inc(flush, 1)
            nc.scalar.activation(cur[:, :, :], PV[:, :, bass.ds(r, 2)], ACT.Copy).then_inc(cur_ok, 1)
            act.wait_ge(cur_ok, it + 1)
            split_hi("mix", 2, it)
            for bb in range(2):
                p = bb
                act.wait_ge(xc_ok, it * 2)
                made(act, "mix", bb, it)
                nc.scalar.activation(xr[:, bb, 2:T + 2].rearrange("p (h c) -> p h c", h=2),
                                     pj[:, 2 * p:2 * p + 2, 0:HALF], ACT.Copy).then_inc(xr_ok, 1)
                split_hi("mix", 3 + bb, it)
            s4, n4 = unit("mix", 4, it)
            for bb in range(2):
                act.wait_ge(xc_ok, it * 2 + (bb + 1))
                act.wait_ge(w_used[s4], n4)
                nc.scalar.activation(xc_hi[:, bb, :], xc[:, bb, :], ACT.Copy).then_inc(xch_ok, 1)
            split_hi("mix", 5, it)
            for hh in range(2):
                made(act, "mix", 2 + hh, it)
                if hh == 0:
                    act.wait_ge(s_full, it * 8)
                nc.scalar.activation(qT_hi[:, hh, :], pj[:, hh, :], ACT.Copy, scale=HD ** -0.5).then_inc(qh_ok, 1)

            def lru_a(j, bd):
                d, bb = divmod(bd, 2)
                o = META * d
                act.wait_ge(scan_ok, it * 4)
                act.wait_ge(rec_ok, it * 2)
                p = j % 2
                if j == 8:
                    made(act, "mix", 4, it)
                else:
                    act.wait_ge(lru_full, it * 5 + (j - 2))
                if d == 0:
                    two = lambda t: t.rearrange("p (h c) -> p h c", h=2)
                    nc.scalar.activation(two(ab[:, bd, :]), pj[:, 2 * p:2 * p + 2, 0:HALF], ACT.Tanh,
                                         bias=cur[:, 5, bb:bb + 1], scale=0.5).then_inc(tha_ok, 1)
                    return None
                q = ch.mark(nc.scalar.activation(ab[:, bd, o:T], pj[:, 2 * p, :], ACT.Tanh,
                                                 bias=cur[:, 6, bb:bb + 1], scale=0.5))
                nc.scalar.activation(vb[:, bd, o:T], pj[:, 2 * p + 1, :], ACT.Tanh, bias=cur[:, 8, bb:bb + 1],
                                     scale=0.5).then_inc(thi_ok, 1)
                return q

            def lru_x(j, bb):
                p = j % 2
                act.wait_ge(lru_full, it * 5 + (j - 2))
                nc.scalar.activation(vb[:, bb, :].rearrange("p (h c) -> p h c", h=2), pj[:, 2 * p:2 * p + 2, 0:HALF],
                                     ACT.Tanh, bias=cur[:, 7, bb:bb + 1], scale=0.5).then_inc(thi_ok, 1)

            def lru_decay(q, bd):
                d, bb = divmod(bd, 2)
                o = META * d
                if q is None:
                    act.wait_ge(tha_ok, it * 2 + (bb + 1))
                else:
                    ch.need(q)
                q2 = ch.mark(nc.scalar.activation(wb[:, bd, o:T], ab[:, bd, o:T], ACT.Tanh,
                                                  bias=cur[:, 11 + d, bb:bb + 1], scale=cur[:, 11 + d, bb:bb + 1]))
                ch.need(q2)
                nc.scalar.activation(ab[:, bd, o:T], ab[:, bd, o:T], ACT.Exp,
                                     bias=cur[:, 9 + d, bb:bb + 1], scale=cur[:, 9 + d, bb:bb + 1]).then_inc(a_ok, 1)

            def exps(a):
                hh, j = divmod(a, 4)
                act.wait_ge(neg_ok, it * 8 + (a + 1))
                if a < 4:
                    act.wait_ge(onorm_ok, it * 2)
                w = S_W[j + 1]
                nc.scalar.activation(s_sb[a % 2][:, 0:w], s_sb[a % 2][:, 0:w], ACT.Exp, bias=nmax[:, hh, j:j + 1],
                                     accum_out=rsum[:, hh, j:j + 1]).then_inc(p_ok, 1)

            def exp_sink(hh):
                act.wait_ge(onorm_ok, it * 2 + hh)
                nc.scalar.activation(esink[:, :], nmax[:, hh, :], ACT.Exp, bias=cur[:, 14, hh:hh + 1]
                                     ).then_inc(es_ok, 1)

            def evac_o(hh):
                act.wait_ge(pt_full, it * 10 + OT_N[hh])
                act.sem_inc(flush, 1)
                nc.scalar.activation(attn[:, bass.ds(r + hh, 1), :].rearrange("p a t -> p (a t)"), pt_ps[:, :],
                                     ACT.Copy).then_inc(pt_free, 1)

            q0 = lru_a(3, 0)
            lru_x(4, 0)
            exps(0)
            q1 = lru_a(5, 2)
            exps(1)
            lru_decay(q0, 0)
            lru_decay(q1, 2)
            exps(2)
            q2 = lru_a(6, 1)
            lru_x(7, 1)
            exps(3)
            exp_sink(0)
            q3 = lru_a(8, 3)
            split_hi("mix", 6, it)
            exps(4)
            lru_decay(q2, 1)
            lru_decay(q3, 3)
            exps(5)
            split_hi("mix", 7, it)
            exps(6)
            evac_o(0)
            exps(7)
            exp_sink(1)
            act.wait_ge(w_ok, it * 4 + 4)
            for d in range(2):
                o = META * d
                nc.scalar.activation(wb[:, 2 * d:2 * d + 2, o:T], wb[:, 2 * d:2 * d + 2, o:T], ACT.Sqrt, scale=0.25
                                     ).then_inc(sq_ok, 1)
            p = 1
            made(act, "mix", 6, it)
            act.sem_inc(flush, 1)
            nc.scalar.activation(rec[:, bass.ds(r, 2), :], pj[:, 2 * p:2 * p + 2, :], ACT.Gelu_apprx_tanh
                                 ).then_inc(gelu_ok, 1)
            act.wait_ge(gelu_ok, it + 1)
            evac_o(1)
            split_hi("mix", 8, it)
        ch.close(4)

        def branch_run(m):
            split_hi("branch", 2, m)
            if is_const(m):
                act.wait_ge(pt_free, 40)
                act.wait_ge(o_done, 32)
                act.wait_ge(scan_ok, 16)
                for k in range(KT):
                    nc.scalar.activation(attn_hi[:, k, :], attn[:, k, :], ACT.Copy).then_inc(br_hi_ok, 1)
                act.wait_ge(rec_ok, KT)
                for k in range(KT):
                    nc.scalar.activation(rec_hi[:, k, :], rec[:, k, :], ACT.Copy).then_inc(br_hi_ok, 1)
            after(act, m2_ok, m)
            made(act, "branch", 1, m)
            nc.scalar.activation(g_sb[:, :, :], pj[:, 0:2, :], ACT.Tanh, scale=0.5).then_inc(gate_ok, 1)
            split_hi("branch", 3, m)
            split_hi("branch", 4, m)
            split_hi("branch", 5, m)
            act.wait_ge(ms_ok, m + 1)
            act.sem_inc(flush, 1)
            nc.scalar.activation(mg_hi[:, bass.ds(m, 1), :].rearrange("p a t -> p (a t)"), ms[:, :], ACT.Copy,
                                 scale=0.5).then_inc(mh_ok, 1)

        branch_run(0)
        with act.Fori(0, KT - 1) as q:
            branch_run(q + 1)

        def split_unit_hi(j, p):
            n = j if p is None else p * RAW + j
            at = (1 if p is None else p + 1) if j < RAW else p + 2
            act.wait_ge(ew_in[j % RAW], at * 16)
            if p is not None:
                act.wait_ge(e_used, n - (CONV - 1))
            nc.scalar.activation(e_hi[j % CONV][:, :], e_raw[j % RAW][:, :], ACT.Copy).then_inc(e_hi_ok, 1)

        def n2_hi(k):
            act.wait_ge(rt_full, k + 1)
            if k >= 2:
                act.wait_ge(lg_mm, k - 1)
            nc.scalar.activation(n2t_hi[:, k % 2, :], pj[:, 2 * (k % 2) + 1, :], ACT.Copy, scale=g12[:, 1, k:k + 1]
                                 ).then_inc(n2h_ok, 1)

        def sum_squares(i, c0, c1, col):
            nc.scalar.activation(xn2[:, i, c0:c1], X[:, i, c0:c1], ACT.Square, accum_out=stat2[:, col, i:i + 1]
                                 ).then_inc(ssq_ok, 1)

        for it in range(4):
            if it == 3:
                warm_sqrt(stat2[:, 2, :])
                act.wait_ge(h_ok, 6)
                for i in range(TT):
                    sum_squares(i, 0, 6 * P, 0)
            for j in range(2):
                if it:
                    act.wait_ge(oT_full, it * 2 + j - 1)
                made(act, "out", j, it)
                nc.scalar.activation(oT_sb[j][:, :], pj[:, 2 * j, :], ACT.Copy).then_inc(oT_ok, 1)
                if it < 3:
                    split_hi("out", 2 + j, it)
                if it == 0 and j == 1:
                    act.wait_ge(wrt0_ok, 1)
                    act.wait_ge(wrt_in, 64)
                    nc.scalar.activation(wrt_hi[:, :, 0:N_G + N_E], wrt[:, :, :], ACT.Copy).then_inc(wrt_hi_ok, 1)
                if it and j == 0:
                    n2_hi(2 * it - 2)
                    n2_hi(2 * it - 1)
        n2_hi(KT - 2)
        act.wait_ge(h_ok, KT)
        n2_hi(KT - 1)
        for i in range(TT):
            sum_squares(i, 6 * P, KT * P, 3)
        act.wait_ge(var_ok, 2)
        nc.scalar.activation(stat2[:, 2, :], stat2[:, 1, :], ACT.Sqrt).then_inc(std_ok, 1)
        act.wait_ge(lg_mm, KT)
        nc.scalar.activation(lgT[:, :], o_ps[0:N_G + N_E, :], ACT.Copy).then_inc(lgT_ok, 1)
        act.wait_ge(rstd_ok, 2)
        for i in range(TT - 1):
            nc.scalar.activation(xn2[:, i, :], X[:, i, :], ACT.Copy, scale=stat2[:, 0, i:i + 1]).then_inc(xs_ok, 1)
        act.wait_ge(lg_ok, 1)
        for j in range(CONV - 1):
            split_unit_hi(j, None)
        act.wait_ge(gd_ok, 1)
        nc.scalar.activation(gex[:, :, :], gex[:, :, :], ACT.Exp).then_inc(gexp_ok, 1)
        act.wait_ge(ed_ok, 1)
        nc.scalar.activation(ediff[:, :], ediff[:, :], ACT.Exp).then_inc(eexp_ok, 1)

        def x_hi_half(p, odd, h):
            act.wait_ge(xt_full[odd], p * 2 + (h + 1))
            nc.scalar.activation(xT_hi[:, 4 * h:4 * h + 4, :],
                                 pj[:, 2 + h, :].rearrange("p (k c) -> p k c", c=P), ACT.Copy).then_inc(x_hi_ok, 1)

        def chunk(p, h):
            c, u, m = p * 2 + h, h * UNITS, p * 4 + 2 * h
            split_unit_hi(u + 3, p)
            split_unit_hi(u + 4, p)
            act.wait_ge(e_used, p * RAW + (u + 2))
            act.wait_ge(ht_full, m)
            nc.scalar.activation(hid[:, :], pj[:, 0, :], ACT.Silu).then_inc(silu_ok, 1)
            split_unit_hi(u + 5, p)

            def h_hi(half):
                act.wait_ge(ht_full, m + (half + 1))
                nc.scalar.activation(hT_hi[:, 2 * half:2 * half + 2, :],
                                     ht_ps[half][:, 0:2 * P].rearrange("p (k c) -> p k c", c=P),
                                     ACT.Copy).then_inc(h_hi_ok, 1)

            split_unit_hi(u + 6, p)
            h_hi(0)
            x_hi_half(p + h, 1 - h, 0)
            h_hi(1)
            x_hi_half(p + h, 1 - h, 1)
            split_unit_hi(u + 7, p)
            split_unit_hi(u + 8, p)
            row = act.snap(c * CHUNK)
            act.wait_ge(y_out, c * 16)
            act.wait_ge(e_used, p * RAW + (u + 6))
            nc.scalar.activation(y_sb[:, :].rearrange("p (h d) -> p h d", h=2), s_ps[:, :, :], ACT.Copy
                                 ).then_inc(y_ok, 1)
            act.wait_ge(y_ok, c + 1)
            act.dma_start(y_dram[bass.ds(row, CHUNK), :], y_sb[:, :]).then_inc(y_out, 16)

        x_hi_half(0, 0, 0)
        x_hi_half(0, 0, 1)
        pairs = act.value_load(table[0:1, MAXC + 1:MAXC + 2], min_val=N_E // 2, max_val=MAXC // 2)
        with act.Fori(0, pairs) as p:
            nc.scalar.activation(silu_warm[:, :], ident[:, 0:1], ACT.Silu)
            for h in range(2):
                chunk(p, h)

        def final_ssq(i):
            act.wait_ge(hf_ok, i + 1)
            nc.scalar.activation(F[0][:, i, :], X[:, i, :], ACT.Square, accum_out=stat3[:, 0, i:i + 1]
                                 ).then_inc(ssq_ok, 1)

        def final_root(i):
            act.wait_ge(var_ok, 2 + i + 1)
            nc.scalar.activation(stat3[:, 2, i:i + 1], stat3[:, 1, i:i + 1], ACT.Sqrt).then_inc(std_ok, 1)

        warm_sqrt(stat3[:, 2, :])
        final_ssq(0)
        final_root(0)
        for i in range(TT - 1):
            final_ssq(i + 1)
            if i < TT - 2:
                act.wait_ge(rstd_ok, 2 + i + 1)
                nc.scalar.activation(fo[:, i, :], X[:, i, :], ACT.Copy, scale=stat3[:, 0, i:i + 1]
                                     ).then_inc(fs_ok, 1)
            final_root(i + 1)

    @block.vector
    def _(dve):
        ch = Chain(dve, dve_chain)
        V_ = nc.vector
        ch.link(V_.memset(pt_ps[:, :], 0.0))
        dve.wait_ge(prmT_ok, 1)
        tp = s_ps[:, 0, 0:104]
        V_.tensor_copy(g12[:, :, :], tp[:, 88:104].rearrange("p (g b) -> p g b", b=8)).then_inc(gain_ok, 1)
        V_.tensor_copy(PV[:, 0:5, :], tp[:, 0:40].rearrange("p (g b) -> p g b", b=8))
        V_.tensor_scalar(PV[:, 5:9, :], tp[:, 40:72].rearrange("p (g b) -> p g b", b=8), 0.5, None, ALU.mult)
        V_.tensor_copy(spt[:, 2, :], tp[:, 72:88]).then_inc(prm_ok, 1)

        dve.wait_ge(ssq_ok, 1)
        V_.tensor_scalar(stat[:, 1, :], stat[:, 0, :], 1.0 / D, EPS, ALU.mult, ALU.add).then_inc(var_ok, 1)
        dve.wait_ge(std_ok, 1)
        V_.reciprocal(stat[:, 0, :], stat[:, 2, :]).then_inc(rstd_ok, 1)
        dve.wait_ge(rstd_ok, 1)
        for i in range(TT):
            V_.tensor_scalar(xn[:, i, :], X[:, i, :], stat[:, 0, i:i + 1], None, ALU.mult).then_inc(xn_ok, 1)
        dve.wait_ge(prm_ok, 1)

        def split_lo(phase, u, it=0):
            s, n = unit(phase, u, it)
            dve.wait_ge(w_hi_ok[s], n + 1)
            V_.tensor_tensor(w_lo[s][:, :, :], w_raw[s][:, :, :], w_hi[s][:, :, :].bitcast(F32), ALU.subtract
                             ).then_inc(w_lo_ok[s], 1)

        for k in range(KT):
            dve.wait_ge(nT_hi_ok, k + 1)
            V_.scalar_tensor_tensor(nT_lo[:, k, 0:400], nt_ps(k, 0)[:, 0:400], g12[:, 0, k:k + 1],
                                    nT_hi[:, k, 0:400].bitcast(F32), ALU.mult, ALU.subtract)
            V_.scalar_tensor_tensor(nT_lo[:, k, 400:T], nt_ps(k, 1)[:, 0:P], g12[:, 0, k:k + 1],
                                    nT_hi[:, k, 400:T].bitcast(F32), ALU.mult, ALU.subtract).then_inc(nt_lo_ok, 1)

        split_lo("kv", 1)
        lam = spt[:, 2, :]
        ch.link(V_.tensor_scalar(spt[:, 3, :], lam, -1.0, None, ALU.mult))
        V_.tensor_tensor(spt[:, 0, :], lam, spt[:, 3, :], ALU.max).then_inc(lam_abs_ok, 1)
        ch.link(V_.tensor_scalar(spt[:, 3, :], spt[:, 3, :], 0.0, None, ALU.max))

        def softplus():
            dve.wait_ge(lam_exp_ok, 1)
            e_, s_, z_, p_ = spt[:, 1, :], spt[:, 4, :], spt[:, 5, :], spt[:, 6, :]
            ch.link(V_.tensor_scalar(s_, e_, 2.0, None, ALU.add))
            ch.link(V_.reciprocal(z_, s_))
            ch.link(V_.tensor_tensor(s_, e_, z_, ALU.mult))
            ch.link(V_.tensor_tensor(z_, s_, s_, ALU.mult))
            ch.link(V_.tensor_scalar(p_, z_, 2.0 / 19, None, ALU.mult))
            for k in range(8, 0, -1):
                ch.link(V_.scalar_tensor_tensor(p_, p_, 2.0 / (2 * k + 1), z_, ALU.add, ALU.mult))
            ch.link(V_.scalar_tensor_tensor(p_, p_, 2.0, s_, ALU.add, ALU.mult))
            ch.link(V_.tensor_tensor(p_, p_, spt[:, 3, :], ALU.add))
            p2 = p_.rearrange("p (g b) -> p g b", b=8)
            V_.tensor_scalar(PV[:, 9:11, :], p2, -4.0, None, ALU.mult)
            V_.tensor_scalar(PV[:, 11:13, :], p2, 4.0, None, ALU.mult).then_inc(par_ok, 1)

        for kv in range(KV):
            if kv == 0:
                split_lo("kv", 2)
            dve.wait_ge(k_hi_ok, kv + 1)
            two = lambda t: t.rearrange("p (h c) -> p h c", h=2)
            V_.tensor_tensor(two(kT_lo[:, kv, :]), kv_ps(kv), two(kT_hi[:, kv, :]).bitcast(F32),
                             ALU.subtract).then_inc(k_lo_ok, 1)
        split_lo("kv", 3)
        split_lo("kv", 4)
        softplus()
        split_lo("kv", 5)
        ch.close()

        with dve.Fori(0, 4) as it:
            ch.body(it, 10)
            dve.wait_ge(cur_ok, it + 1)
            dve.wait_ge(pad_ok, 1)
            split_lo("mix", 2, it)
            for bb in range(2):
                dve.wait_ge(xr_ok, it * 2 + (bb + 1))
                ch.link(V_.tensor_scalar(xc[:, bb, :], xr[:, bb, 0:T], cur[:, 0, bb:bb + 1], cur[:, 4, bb:bb + 1],
                                         ALU.mult, ALU.add))
                for i in range(1, 4):
                    ins = V_.scalar_tensor_tensor(xc[:, bb, :], xr[:, bb, i:i + T], cur[:, i, bb:bb + 1],
                                                  xc[:, bb, :], ALU.mult, ALU.add)
                    ch.link(ins) if i < 3 else ins.then_inc(xc_ok, 1)
                split_lo("mix", 3 + bb, it)
            for bb in range(2):
                dve.wait_ge(xch_ok, it * 2 + (bb + 1))
                V_.tensor_tensor(xc_lo[:, bb, :], xc[:, bb, :], xc_hi[:, bb, :].bitcast(F32), ALU.subtract
                                 ).then_inc(xcl_ok, 1)
            split_lo("mix", 5, it)
            for hh in range(2):
                dve.wait_ge(qh_ok, it * 2 + (hh + 1))
                V_.scalar_tensor_tensor(qT_lo[:, hh, :], pj[:, hh, :], HD ** -0.5, qT_hi[:, hh, :].bitcast(F32),
                                        ALU.mult, ALU.subtract).then_inc(q_ok, 1)

            def scores(a):
                hh, j = divmod(a, 4)
                w, o = S_W[j + 1], S_ND[j + 1]
                dve.wait_ge(s_full, it * 8 + (a + 1))
                dve.wait_ge(ndh_ok, it * 2 + (hh + 1))
                dve.wait_ge(pt_full, it * 10 + (PT_N[a - 2] if a >= 2 else 0))
                dve.sem_inc(flush, 1)
                V_.tensor_tensor_reduce(s_sb[a % 2][:, 0:w], ndh[:, o:o + w], s_ps[:, a % 2, 0:w], 1.0,
                                        cur[:, 14, hh:hh + 1], ALU.add, ALU.max, mx[:, hh, j:j + 1]
                                        ).then_inc(tt_ok, 1)
                dve.wait_ge(tt_ok, it * 8 + (a + 1))
                V_.tensor_scalar(nmax[:, hh, j:j + 1], mx[:, hh, j:j + 1], -1.0, None, ALU.mult).then_inc(neg_ok, 1)

            def evac_pt(a):
                nb = len(S_V[a % 4 + 1]) + 1
                dve.wait_ge(o_done, it * 8 + (a - 1 if a >= 2 else 0))
                dve.wait_ge(pt_full, it * 10 + PT_N[a])
                V_.tensor_copy(pt_sb[a % 2][:, 0:nb * P], pt_ps[:, 0:nb * P]).then_inc(pt_free, 1)

            def gate_in(i, bd):
                d, bb = divmod(bd, 2)
                o = META * d
                dve.wait_ge(thi_ok, it * 4 + (i + 1))
                V_.scalar_tensor_tensor(vb[:, bd, o:T], vb[:, bd, o:T], 1.0, xc[:, bb, o:T], ALU.add, ALU.mult
                                        ).then_inc(v_ok, 1)

            def one_minus(i, bd):
                o = META * (bd // 2)
                dve.wait_ge(a2_ok, it * 4 + (i + 1))
                V_.scalar_tensor_tensor(wb[:, bd, o:T], a2[i % 2][:, o:T], 1.0, wb[:, bd, o:T], ALU.add, ALU.mult
                                        ).then_inc(w_ok, 1)

            def normalise(hh):
                dve.wait_ge(es_ok, it * 2 + (hh + 1))
                dve.wait_ge(p_ok, it * 8 + 4 * (hh + 1))
                ch.link(V_.tensor_tensor(den[:, :], rsum[:, hh, :], esink[:, :], ALU.add))
                ch.link(V_.reciprocal(den[:, :], den[:, :]))
                dve.wait_ge(o_done, it * 8 + 4 * (hh + 1))
                dve.wait_ge(pt_full, it * 10 + (OT_N[0] if hh else 0))
                V_.tensor_tensor(o_sb[:, :, :], o_ps[:, :].rearrange("p (j d) -> p j d", d=P),
                                 den[:, :].unsqueeze(2).broadcast_to([P, TT, P]), ALU.mult).then_inc(onorm_ok, 1)

            scores(0)
            scores(1)
            gate_in(0, 0)
            evac_pt(0)
            scores(2)
            gate_in(1, 2)
            evac_pt(1)
            one_minus(0, 0)
            scores(3)
            one_minus(1, 2)
            evac_pt(2)
            scores(4)
            gate_in(2, 1)
            evac_pt(3)
            scores(5)
            gate_in(3, 3)
            split_lo("mix", 6, it)
            normalise(0)
            evac_pt(4)
            scores(6)
            one_minus(2, 1)
            evac_pt(5)
            one_minus(3, 3)
            scores(7)
            split_lo("mix", 7, it)
            evac_pt(6)
            evac_pt(7)
            normalise(1)
            for bd in range(4):
                d = bd // 2
                dve.wait_ge(u_ok, it * 4 + (bd + 1))
                fw = lambda t: t[:, bd, META:T][:, ::-1] if d else t[:, bd, :]
                V_.tensor_tensor_scan(fw(wb), fw(ab), fw(vb), 0.0, ALU.mult, ALU.add).then_inc(scan_ok, 1)
            split_lo("mix", 8, it)
        ch.close(4)

        def branch_run(m):
            split_lo("branch", 2, m)
            if is_const(m):
                for k in range(2 * KT):
                    src, hi, lo = (attn, attn_hi, attn_lo) if k < KT else (rec, rec_hi, rec_lo)
                    dve.wait_ge(br_hi_ok, k + 1)
                    V_.tensor_tensor(lo[:, k % KT, :], src[:, k % KT, :], hi[:, k % KT, :].bitcast(F32), ALU.subtract
                                     ).then_inc(br_lo_ok, 1)
            split_lo("branch", 3, m)
            split_lo("branch", 4, m)
            dve.wait_ge(gate_ok, m + 1)
            after(dve, ms_ok, m)
            made(dve, "branch", 3, m)
            V_.scalar_tensor_tensor(m2[:, :, :], g_sb[:, :, :], 1.0, pj[:, 2:4, :], ALU.add, ALU.mult
                                    ).then_inc(m2_ok, 1)
            split_lo("branch", 5, m)
            dve.wait_ge(mh_ok, m + 1)
            dve.sem_inc(flush, 1)
            one = lambda t: t[:, bass.ds(m, 1), :].rearrange("p a t -> p (a t)")
            V_.scalar_tensor_tensor(one(mg_lo), ms[:, :], 0.5, one(mg_hi).bitcast(F32), ALU.mult, ALU.subtract
                                    ).then_inc(ml_ok, 1)

        branch_run(0)
        with dve.Fori(0, KT - 1) as q:
            branch_run(q + 1)

        def n2_lo(k):
            dve.wait_ge(n2h_ok, k + 1)
            V_.scalar_tensor_tensor(n2t_lo[:, k % 2, :], pj[:, 2 * (k % 2) + 1, :], g12[:, 1, k:k + 1],
                                    n2t_hi[:, k % 2, :].bitcast(F32), ALU.mult, ALU.subtract).then_inc(n2l_ok, 1)

        for it in range(4):
            if it < 3:
                split_lo("out", 2, it)
            if it:
                n2_lo(2 * it - 2)
                n2_lo(2 * it - 1)
            if it < 3:
                split_lo("out", 3, it)
            for j in range(2):
                dve.wait_ge(oT_full, it * 2 + (j + 1))
                dst = X[:, :, (2 * it + j) * P:(2 * it + j + 1) * P]
                V_.tensor_tensor(dst, dst, s_ps[:, j, :].rearrange("p (i c) -> p i c", c=P), ALU.add
                                 ).then_inc(h_ok, 1)
            if it == 0:
                dve.wait_ge(wrt_hi_ok, 1)
                V_.tensor_tensor(wrt_lo[:, :, 0:N_G + N_E], wrt[:, :, :], wrt_hi[:, :, 0:N_G + N_E].bitcast(F32),
                                 ALU.subtract).then_inc(wrt_ok, 1)
        n2_lo(KT - 2)
        n2_lo(KT - 1)

        dve.wait_ge(ssq_ok, NORM2_SSQ + 2 * TT)
        ch.link(V_.tensor_tensor(stat2[:, 0, :], stat2[:, 0, :], stat2[:, 3, :], ALU.add))
        V_.tensor_scalar(stat2[:, 1, :], stat2[:, 0, :], 1.0 / D, EPS, ALU.mult, ALU.add).then_inc(var_ok, 1)
        dve.wait_ge(std_ok, 2)
        V_.reciprocal(stat2[:, 0, :], stat2[:, 2, :]).then_inc(rstd_ok, 1)

        NC = N_G + N_E
        dve.wait_ge(lg_ok, 1)
        dve.wait_ge(rstd_ok, 2)
        lp = pt_ps[:, 0:TT * NC].rearrange("p (i c) -> p i c", c=NC)
        ch.link(V_.tensor_tensor(lg[:, :, :], lp, stat2[:, 0, :].unsqueeze(2).broadcast_to([P, TT, NC]), ALU.mult))
        ch.link(V_.tensor_tensor(lg[:, :, :], lg[:, :, :], bias_r[:, :].unsqueeze(1).broadcast_to([P, TT, NC]),
                                 ALU.add))
        b4 = lambda t: t[:, :].unsqueeze(2).broadcast_to([P, TT, 4])
        ie, ie8 = (iota_e[:, i, :].unsqueeze(1).broadcast_to([P, TT, 4]) for i in range(2))

        def first_max(vals, top, onehot):
            ch.link(V_.tensor_reduce(top[:, :], vals, AX.X, ALU.max))
            ch.link(V_.tensor_tensor(t4[:, :, :], vals, b4(top), ALU.is_equal))
            ch.link(V_.scalar_tensor_tensor(t4[:, :, :], t4[:, :, :], -8.0, ie, ALU.mult, ALU.add))
            ch.link(V_.tensor_reduce(pick[:, :], t4[:, :, :], AX.X, ALU.min))
            ch.link(V_.tensor_tensor(onehot[:, :, :], ie8, b4(pick), ALU.is_equal))

        gl = lg[:, :, 0:N_G]
        first_max(gl, gtop, g1h)
        V_.tensor_tensor(gex[:, :, :], gl, b4(gtop), ALU.subtract).then_inc(gd_ok, 1)
        ge = g1h[:, :, :].unsqueeze(3).broadcast_to([P, TT, N_G, E_G])
        ch.link(V_.tensor_tensor(e16[:, :, :, :], lg[:, :, N_G:].rearrange("p i (g e) -> p i g e", e=E_G), ge,
                                 ALU.mult))
        ch.link(V_.tensor_reduce(e_in[:, :, :], e16[:, :, :, :].rearrange("p i g e -> p i e g"), AX.X, ALU.add))
        first_max(e_in[:, :, :], etop1, o1h[0])
        ch.link(V_.scalar_tensor_tensor(e_in[:, :, :], o1h[0][:, :, :], -3e38, e_in[:, :, :], ALU.mult, ALU.add))
        first_max(e_in[:, :, :], etop2, o1h[1])
        for k in range(2):
            ch.mark(V_.tensor_tensor(masks[:, k], ge, o1h[k][:, :, :].unsqueeze(2).broadcast_to([P, TT, N_G, E_G]),
                                     ALU.mult))
        ch.need(ch.n)
        dve.wait_ge(iota_ok, 1)
        flat = lambda k: masks[:, k].rearrange("p i g e -> p (i g e)")
        ch.link(V_.tensor_tensor(both[:, 0:TT, :].rearrange("p i e -> p (i e)"), flat(0), flat(1), ALU.add))
        for i in range(TT):
            ins = V_.tensor_tensor(past[:, i + 1, :], past[:, i, :], both[:, i, :], ALU.add)
            ch.link(ins) if i < TT - 1 else ins.then_inc(m_ok, 1)
        dve.wait_ge(g2_in, 16)
        V_.scalar_tensor_tensor(xn2[:, TT - 1, :], X[:, TT - 1, :], stat2[:, 0, TT - 1:TT], g2row[:, :],
                                ALU.mult, ALU.mult).then_inc(xn2_last_ok, 1)
        V_.tensor_tensor(ediff[:, :], etop2[:, :], etop1[:, :], ALU.subtract).then_inc(ed_ok, 1)
        m01 = masks[:, :, :, :, :].rearrange("p k i g e -> p (k i) (g e)")
        per = lambda t: t.unsqueeze(1).broadcast_to([P, 2 * TT, N_E])
        ch.link(V_.tensor_tensor(pr[:, :, :], m01, per(io_r[:, 0:N_E]), ALU.mult))
        ch.link(V_.tensor_reduce(pex[:, :], pr[:, :, :], AX.X, ALU.add))
        dve.wait_ge(rank_ok, 1)
        cnt = o_ps[:, TT * N_E:(TT + 1) * N_E]
        ch.link(V_.tensor_scalar(nch[:, :], cnt, thr[:, 0:1], None, ALU.is_gt))
        for k in range(1, MAXR - 1):
            ch.link(V_.scalar_tensor_tensor(nch[:, :], cnt, thr[:, k:k + 1], nch[:, :], ALU.is_gt, ALU.add))
        ch.link(V_.tensor_tensor_scan(oend[:, :], one16[:, :], nch[:, :], 0.0, ALU.mult, ALU.add))
        ch.link(V_.tensor_tensor(obase[:, :], oend[:, :], nch[:, :], ALU.subtract))
        ch.link(V_.scalar_tensor_tensor(obase[:, :], obase[:, :], N_E - 1.0, io_r[:, 0:N_E], ALU.add, ALU.subtract))
        ch.link(V_.tensor_tensor(pr[:, :, :], m01, per(obase[:, :]), ALU.mult))
        ch.link(V_.tensor_reduce(pob[:, :], pr[:, :, :], AX.X, ALU.add))
        ch.link(V_.tensor_tensor(pr[:, :, :].rearrange("p (k i) e -> p k (i e)", k=2),
                                 m01.rearrange("p (k i) e -> p k (i e)", k=2),
                                 o_ps[:, 0:TT * N_E].unsqueeze(1).broadcast_to([P, 2, TT * N_E]), ALU.mult))
        ch.link(V_.tensor_reduce(prk[:, :], pr[:, :, :], AX.X, ALU.add))
        ch.link(V_.tensor_scalar(pf1[:, :], prk[:, :], thr[:, 0:1], None, ALU.is_ge))
        ch.link(V_.scalar_tensor_tensor(pfl[:, :], prk[:, :], thr[:, 1:2], pf1[:, :], ALU.is_ge, ALU.add))
        for k in range(2, MAXR - 1):
            ch.link(V_.scalar_tensor_tensor(pfl[:, :], prk[:, :], thr[:, k:k + 1], pfl[:, :], ALU.is_ge, ALU.add))
        ch.link(V_.scalar_tensor_tensor(prow[:, :], pfl[:, :], -float(CHUNK), prk[:, :], ALU.mult, ALU.add))
        ch.mark(V_.tensor_tensor(roh[:, :, :], io_r[:, :].unsqueeze(1).broadcast_to([P, 2 * TT, CHUNK]),
                                 prow[:, :].unsqueeze(2).broadcast_to([P, 2 * TT, CHUNK]), ALU.is_equal))
        ch.link(V_.tensor_tensor(pf1[:, :], pf1[:, :], pob[:, :], ALU.mult))
        ch.link(V_.tensor_tensor(pch[:, :], pex[:, :], pfl[:, :], ALU.add))
        ch.link(V_.tensor_tensor(pch[:, :], pch[:, :], pf1[:, :], ALU.add))
        ch.link(V_.tensor_tensor(ceq[:, :, :], io_r[:, 0:NIDX].unsqueeze(1).broadcast_to([P, 2 * TT, NIDX]),
                                 pch[:, :].unsqueeze(2).broadcast_to([P, 2 * TT, NIDX]), ALU.is_equal))
        V_.tensor_tensor(coh[:, :, :].rearrange("p (k i) c -> p k i c", k=2),
                         ceq[:, :, :].rearrange("p (k i) c -> p k i c", k=2),
                         tok[:, :].unsqueeze(1).unsqueeze(3).broadcast_to([P, 2, TT, NIDX]), ALU.mult
                         ).then_inc(oh_ok, 1)
        ch.mark(V_.tensor_copy(tablef[:, 0:N_E], io_r[:, 0:N_E]))
        ch.link(V_.tensor_tensor(over9[:, :, :], io_r[:, 0:MAXO + 1].unsqueeze(2).broadcast_to([P, MAXO + 1, N_E]),
                                 oend[:, :].unsqueeze(1).broadcast_to([P, MAXO + 1, N_E]), ALU.is_ge))
        ch.link(V_.tensor_tensor(npair[:, :], oend[:, N_E - 1:N_E].broadcast_to([P, MAXO // 2]), even[:, :],
                                 ALU.is_gt))
        ch.link(V_.tensor_reduce(tablef[:, N_E:MAXC + 1], over9[:, :, :], AX.X, ALU.add))
        ch.link(V_.tensor_scalar(tablef[:, N_E:MAXC + 1], tablef[:, N_E:MAXC + 1], N_E - 1.0, None, ALU.min))
        ch.link(V_.tensor_reduce(tablef[:, MAXC + 1:MAXC + 2], npair[:, :], AX.X, ALU.add))
        ch.link(V_.tensor_scalar(tablef[:, MAXC + 2:MAXC + 3], tablef[:, MAXC + 1:MAXC + 2], N_E // 2 - 1.0, None,
                                 ALU.add))
        ch.link(V_.tensor_scalar(tablef[:, MAXC + 1:MAXC + 2], tablef[:, MAXC + 1:MAXC + 2], N_E // 2 + 0.0, None,
                                 ALU.add))
        V_.tensor_copy(table[:, :], tablef[:, :]).then_inc(table_ok, 1)
        ch.link(V_.scalar_tensor_tensor(slot_i[:, :], pch[:, :], float(CHUNK), prow[:, :], ALU.mult, ALU.add))
        dve.wait_ge(idxp_ok, 1)
        dve.wait_ge(table_ok, 1)
        V_.tensor_copy(idx[:, :], o_ps[0:CHUNK, 128:128 + NIDX]).then_inc(route_ok, 1)
        dve.wait_ge(gexp_ok, 1)
        ch.link(V_.tensor_reduce(gsum[:, :], gex[:, :, :], AX.X, ALU.add))
        dve.wait_ge(eexp_ok, 1)
        ch.link(V_.tensor_scalar(wden[:, :], ediff[:, :], 1.0, None, ALU.add))
        ch.link(V_.tensor_tensor(wden[:, :], wden[:, :], gsum[:, :], ALU.mult))
        ch.link(V_.reciprocal(slot_w[0][:, :], wden[:, :]))
        ch.link(V_.tensor_tensor(slot_w[1][:, :], slot_w[0][:, :], ediff[:, :], ALU.mult))

        def split_unit_lo(j, p):
            dve.wait_ge(e_hi_ok, j + 1 if p is None else p * RAW + (j + 1))
            V_.tensor_tensor(e_lo[j % CONV][:, :], e_raw[j % RAW][:, :], e_hi[j % CONV][:, :].bitcast(F32),
                             ALU.subtract).then_inc(e_lo_ok, 1)

        def x_lo_half(m, h):
            dve.wait_ge(x_hi_ok, m + 1)
            V_.tensor_tensor(xT_lo[:, 4 * h:4 * h + 4, :], pj[:, 2 + h, :].rearrange("p (k c) -> p k c", c=P),
                             xT_hi[:, 4 * h:4 * h + 4, :].bitcast(F32), ALU.subtract).then_inc(x_lo_ok, 1)

        def chunk(p, h):
            u, m = h * UNITS, p * 4 + 2 * h
            split_unit_lo(u + 3, p)
            split_unit_lo(u + 4, p)
            split_unit_lo(u + 5, p)
            dve.wait_ge(silu_ok, p * 2 + (h + 1))
            dve.wait_ge(e_used, p * RAW + (u + 4))
            for half in range(2):
                f = slice(half * 256, (half + 1) * 256)
                V_.tensor_tensor(hid[:, f], hid[:, f], pj[:, 1, f], ALU.mult).then_inc(hid_ok, 1)

            def h_lo(half):
                dve.wait_ge(h_hi_ok, m + (half + 1))
                V_.tensor_tensor(hT_lo[:, 2 * half:2 * half + 2, :],
                                 ht_ps[half][:, 0:2 * P].rearrange("p (k c) -> p k c", c=P),
                                 hT_hi[:, 2 * half:2 * half + 2, :].bitcast(F32), ALU.subtract).then_inc(h_lo_ok, 1)

            h_lo(0)
            h_lo(1)
            split_unit_lo(u + 6, p)
            x_lo_half(m + 2, 0)
            x_lo_half(m + 3, 1)
            split_unit_lo(u + 7, p)
            split_unit_lo(u + 8, p)

        for j in range(CONV - 2):
            split_unit_lo(j, None)
        x_lo_half(0, 0)
        x_lo_half(1, 1)
        split_unit_lo(CONV - 2, None)
        pairs = dve.value_load(table[0:1, MAXC + 1:MAXC + 2], min_val=N_E // 2, max_val=MAXC // 2)
        with dve.Fori(0, pairs) as p:
            for h in range(2):
                chunk(p, h)

        dve.wait_ge(gfin_in, 16)
        def combine(i):
            dve.wait_ge(f_in[i], 32)
            for j in range(2):
                ins = V_.scalar_tensor_tensor(X[:, i, :], F[j][:, i, :], slot_w[j][:, i:i + 1], X[:, i, :],
                                              ALU.mult, ALU.add)
                ch.link(ins) if j == 0 else ins.then_inc(hf_ok, 1)

        combine(0)
        combine(1)
        for i in range(TT):
            dve.wait_ge(ssq_ok, NORM2_SSQ + 2 * TT + i + 1)
            V_.tensor_scalar(stat3[:, 1, i:i + 1], stat3[:, 0, i:i + 1], 1.0 / D, EPS, ALU.mult, ALU.add
                             ).then_inc(var_ok, 1)
            dve.wait_ge(std_ok, 2 + i + 1)
            V_.reciprocal(stat3[:, 0, i:i + 1], stat3[:, 2, i:i + 1]).then_inc(rstd_ok, 1)
            if i + 2 < TT:
                combine(i + 2)
            else:
                dve.wait_ge(rstd_ok, 2 + i + 1)
                V_.scalar_tensor_tensor(fo[:, i, :], X[:, i, :], stat3[:, 0, i:i + 1], gfin[:, :],
                                        ALU.mult, ALU.mult).then_inc(fo_last_ok, 1)

    @block.tensor
    def _(pe):
        mm, tp = nc.tensor.matmul, nc.tensor.transpose
        pe.wait_ge(const_ok, 1)
        pe.wait_ge(prm_in, 128)
        tp(s_ps[:, 0, 0:104], prm[:, :], ident[0:104, 0:104]).then_inc(prmT_ok, 1)
        pe.wait_ge(mn_ok, 1)
        for k in range(KT):
            if k >= 3:
                pe.wait_ge(nt_lo_ok, k - 2)
            elif k == 2:
                pe.wait_ge(prm_ok, 1)
            c = slice(k * P, (k + 1) * P)
            tp(nt_ps(k, 0)[:, 0:META], mn[:, c], ident[0:META, 0:META])
            for i in range(TT - 1):
                if k == 0:
                    pe.wait_ge(xn_ok, i + 1)
                tp(nt_ps(k, 0)[:, META + i * P:META + (i + 1) * P], xn[:, i, c], ident[:, :])
            if k == 0:
                pe.wait_ge(xn_ok, TT)
            tp(nt_ps(k, 1)[:, 0:P], xn[:, TT - 1, c], ident[:, :]).then_inc(nt_full, 1)

        def weights(phase, u, it=0):
            s, n = unit(phase, u, it)
            pe.wait_ge(w_lo_ok[s], n + 1)
            return s, (w_hi[s], w_lo[s])

        def project_T(phase, u, it, p=None, dst=None, as_it_comes=False):
            s, w = weights(phase, u, it)
            if dst is None:
                dst = pj[:, 2 * p:2 * p + 2, 0:HALF]
            for k in range(KT):
                if as_it_comes:
                    pe.wait_ge(nt_lo_ok, max(k, 5) + 1)
                for n, (i, j) in enumerate(PASSES):
                    for h in range(2):
                        st, sp_ = k == 0 and n == 0, k == KT - 1 and n == 2
                        last = mm(dst[:, h, :], w[i][:, k, :], NT[j][:, k, h * HALF:(h + 1) * HALF],
                                  start=st, stop=sp_)
            last.then_inc(w_used[s], 1)

        def project(phase, u, it, dst, act_parts, k0=0, k1=KT, off=0):
            s, w = unit(phase, u, it)[0], None
            if k0 == 0:
                weights(phase, u, it)
            w = (w_hi[s], w_lo[s])
            for k in range(k0, k1):
                for n, (i, j) in enumerate(PASSES):
                    last = mm(dst, w[i][:, k, :], act_parts[j][:, k, off:off + SEQ],
                              start=k == 0 and n == 0, stop=k == KT - 1 and n == 2)
            if k1 == KT:
                last.then_inc(w_used[s], 1)

        for kv in range(KV):
            project_T("kv", kv, 0, dst=kv_ps(kv), as_it_comes=kv == 0)
        for c in range(2):
            if c == 1:
                pe.wait_ge(k_lo_ok, 2)
            project_T("kv", 2 + c, 0, c)
        for c in range(2):
            pe.wait_ge(vT_ok, c + 1)
            tp(s_ps[0:META, c, 0:P], a2[c][:, 0:META], ident[:, :])
            for t in range(TT):
                last = tp(v_ps[c][:, t * P:(t + 1) * P], a2[c][:, META + t * P:META + (t + 1) * P], ident[:, :])
            last.then_inc(v_full, 1)

        with pe.Fori(0, 4) as it:
            kv = pe.snap(it // 2)
            pe.wait_ge(thi_ok, it * 4)
            project_T("mix", 0, it, 0)
            pe.wait_ge(gelu_ok, it)
            project_T("mix", 1, it, 1)
            pe.wait_ge(xr_ok, it * 2 + 1)
            project("mix", 2, it, pj[:, 0, :], NT, off=META)
            project("mix", 3, it, pj[:, 1, :], NT, off=META)
            QT, K = (qT_hi, qT_lo), (kT_hi, kT_lo)

            def scores(a):
                hh, j = divmod(a, 4)
                w, k0 = S_W[j + 1], S_K[j + 1]
                if a in (0, 4):
                    pe.wait_ge(q_ok, it * 2 + (hh + 1))
                pe.wait_ge(tt_ok, it * 8 + max(a - 1, 0))
                parts = ((0, 0, w),) if k0 == 16 else ((0, 0, 16), (16, k0, w - 16))
                for d0, s0, n_ in parts:
                    for n, (i, l) in enumerate(PASSES):
                        last = mm(s_ps[:, a % 2, d0:d0 + n_], QT[i][:, hh, j * P:(j + 1) * P],
                                  K[l][:, bass.ds(kv, 1), s0:s0 + n_].rearrange("p a t -> p (a t)"),
                                  start=n == 0, stop=n == 2)
                last.then_inc(s_full, 1)

            def transpose_p(a):
                hh, j = divmod(a, 4)
                pe.wait_ge(p_ok, it * 8 + (a + 1))
                pe.wait_ge(pt_free, it * 10 + (PT_N[a] - 1))
                nb = len(S_V[j + 1])
                tp(pt_ps[0:META, 0:P], s_sb[a % 2][:, 0:META], ident[:, :])
                for b in range(nb):
                    last = tp(pt_ps[:, (b + 1) * P:(b + 2) * P], s_sb[a % 2][:, META + b * P:META + (b + 1) * P],
                              ident[:, :])
                last.then_inc(pt_full, 1)

            def values(a):
                hh, j = divmod(a, 4)
                if j == 0:
                    pe.wait_ge(onorm_ok, it * 2 + hh)
                pe.wait_ge(pt_free, it * 10 + PT_N[a])
                dst = o_ps[:, j * P:(j + 1) * P]
                vs = lambda r, t: V[r, t, bass.ds(vo, P)]
                for b, t in enumerate(S_V[j + 1]):
                    mm(dst, pt_sb[a % 2][:, (b + 1) * P:(b + 2) * P], vs(slice(0, P), t), start=b == 0, stop=False)
                mm(dst, pt_sb[a % 2][0:META, 0:P], vs(slice(0, META), 0), start=False, stop=True
                   ).then_inc(o_done, 1)

            def transpose_o(hh):
                pe.wait_ge(onorm_ok, it * 2 + (hh + 1))
                pe.wait_ge(pt_free, it * 10 + (OT_N[hh] - 1))
                for j in range(TT):
                    last = tp(pt_ps[:, j * P:(j + 1) * P], o_sb[:, j, :], ident[:, :])
                last.then_inc(pt_full, 1)

            def lru(j, bb, d, which):
                s = unit("mix", 4, it)[0]
                w = (w_hi[s], w_lo[s])
                XC = (xc_hi, xc_lo)
                p = j % 2
                if d == 0:
                    for n_, (i, l) in enumerate(PASSES):
                        for h in range(2):
                            last = mm(pj[:, 2 * p + h, 0:HALF], w[i][:, 4 * which + bb, :],
                                      XC[l][:, bb, h * HALF:(h + 1) * HALF], start=n_ == 0, stop=n_ == 2)
                else:
                    for q in range(2):
                        for n_, (i, l) in enumerate(PASSES):
                            last = mm(pj[:, 2 * p + q, :], w[i][:, 4 * q + 2 + bb, :], XC[l][:, bb, META:T],
                                      start=n_ == 0, stop=n_ == 2)
                last.then_inc(lru_full if j < 8 else w_used[s], 1)

            vo = pe.snap(kv * P)
            weights("mix", 4, it)
            pe.wait_ge(xcl_ok, it * 2 + 2)
            pe.wait_ge(xr_ok, it * 2 + 2)
            lru(3, 0, 0, 0)
            pe.wait_ge(v_rows_ok, 2)
            scores(0)
            scores(1)
            pe.wait_ge(q_ok, it * 2 + 2)
            lru(4, 0, 0, 1)
            pe.wait_ge(tha_ok, it * 2 + 1)
            lru(5, 0, 1, 0)
            transpose_p(0)
            scores(2)
            pe.wait_ge(thi_ok, it * 4 + 1)
            lru(6, 1, 0, 0)
            values(0)
            transpose_p(1)
            scores(3)
            pe.wait_ge(thi_ok, it * 4 + 2)
            lru(7, 1, 0, 1)
            values(1)
            transpose_p(2)
            scores(4)
            pe.wait_ge(tha_ok, it * 2 + 2)
            lru(8, 1, 1, 0)
            values(2)
            transpose_p(3)
            scores(5)
            pe.wait_ge(thi_ok, it * 4 + 3)
            y0, y1 = pj[:, 2, :], pj[:, 3, :]
            project("mix", 5, it, y0, NT, 0, 4, META)
            values(3)
            transpose_p(4)
            scores(6)
            project("mix", 5, it, y0, NT, 4, KT, META)
            transpose_o(0)
            values(4)
            transpose_p(5)
            scores(7)
            project("mix", 6, it, y1, NT, 0, 2, META)
            values(5)
            transpose_p(6)
            project("mix", 6, it, y1, NT, 2, 4, META)
            values(6)
            transpose_p(7)
            project("mix", 6, it, y1, NT, 4, 6, META)
            values(7)
            project("mix", 6, it, y1, NT, 6, KT, META)
            transpose_o(1)

        REC, ATT, MG = (rec_hi, rec_lo), (attn_hi, attn_lo), (mg_hi, mg_lo)

        def branch_run(m):
            after(pe, gate_ok, m)
            project("branch", 0, m, pj[:, 0, :], NT, off=META)
            project("branch", 1, m, pj[:, 1, :], NT, off=META)
            if is_const(m):
                pe.wait_ge(gelu_ok, 4)
            after(pe, m2_ok, m)
            for j, parts in enumerate((ATT, REC)):
                for k in range(KT):
                    if is_const(m):
                        pe.wait_ge(br_lo_ok, j * KT + k + 1)
                    project("branch", 2 + j, m, pj[:, 2 + j, :], parts, k, k + 1)

        pe.wait_ge(thi_ok, 16)
        branch_run(0)
        with pe.Fori(0, KT - 1) as q:
            branch_run(q + 1)

        def h_rows_T(k):
            pe.wait_ge(h_ok, k + 1)
            if k >= 2:
                pe.wait_ge(n2l_ok, k - 1)
            for i in range(TT):
                last = tp(pj[:, 2 * (k % 2) + 1, i * P:(i + 1) * P], X[:, i, k * P:(k + 1) * P], ident[:, :])
            last.then_inc(rt_full, 1)

        def logits(k):
            pe.wait_ge(n2l_ok, k + 1)
            for n, (i, j) in enumerate(PASSES):
                last = mm(o_ps[:, :], (wrt_hi, wrt_lo)[i][:, k, :], (n2t_hi, n2t_lo)[j][:, k % 2, :],
                          start=k == 0 and n == 0, stop=k == KT - 1 and n == 2)
            last.then_inc(lg_mm, 1)

        def back(it, j):
            if it:
                pe.wait_ge(h_ok, it * 2 - 1 + j)
            pe.wait_ge(oT_ok, it * 2 + (j + 1))
            for i in range(TT):
                last = tp(s_ps[:, j, i * P:(i + 1) * P], oT_sb[j][:, i * P:(i + 1) * P], ident[:, :])
            last.then_inc(oT_full, 1)

        for it in range(4):
            if it:
                pe.wait_ge(oT_ok, it * 2 - 1)
            else:
                pe.wait_ge(ml_ok, KT - 1)
            project("out", 0, it, pj[:, 0, :], MG, 0, KT - 1)
            pe.wait_ge(ml_ok, KT)
            project("out", 0, it, pj[:, 0, :], MG, KT - 1, KT)
            if it:
                h_rows_T(2 * it - 2)
                h_rows_T(2 * it - 1)
                pe.wait_ge(oT_ok, it * 2)
            project("out", 1, it, pj[:, 2, :], MG)
            back(it, 0)
            if it:
                if it == 1:
                    pe.wait_ge(wrt_ok, 1)
                logits(2 * it - 2)
                logits(2 * it - 1)
            back(it, 1)
        h_rows_T(KT - 2)
        h_rows_T(KT - 1)
        logits(KT - 2)
        logits(KT - 1)

        NC = N_G + N_E
        pe.wait_ge(lgT_ok, 1)
        for i in range(TT):
            last = tp(pt_ps[:, i * NC:(i + 1) * NC], lgT[:, i * P:(i + 1) * P], ident[0:NC, 0:NC])
        last.then_inc(lg_ok, 1)
        pe.wait_ge(m_ok, 1)
        rk = o_ps[:, 0:(TT + 1) * N_E]
        mm(rk, tri[:, :], both[:, :, :].rearrange("p i e -> p (i e)"), start=True, stop=False)
        mm(rk, ones[:, :], past[:, :, :].rearrange("p i e -> p (i e)"), start=False, stop=True).then_inc(rank_ok, 1)
        pe.wait_ge(oh_ok, 1)
        for i in range(2 * TT):
            last = mm(o_ps[0:CHUNK, 128:128 + NIDX], roh[:, i, :], coh[:, i, :], start=i == 0, stop=i == 2 * TT - 1)
        last.then_inc(idxp_ok, 1)
        pe.wait_ge(route_ok, 1)

        def x_rows(odd, h):
            for k in range(4 * h, 4 * h + 4):
                last = tp(pj[:, 2 + h, (k % 4) * CHUNK:(k % 4 + 1) * CHUNK], G[odd][:, k * P:(k + 1) * P],
                          ident[:, :])
            last.then_inc(xt_full[odd], 1)

        XT, HT = (xT_hi, xT_lo), (hT_hi, hT_lo)

        def half_product(dst, act_parts, u, p):
            s = u % CONV
            unit_split(pe, u, p)
            for k in range(4):
                for n, (i, j) in enumerate(PASSES):
                    last = mm(dst, act_parts[i][:, 4 * (u % 2) + k, :], (e_hi, e_lo)[j][s][:, k * FF:(k + 1) * FF],
                              start=u % 2 == 0 and k == 0 and n == 0, stop=u % 2 == 1 and k == 3 and n == 2)
            last.then_inc(e_used, 1)

        def chunk(p, h):
            c, u, m = p * 2 + h, h * UNITS, p * 4 + 2 * h
            pe.wait_ge(x_lo_ok, m + 2)
            pe.wait_ge(silu_ok, c)
            half_product(pj[:, 0, :], XT, u, p)
            half_product(pj[:, 0, :], XT, u + 1, p)
            pe.wait_ge(hid_ok, m)
            half_product(pj[:, 1, :], XT, u + 2, p)
            half_product(pj[:, 1, :], XT, u + 3, p)

            def h_rows(half):
                pe.wait_ge(hid_ok, m + (half + 1))
                for k in range(2 * half, 2 * half + 2):
                    last = tp(ht_ps[half][:, (k % 2) * P:(k % 2 + 1) * P], hid[:, k * P:(k + 1) * P], ident[:, :])
                last.then_inc(ht_full, 1)

            pe.wait_ge(g_in[1 - h], p * 16 + (h + 1) * 16)
            x_rows(1 - h, 0)
            h_rows(0)
            x_rows(1 - h, 1)
            h_rows(1)
            for half in range(2):
                v = u + 4 + half
                s = v % CONV
                pe.wait_ge(h_lo_ok, m + (half + 1))
                unit_split(pe, v, p)
                if half == 0:
                    pe.wait_ge(y_ok, c)
                for k in range(2):
                    for n, (i, j) in enumerate(PASSES):
                        for d in range(2):
                            last = mm(s_ps[:, d, :], HT[i][:, 2 * half + k, :],
                                      (e_hi, e_lo)[j][s][:, k * D + d * 512:k * D + (d + 1) * 512],
                                      start=half == 0 and k == 0 and n == 0, stop=half == 1 and k == 1 and n == 2)
                last.then_inc(e_used, 1)

        pe.wait_ge(g_in[0], 16)
        x_rows(0, 0)
        x_rows(0, 1)
        pairs = pe.value_load(table[0:1, MAXC + 1:MAXC + 2], min_val=N_E // 2, max_val=MAXC // 2)
        pe.sem_inc(flush, 1)
        with pe.Fori(0, pairs) as p:
            for h in range(2):
                chunk(p, h)

    ctx.close()


_INS = ['x', 'meta_tokens', 'norm_mix_g', 'w_in', 'conv_w', 'conv_b', 'lru_w_a', 'lru_b_a', 'lru_w_x', 'lru_b_x',
        'lru_lambda', 'attn_sink', 'w_attn_branch', 'w_rec_branch', 'w_out', 'norm_ffn_g', 'w_group', 'b_group',
        'w_router', 'b_router', 'moe_w_gate', 'moe_w_up', 'moe_w_down', 'final_norm_g']
_OUTS = [((1, SEQ, D), 'float32')]


def kernel(**inputs):
    import numpy as _np
    import concourse.bacc as _bacc
    from concourse import mybir as _mybir
    from concourse.bass_utils import run_bass_kernel_spmd as _run

    nc = _bacc.Bacc("TRN2", target_bir_lowering=False, num_devices=1)
    arrays, args = {}, []
    for name in _INS:
        a = _np.ascontiguousarray(inputs[name])
        arrays[f"in_{name}_dram"] = a
        args.append(nc.dram_tensor(f"in_{name}_dram", a.shape, _mybir.dt.from_np(a.dtype), kind="ExternalInput").ap())
    for i, (shape, dtype) in enumerate(_OUTS):
        dt = _mybir.dt.from_np(_np.dtype(dtype))
        args.append(nc.dram_tensor(f"out_{i}_dram", shape, dt, kind="ExternalOutput").ap())
    block_program(nc, *args)
    r = _run(nc, [arrays], core_ids=[0])
    return r.results[0]["out_0_dram"]
```
